# Optimizing a Trainium2 kernel written in Bass

```python
import jax, jax.numpy as jnp
from jax import lax
import numpy as np

D_MODEL = 1024
BATCH = 1
SEQ = 512
DEPTH = 2

CHUNK = 64
Q_BLOCK = 128
N_EVEN = (DEPTH + 1) // 2
N_ODD = DEPTH // 2
EPS = 1e-6

CONV_DIM = D_MODEL // 2
CONV_WIDTH = 3
MLA_HEADS = 8
MLA_Q_RANK = D_MODEL // 4
MLA_KV_RANK = D_MODEL // 4
MLA_NOPE = 64
MLA_ROPE = 32
MLA_V = (D_MODEL // 2) // MLA_HEADS
ROPE_THETA = 10000.0
ML_HEADS = 4
ML_DH = D_MODEL // ML_HEADS
D_FF = 4 * D_MODEL
POS_OFFSET_MAX = 4096

HYB_SPLITS = [CONV_DIM, CONV_DIM, CONV_DIM, MLA_Q_RANK, MLA_KV_RANK, MLA_ROPE]
HYB_IN = sum(HYB_SPLITS)
ML_SPLITS = [D_MODEL, D_MODEL, D_MODEL, D_MODEL, ML_HEADS, ML_HEADS]
ML_IN = sum(ML_SPLITS)

kernel_name = 'chunk_causal_conv_mla_mlstm_hybrid'

def _split(a, sizes):
    return jnp.split(a, np.cumsum(sizes)[:-1].tolist(), axis=-1)

def rmsnorm(x, g):
    xf = x.astype(jnp.float32)
    y = xf * lax.rsqrt(jnp.mean(xf * xf, axis=-1, keepdims=True) + EPS)
    return (y * g.astype(jnp.float32)).astype(x.dtype)

def rope(x, positions):
    half = x.shape[-1] // 2
    inv = ROPE_THETA ** (-jnp.arange(half, dtype=jnp.float32) / half)
    ang = positions.astype(jnp.float32)[..., None] * inv
    ang = ang.reshape(ang.shape[:2] + (1,) * (x.ndim - 3) + (half,))
    cos, sin = jnp.cos(ang), jnp.sin(ang)
    xf = x.astype(jnp.float32)
    x1, x2 = xf[..., :half], xf[..., half:]
    return jnp.concatenate([x1 * cos - x2 * sin, x1 * sin + x2 * cos], axis=-1).astype(x.dtype)

def short_conv_mixer(b_gate, c_gate, h, conv_w):
    u = c_gate * h
    y = lax.conv_general_dilated(
        u, conv_w[:, None, :].astype(u.dtype), window_strides=(1,),
        padding=[(CONV_WIDTH - 1, 0)], dimension_numbers=('NWC', 'WIO', 'NWC'),
        feature_group_count=CONV_DIM)
    return b_gate * y

def mla_mixer(c_q, c_kv, k_r, positions, q_norm, kv_norm, w_uq, w_ukv):
    B, S, _ = c_q.shape
    q = jnp.einsum('bsr,rf->bsf', rmsnorm(c_q, q_norm), w_uq).reshape(B, S, MLA_HEADS, MLA_NOPE + MLA_ROPE)
    q_nope, q_rope = q[..., :MLA_NOPE], rope(q[..., MLA_NOPE:], positions)
    kv = jnp.einsum('bsr,rf->bsf', rmsnorm(c_kv, kv_norm), w_ukv).reshape(B, S, MLA_HEADS, MLA_NOPE + MLA_V)
    k_nope, v = kv[..., :MLA_NOPE], kv[..., MLA_NOPE:]
    k_rope = rope(k_r, positions)
    scale = (MLA_NOPE + MLA_ROPE) ** -0.5
    outs = []
    for qb in range(S // Q_BLOCK):
        q0, kv_end = qb * Q_BLOCK, (qb + 1) * Q_BLOCK
        s = (jnp.einsum('bqhd,bkhd->bhqk', q_nope[:, q0:kv_end], k_nope[:, :kv_end])
             + jnp.einsum('bqhd,bkd->bhqk', q_rope[:, q0:kv_end], k_rope[:, :kv_end]))
        s = s.astype(jnp.float32) * scale
        mask = (np.arange(kv_end) // CHUNK)[None, :] <= (np.arange(q0, kv_end) // CHUNK)[:, None]
        p = jax.nn.softmax(jnp.where(mask, s, -jnp.inf), axis=-1).astype(v.dtype)
        outs.append(jnp.einsum('bhqk,bkhd->bqhd', p, v[:, :kv_end]))
    return jnp.concatenate(outs, axis=1).reshape(B, S, MLA_HEADS * MLA_V)

def mlstm_cell(q, k, v, i_pre, f_pre):
    B, S, H, DH = q.shape
    NC, L = S // CHUNK, CHUNK
    to_chunks = lambda a: a.reshape(B, NC, L, H, DH).transpose(0, 3, 1, 2, 4)
    q, k, v = to_chunks(q) * (DH ** -0.5), to_chunks(k), to_chunks(v)
    log_f = jax.nn.log_sigmoid(f_pre).reshape(B, NC, L, H).transpose(0, 3, 1, 2)
    log_i = i_pre.reshape(B, NC, L, H).transpose(0, 3, 1, 2)
    b = jnp.cumsum(log_f, axis=-1)
    causal = np.tril(np.ones((L, L), dtype=bool))
    d_log = jnp.where(causal, b[..., :, None] - b[..., None, :] + log_i[..., None, :], -jnp.inf)
    m_intra = jnp.max(d_log, axis=-1)
    b_last = b[..., -1]
    a = b_last[..., None] - b + log_i
    a_max = jnp.max(a, axis=-1)
    kw = k * jnp.exp(a - a_max[..., None])[..., None]
    c_loc = jnp.einsum('bhcsk,bhcsv->bhckv', kw, v)
    n_loc = jnp.sum(kw, axis=3)

    def step(carry, inp):
        c_st, n_st, m_st = carry
        cl, nl, am, bl = inp
        m_new = jnp.maximum(bl + m_st, am)
        sp, sl = jnp.exp(bl + m_st - m_new), jnp.exp(am - m_new)
        return (sp[..., None, None] * c_st + sl[..., None, None] * cl,
                sp[..., None] * n_st + sl[..., None] * nl, m_new), (c_st, n_st, m_st)

    init = (jnp.zeros((B, H, DH, DH), jnp.float32), jnp.zeros((B, H, DH), jnp.float32),
            jnp.zeros((B, H), jnp.float32))
    xs = (c_loc.transpose(2, 0, 1, 3, 4), n_loc.transpose(2, 0, 1, 3),
          a_max.transpose(2, 0, 1), b_last.transpose(2, 0, 1))
    _, (c_prev, n_prev, m_prev) = lax.scan(step, init, xs)
    c_prev = c_prev.transpose(1, 2, 0, 3, 4)
    n_prev = n_prev.transpose(1, 2, 0, 3)
    m_prev = m_prev.transpose(1, 2, 0)[..., None]

    m_t = jnp.maximum(b + m_prev, m_intra)
    inter = jnp.exp(b + m_prev - m_t)
    scores = jnp.einsum('bhctd,bhcsd->bhcts', q, k) * jnp.exp(d_log - m_t[..., None])
    num = (inter[..., None] * jnp.einsum('bhctk,bhckv->bhctv', q, c_prev)
           + jnp.einsum('bhcts,bhcsv->bhctv', scores, v))
    den = inter * jnp.einsum('bhctk,bhck->bhct', q, n_prev) + jnp.sum(scores, axis=-1)
    h = num / jnp.maximum(jnp.abs(den), jnp.exp(-m_t))[..., None]
    return h.transpose(0, 2, 3, 1, 4).reshape(B, S, H * DH)

def conv_mla_layer(h, positions, w_in, conv_w, q_norm, kv_norm, w_uq, w_ukv, w_out):
    proj = jnp.einsum('bsd,df->bsf', h, w_in)
    b_gate, c_gate, hc, c_q, c_kv, k_r = _split(proj, HYB_SPLITS)
    y_a = short_conv_mixer(b_gate, c_gate, hc, conv_w)
    y_b = mla_mixer(c_q, c_kv, k_r, positions, q_norm, kv_norm, w_uq, w_ukv)
    return jnp.einsum('bsf,fd->bsd', jnp.concatenate([y_a, y_b], axis=-1), w_out)

def mlstm_layer(h, w_in, b_i, b_f, head_norm, w_out):
    B, S, _ = h.shape
    proj = jnp.einsum('bsd,df->bsf', h, w_in)
    q, k, v, o, i_pre, f_pre = _split(proj, ML_SPLITS)
    heads = lambda a: a.astype(jnp.float32).reshape(B, S, ML_HEADS, ML_DH)
    cell = mlstm_cell(heads(q), heads(k), heads(v),
                      i_pre.astype(jnp.float32) + b_i.astype(jnp.float32),
                      f_pre.astype(jnp.float32) + b_f.astype(jnp.float32)).astype(h.dtype)
    cell = rmsnorm(cell.reshape(B, S, ML_HEADS, ML_DH), head_norm.reshape(ML_HEADS, ML_DH)).reshape(B, S, D_MODEL)
    return jnp.einsum('bsf,fd->bsd', jax.nn.sigmoid(o) * cell, w_out)

def squared_relu_mlp(h, w1, w2):
    return jnp.einsum('bsf,fd->bsd', jnp.square(jax.nn.relu(jnp.einsum('bsd,df->bsf', h, w1))), w2)

def setup_inputs(seed: int = 0) -> dict:
    key = jax.random.key(seed)
    ks = jax.random.split(key, 24)
    nrm = lambda k, shape, fan_in: jax.random.normal(k, shape, jnp.float32) * (fan_in ** -0.5)
    gain = lambda k, shape: 1.0 + 0.05 * jax.random.normal(k, shape, jnp.float32)
    offset = jax.random.randint(ks[1], (BATCH, 1), 0, POS_OFFSET_MAX, dtype=jnp.int32)
    return {
        'x': jax.random.normal(ks[0], (BATCH, SEQ, D_MODEL), jnp.float32),
        'positions': offset + jnp.arange(SEQ, dtype=jnp.int32)[None, :],
        'norm_mix_pre': gain(ks[2], (DEPTH, D_MODEL)),
        'norm_mix_post': gain(ks[3], (DEPTH, D_MODEL)),
        'norm_mlp_pre': gain(ks[4], (DEPTH, D_MODEL)),
        'norm_mlp_post': gain(ks[5], (DEPTH, D_MODEL)),
        'hyb_w_in': nrm(ks[6], (N_EVEN, D_MODEL, HYB_IN), D_MODEL),
        'conv_w': nrm(ks[7], (N_EVEN, CONV_WIDTH, CONV_DIM), CONV_WIDTH),
        'mla_q_norm': gain(ks[8], (N_EVEN, MLA_Q_RANK)),
        'mla_kv_norm': gain(ks[9], (N_EVEN, MLA_KV_RANK)),
        'mla_w_uq': nrm(ks[10], (N_EVEN, MLA_Q_RANK, MLA_HEADS * (MLA_NOPE + MLA_ROPE)), MLA_Q_RANK),
        'mla_w_ukv': nrm(ks[11], (N_EVEN, MLA_KV_RANK, MLA_HEADS * (MLA_NOPE + MLA_V)), MLA_KV_RANK),
        'hyb_w_out': nrm(ks[12], (N_EVEN, D_MODEL, D_MODEL), D_MODEL),
        'ml_w_in': nrm(ks[13], (N_ODD, D_MODEL, ML_IN), D_MODEL),
        'ml_b_i': 0.1 * jax.random.normal(ks[14], (N_ODD, ML_HEADS), jnp.float32),
        'ml_b_f': jnp.linspace(3.0, 6.0, ML_HEADS, dtype=jnp.float32)[None, :]
                  + 0.1 * jax.random.normal(ks[15], (N_ODD, ML_HEADS), jnp.float32),
        'ml_head_norm': gain(ks[16], (N_ODD, D_MODEL)),
        'ml_w_out': nrm(ks[17], (N_ODD, D_MODEL, D_MODEL), D_MODEL),
        'mlp_w1': nrm(ks[18], (DEPTH, D_MODEL, D_FF), D_MODEL),
        'mlp_w2': nrm(ks[19], (DEPTH, D_FF, D_MODEL), D_FF),
    }

def reference(x, positions, norm_mix_pre, norm_mix_post, norm_mlp_pre, norm_mlp_post,
              hyb_w_in, conv_w, mla_q_norm, mla_kv_norm, mla_w_uq, mla_w_ukv, hyb_w_out,
              ml_w_in, ml_b_i, ml_b_f, ml_head_norm, ml_w_out, mlp_w1, mlp_w2):
    for l in range(DEPTH):
        h = rmsnorm(x, norm_mix_pre[l])
        if l % 2 == 0:
            e = l // 2
            y = conv_mla_layer(h, positions, hyb_w_in[e], conv_w[e], mla_q_norm[e], mla_kv_norm[e],
                               mla_w_uq[e], mla_w_ukv[e], hyb_w_out[e])
        else:
            o = l // 2
            y = mlstm_layer(h, ml_w_in[o], ml_b_i[o], ml_b_f[o], ml_head_norm[o], ml_w_out[o])
        x = x + rmsnorm(y, norm_mix_post[l])
        h = rmsnorm(x, norm_mlp_pre[l])
        x = x + rmsnorm(squared_relu_mlp(h, mlp_w1[l], mlp_w2[l]), norm_mlp_post[l])
    return x


_drawn_inputs = setup_inputs


def setup_inputs(seed=0):
    import zlib

    import numpy as np

    out = dict(_drawn_inputs(seed))
    spreads = {}
    factors = {'mla_q_norm': 7.481, 'mla_kv_norm': 5.295, 'ml_b_i': 64.0}
    for name, (base, spread) in spreads.items():
        noise = np.random.default_rng([zlib.crc32(name.encode()), seed]).standard_normal(out[name].shape)
        drawn = base * np.exp(spread * noise) if base else spread * noise
        out[name] = __import__('jax').numpy.asarray(drawn.astype(out[name].dtype))
    for name, factor in factors.items():
        out[name] = (out[name] * factor).astype(out[name].dtype)
    return out
```

```python
import concourse.bass as bass
from concourse import mybir
from contextlib import ExitStack

P = 128
D, S, DFF = 1024, 512, 4096
EPS = 1e-6
NT = S // P
KT = D // P
CW = 512
CK = 4
HEADS, NOPE, ROPE, VD = 8, 64, 32, 64
QK = NOPE + ROPE
RANK = 256
ML_HEADS, DH = 4, 256
CHUNK = 64
ATT_SCALE = float(QK) ** -0.5
ML_SCALE = float(DH) ** -0.5
NEG = -3.0e38
FH = 2
FG = DFF // FH // CW
PAIRS = [(s, t) for t in range(NT) for s in range(t + 1)]

MAGIC = 12582912.0
BIG = 25735.927018207585
BIG_PARTS = (25600.0, 136.0, BIG - 25736.0)
TWO_PI = 6.283185307179586
C2 = 0.0019350051879882812
PI_PARTS = (6.28125, C2, TWO_PI - 6.28125 - C2)
PI_MAX = 3.1415925


def build_schedule():
    a, b, none = (1, 1, 1, 1, 0, 0, 0, 0), (0, 0, 0, 0, 1, 1, 1, 1), (0,) * 8
    aw, bw = (1, 1, 1, 0, 0, 0, 0, 0), (0, 0, 0, 0, 1, 1, 1, 0)

    def times(u, n):
        return tuple(n * x for x in u)

    def plus(u, v):
        return tuple(x + y for x, y in zip(u, v))

    mlp = [("w1a", times(a, FG), times(aw, FG), 2 * FG), ("w2a", times(b, 2), times(bw, 2), 8),
           ("w1b", times(a, FG), times(aw, FG), 2 * FG), ("w2b", times(b, 2), times(bw, 2), 8)]
    phases = [
        ("norm0", times(a, 2), times(a, 2), 0),
        ("latent", a, aw, 2),
        ("krope", (0, 0, 0, 0, 1, 0, 0, 0), (0, 0, 0, 0, 1, 0, 0, 0), 0),
        ("bgate", a, aw, 2),
        ("sumsq", (0, 0, 0, 0, 0, 1, 1, 0), (0, 0, 0, 0, 0, 1, 1, 0), 0),
        ("cgate", a, aw, 2),
        ("hconv", a, aw, 2),
        ("uq", times(a, 2), plus(a, aw), 1),
        ("ukv", plus(a, b), plus(a, bw), 1),
        ("att", (16, 16, 16, 16, 2, 2, 2, 2), (16, 16, 16, 16, 1, 1, 1, 1), 0),
        ("out0", times(b, 2), times(bw, 2), 4),
        ("norm1", times(a, 2), times(a, 2), 0),
        *[(n + "0", u, v, c) for n, u, v, c in mlp],
        ("norm2", times(a, 2), times(a, 2), 0),
        ("gates", (0, 0, 0, 0, 1, 0, 0, 0), (0, 0, 0, 0, 1, 0, 0, 0), 0),
        ("qk", times(a, 4), times(aw, 4), 8),
        ("ogate", times(a, 2), times(aw, 2), 4),
        ("v", times(b, 2), times(bw, 2), 4),
        ("core", (0, 0, 0, 1, 4, 4, 4, 4), (4, 8, 8, 1, 4, 4, 4, 4), 0),
        ("cellT", times(a, 2), times(a, 2), 0),
        ("out1", times(b, 2), times(bw, 2), 4),
        ("norm3", times(a, 2), times(a, 2), 0),
        *[(n + "1", u, v, c) for n, u, v, c in mlp],
    ]
    drains, readies, chunks = {}, {}, {}
    d, r, c = none, none, 0
    for name, uses, ready, n in phases:
        drains[name], readies[name], chunks[name] = d, r, c
        d, r, c = plus(d, uses), plus(r, ready), c + n
    return drains, readies, chunks


def trunk(nc, x_in, pos_in, g_mix_pre, g_mix_post, g_mlp_pre, g_mlp_post, w_hyb, conv_w, q_gain, kv_gain,
          w_uq, w_ukv, w_hyb_out, w_ml, ml_bi, ml_bf, head_gain, w_ml_out, w_mlp1, w_mlp2, rope_const, out):
    fp32, f32r, i32 = mybir.dt.float32, mybir.dt.float32r, mybir.dt.int32
    ACT, ALU, AX = mybir.ActivationFunctionType, mybir.AluOpType, mybir.AxisListType
    DR, RD, CH = build_schedule()

    with ExitStack() as ctx:
        base = 16512
        assert nc.sbuf_base <= base

        def at(name, offset, shape, dt=fp32):
            return nc.alloc_sbuf_tensor_at(name, shape, dt, offset=base + offset)

        def sem(name):
            return ctx.enter_context(nc.semaphore(name))

        o = 0
        x = at("x", o, [P, NT, D]); o += 16384
        Y = o; o += 16512
        y_acc = at("y_acc", Y, [P, NT, D])
        lat_hi = at("lat_hi", Y, [P, 4, S], f32r)
        lat_lo = at("lat_lo", Y + 8192, [P, 4, S], f32r)
        v_aug = at("v_aug", Y, [P, NT, ML_HEADS, DH + 1])
        aT_hi = at("aT_hi", o, [P, KT, S], f32r); o += 16384
        aT_lo = at("aT_lo", o, [P, KT, S], f32r); o += 16384
        raw = [at(f"raw{i}", o + 8192 * i, [P, CK * CW]) for i in range(2)]; o += 16384
        w_hi = [at(f"w_hi{i}", o + 16384 * i, [P, CK * CW], f32r) for i in range(2)]
        w_lo = [at(f"w_lo{i}", o + 16384 * i + 8192, [P, CK * CW], f32r) for i in range(2)]; o += 32768
        A = o; o += 65536
        uT_hi = at("uT_hi", A, [P, DFF // FH // P, S], f32r)
        uT_lo = at("uT_lo", A + 32768, [P, DFF // FH // P, S], f32r)
        q_mla = at("q_mla", A, [QK, HEADS, S])
        k_mla = at("k_mla", A + 16384, [QK, HEADS, S])
        v_mla = at("v_mla", A + 32768, [P, NT, HEADS * VD])
        probs = at("probs", A + 40960, [P, 2, S])
        probsT = at("probsT", A + 45056, [P, 2, NT, P])
        b_conv = at("b_conv", A + 49152, [P, 4, S])
        c_conv = at("c_conv", A + 57344, [P, 4, S])
        lat_raw = at("lat_raw", A, [P, 4, S])
        lat_sq = at("lat_sq", A + 8192, [P, 4, S])
        lat_rstd = at("lat_rstd", A + 40960, [P, 2, S])
        lat_f = at("lat_f", A + 32768, [P, 4, S])
        u_conv = at("u_conv", A + 40960, [P, 4, S])
        qk_ml = at("qk_ml", A, [P, 16, S])
        o_ml = at("o_ml", A + 32768, [P, 8, S])
        cell = at("cell", A + 49152, [P, NT, D])
        g_post = at("g_post", o, [P, D]); o += 4096
        g_pre = at("g_pre", o, [P, D]); o += 4096
        head_sel = at("head_sel", o - 4096, [ML_HEADS, ML_HEADS * P])
        H = o; o += 8192
        h_tok = at("h_tok", H, [P, 2, D])
        cos_t = at("cos_t", H, [P, S])
        sin_t = at("sin_t", H + 2048, [P, S])
        rot_a = at("rot_a", H + 4096, [P, S])
        rot_b = at("rot_b", H + 6144, [P, S])
        row_i = at("row_i", H, [ML_HEADS, S])
        row_f = at("row_f", H + 2048, [ML_HEADS, S])
        row_b = at("row_b", H + 4096, [ML_HEADS, S])
        row_m = at("row_m", H + 6144, [ML_HEADS, S])
        R = o; o += 8192
        relu = at("relu", R, [P, 2, S])
        usq = at("usq", R + 4096, [P, 2, S])
        junk = at("junk", R, [P, D])
        y_nrm = at("y_nrm", R + 4096, [P, D])
        pos_i = at("pos_i", R, [P, S], i32)
        ang = at("ang", R + 2048, [P, S])
        turns = at("turns", R + 4096, [P, S])
        half_sin = at("half_sin", R + 6144, [P, S])
        e_row = at("e_row", R, [ML_HEADS, S])
        zero_row = at("zero_row", R + 2048, [ML_HEADS, S])
        abs_row = at("abs_row", R + 4096, [ML_HEADS, S])
        e_gate = at("e_gate", R, [P, 2, S])
        e_gate1 = at("e_gate1", R + 4096, [P, 2, S])
        decay = at("decay", R, [P, 2, S])
        wgtT = at("wgtT", R + 4096, [P, 2, S])
        cell_f = at("cell_f", R, [P, 2, S])
        small_hi = at("small_hi", o, [P, KT, 64], f32r); o += 2048
        small_lo = at("small_lo", o, [P, KT, 64], f32r); o += 2048
        small_f = at("small_f", R + 6144, [P, KT, 64])
        small_raw = at("small_raw", o, [P, KT, 32]); o += 1024
        ident = at("ident", o, [P, P]); o += 512
        ones = at("ones", o, [P, P]); o += 512
        ucol = at("ucol", o, [P, len(PAIRS) + NT, ML_HEADS]); o += 256
        cols = at("cols", o, [P, 192]); o += 768
        assert base + o <= nc.sbuf_usable_end

        def col(i, n=1, p=P):
            return cols[0:p, i:i + n]

        C_QG, C_KVG, C_CONV, C_HEAD, C_INV, C_SIGN, C_BI, C_BF = 0, 2, 4, 16, 24, 25, 26, 27
        C_SSY, C_RY, C_SSX, C_RX = 28, 32, 36, 40
        C_EPS = 44
        C_NMAX, C_RSUM, C_RINV = 48, 80, 112
        C_DEN, C_RDEN, C_RH = 144, 145, 164

        bank = [ctx.enter_context(nc.psum_tensor(f"bank{i}", [P, S], fp32)) for i in range(8)]

        raw_in = [sem(f"raw_in{i}") for i in range(2)]
        hi_split = sem("hi_split")
        lo_split = sem("lo_split")
        chunk_done = sem("chunk_done")
        tile_ready = [sem(f"tile_ready{i}") for i in range(8)]
        drained = [sem(f"drained{i}") for i in range(8)]
        x_in_sem = [sem(f"x_in{i}") for i in range(NT)]
        const_in = sem("const_in")
        small_in = [sem(f"small_in{i}") for i in range(2)]
        pos_in_sem = sem("pos_in")
        gain_in = [sem(f"gain_in{i}") for i in range(4)]
        final_gain_in = sem("final_gain_in")
        pool_const = sem("pool_const")
        pool_step = sem("pool_step")
        dve_done = sem("dve_done")
        act_done = sem("act_done")
        y_sq = sem("y_sq")
        x_sq = sem("x_sq")
        x_new = sem("x_new")
        h_ready = sem("h_ready")
        aT_hi_ready = sem("aT_hi_ready")
        aT_ready = sem("aT_ready")
        small_f_ready = sem("small_f_ready")
        small_hi_ready = sem("small_hi_ready")
        small_ready = sem("small_ready")
        lat_copied = sem("lat_copied")
        lat_sq_ready = sem("lat_sq_ready")
        lat_f_ready = sem("lat_f_ready")
        lat_hi_ready = sem("lat_hi_ready")
        lat_ready = sem("lat_ready")
        angle_ready = sem("angle_ready")
        half_sin_ready = sem("half_sin_ready")
        sin_raw_ready = sem("sin_raw_ready")
        k_rope_ready = sem("k_rope_ready")
        ya_f_ready = sem("ya_f_ready")
        ya_hi_ready = sem("ya_hi_ready")
        ya_ready = sem("ya_ready")
        q_rope_ready = sem("q_rope_ready")
        nmax_ready = sem("nmax_ready")
        yb_f_ready = sem("yb_f_ready")
        u_sq = sem("u_sq")
        u_hi_ready = sem("u_hi_ready")
        u_ready = sem("u_ready")
        gate_f = sem("gate_f")
        gate_ln = sem("gate_ln")
        rows_ready = sem("rows_ready")
        row_step = sem("row_step")
        ucol_ready = sem("ucol_ready")
        v_ones = sem("v_ones")
        o_ready = sem("o_ready")
        o_plus1 = sem("o_plus1")
        decay_raw = sem("decay_raw")
        decay_ready = sem("decay_ready")
        wgt_ready = sem("wgt_ready")
        den_ready = sem("den_ready")
        rms_h_ready = sem("rms_h_ready")
        cell_ready = sem("cell_ready")
        ssh_ready = sem("ssh_ready")
        cell_hi_ready = sem("cell_hi_ready")
        sel_ready = sem("sel_ready")
        pv_done = sem("pv_done")
        out_sem = sem("out_stored")

        block = ctx.enter_context(nc.Block())

        def uq_parts(dst, src):
            d = dst[:, :].rearrange("p (k f) -> p k f", k=2)
            s = src[:, 0:2 * HEADS * QK].rearrange("p (k h f) -> p k h f", k=2, h=HEADS)
            half = ROPE // 2
            for k in range(2):
                yield d[:, k, 0:512].rearrange("p (h f) -> p h f", h=HEADS), s[:, k, :, 0:NOPE]
                yield d[:, k, 512:768].rearrange("p (h f) -> p h f", h=HEADS), s[:, k, :, NOPE:QK]
                swap = d[:, k, 768:1024].rearrange("p (h f) -> p h f", h=HEADS)
                yield swap[:, :, 0:half], s[:, k, :, NOPE + half:QK]
                yield swap[:, :, half:ROPE], s[:, k, :, NOPE:NOPE + half]

        def ukv_parts(dst, src):
            d = dst[:, :].rearrange("p (k f) -> p k f", k=2)
            s = src[:, :].rearrange("p (k h f) -> p k h f", k=2, h=HEADS)
            for k in range(2):
                for n in range(2):
                    yield (d[:, k, n * 512:(n + 1) * 512].rearrange("p (h f) -> p h f", h=HEADS),
                           s[:, k, :, n * 64:(n + 1) * 64])

        def weighted_ready(eng, phase, b, rnd, chunk):
            if b in (3, 7):
                eng.wait_ge(chunk_done, chunk + 1)
            else:
                eng.wait_ge(tile_ready[b], RD[phase][b] + rnd + 1)

        @block.sync
        def _(sp):
            def load(c, half, src, k=CK, first=False):
                if not first:
                    sp.wait_ge(lo_split, c - 1)
                sp.dma_start(raw[half][:, 0:k * src.shape[-1]].rearrange("p (k f) -> p k f", k=k),
                             src.rearrange("(k p) f -> p k f", p=P)).then_inc(raw_in[half], 16)

            def gains(i, post, pre):
                sp.wait_ge(h_ready, NT * i)
                sp.dma_start(g_post[:, :], post.to_broadcast([P, D])).then_inc(gain_in[i], 16)
                sp.dma_start(g_pre[:, :], pre.to_broadcast([P, D])).then_inc(gain_in[i], 16)

            for t in range(NT):
                sp.dma_start(x[:, t, :], x_in[t * P:(t + 1) * P, :]).then_inc(x_in_sem[t], 16)
                if t == 0:
                    sp.dma_start(g_pre[:, :], g_mix_pre[0:1, :].to_broadcast([P, D])).then_inc(gain_in[0], 16)
            c = CH["latent"]
            for kc in range(2):
                load(c + kc, kc, w_hyb[kc * CW:(kc + 1) * CW, 1536:2048], first=True)
            sp.dma_start(small_raw[:, :, :], w_hyb[:, 2048:2080].rearrange("(k p) f -> p k f", p=P)).then_inc(
                small_in[0], 16)
            with nc.allow_non_contiguous_dma(reason="a few KiB of per-feature constants"):
                for dst, src in ((col(C_QG, 2), q_gain.rearrange("a (j p) -> p (a j)", p=P)),
                                 (col(C_KVG, 2), kv_gain.rearrange("a (j p) -> p (a j)", p=P)),
                                 (col(C_HEAD, 8), head_gain.rearrange("a (j p) -> p (a j)", p=P)),
                                 (col(C_INV, 2), rope_const[:, :]),
                                 (col(C_BI, 1, ML_HEADS), ml_bi.rearrange("a h -> h a")),
                                 (col(C_BF, 1, ML_HEADS), ml_bf.rearrange("a h -> h a"))):
                    sp.dma_start(dst, src).then_inc(const_in, 16)
                sp.dma_start(col(C_CONV, 12).rearrange("p (w j) -> p w j", w=3),
                             conv_w.rearrange("w (j p) -> p w j", p=P)).then_inc(const_in, 16)
            sp.wait_ge(x_sq, NT)
            sp.dma_start(pos_i[:, :], pos_in[0:1, :].to_broadcast([P, S])).then_inc(pos_in_sem, 16)
            for phase, col0 in (("bgate", 0), ("cgate", 512), ("hconv", 1024)):
                for kc in range(2):
                    load(CH[phase] + kc, kc, w_hyb[kc * CW:(kc + 1) * CW, col0:col0 + CW])
            load(CH["uq"], 0, w_uq, k=2)
            load(CH["ukv"], 1, w_ukv, k=2)

            def load_out(phase, w):
                for n in range(2):
                    for kc in range(2):
                        load(CH[phase] + 2 * n + kc, kc, w[kc * CW:(kc + 1) * CW, n * CW:(n + 1) * CW])

            load_out("out0", w_hyb_out)

            def load_mlp(l, stage_gains):
                for h in range(FH):
                    c1, c2 = CH[f"w1{'ab'[h]}{l}"], CH[f"w2{'ab'[h]}{l}"]
                    with sp.Fori(0, FG) as g:
                        for kc in range(2):
                            load(g * 2 + (c1 + kc), kc, w_mlp1[l, kc * CW:(kc + 1) * CW,
                                                              bass.ds(g * CW + h * FG * CW, CW)])
                    if h == 0:
                        stage_gains()
                    with sp.Fori(0, 2) as n:
                        for kc in range(4):
                            row = h * (DFF // FH) + kc * CW
                            load(n * 4 + (c2 + kc), kc % 2, w_mlp2[l, row:row + CW, bass.ds(n * CW, CW)])

            def gains_1():
                gains(2, g_mlp_post[0:1, :], g_mix_pre[1:2, :])

            load_mlp(0, gains_1)
            sp.wait_ge(small_f_ready, 1)
            sp.dma_start(small_raw[:, :, 0:8], w_ml[:, 4096:4104].rearrange("(k p) f -> p k f", p=P)).then_inc(
                small_in[1], 16)
            with sp.Fori(0, 4) as g:
                for kc in range(2):
                    load(g * 2 + (CH["qk"] + kc), kc, w_ml[kc * CW:(kc + 1) * CW, bass.ds(g * CW, CW)])
            with sp.Fori(0, 2) as g:
                for kc in range(2):
                    load(g * 2 + (CH["ogate"] + kc), kc, w_ml[kc * CW:(kc + 1) * CW, bass.ds(g * CW + 3072, CW)])
            with sp.Fori(0, 2) as g:
                for kc in range(2):
                    load(g * 2 + (CH["v"] + kc), kc, w_ml[kc * CW:(kc + 1) * CW, bass.ds(g * CW + 2048, CW)])
            load_out("out1", w_ml_out)

            def gains_3():
                sp.wait_ge(h_ready, NT * 4)
                sp.dma_start(g_post[:, :], g_mlp_post[1:2, :].to_broadcast([P, D])).then_inc(final_gain_in, 16)

            load_mlp(1, gains_3)
            for t in range(NT):
                sp.wait_ge(x_new, NT * 3 + t + 1)
                sp.dma_start(out[t * P:(t + 1) * P, :], x[:, t, :]).then_inc(out_sem, 16)
            sp.wait_ge(out_sem, 16 * NT)

        @block.gpsimd
        def _(pool):
            def gains(i, post, pre):
                pool.wait_ge(h_ready, NT * i)
                pool.dma_start(g_post[:, :], post.to_broadcast([P, D])).then_inc(gain_in[i], 16)
                pool.dma_start(g_pre[:, :], pre.to_broadcast([P, D])).then_inc(gain_in[i], 16)

            nc.gpsimd.memset(col(C_EPS), EPS)
            nc.gpsimd.memset(ones[:, :], 1.0).then_inc(pool_step, 1)
            pool.wait_ge(pool_step, 1)
            nc.gpsimd.affine_select(out=ident[:, :], in_=ones[:, :], compare_op=ALU.is_equal, fill=0.0, base=0,
                                    pattern=[[-1, P]], channel_multiplier=1).then_inc(pool_const, 1)
            gains(1, g_mix_post[0:1, :], g_mlp_pre[0:1, :])
            pool.wait_ge(drained[4], DR["krope"][4] + 1)
            for h in range(HEADS):
                nc.gpsimd.tensor_tensor(k_mla[NOPE:QK, h, :], rot_a[NOPE:QK, :], rot_b[NOPE:QK, :],
                                        ALU.add).then_inc(k_rope_ready, 1)
            pool.wait_ge(h_ready, NT * 3)
            nc.gpsimd.memset(head_sel[:, :], 1.0).then_inc(pool_step, 1)
            pool.wait_ge(pool_step, 2)
            nc.gpsimd.affine_select(out=head_sel[:, :].rearrange("p (h j) -> p h j", h=ML_HEADS),
                                    in_=head_sel[:, :].rearrange("p (h j) -> p h j", h=ML_HEADS),
                                    compare_op=ALU.is_equal, fill=0.0, base=0,
                                    pattern=[[-1, ML_HEADS], [0, P]], channel_multiplier=1).then_inc(sel_ready, 1)
            for i in range(ML_HEADS * NT):
                s = i % NT
                pool.wait_ge(decay_raw, i + 1)
                nc.gpsimd.affine_select(out=decay[:, i % 2, s * P:(s + 1) * P], in_=decay[:, i % 2, s * P:(s + 1) * P],
                                        compare_op=ALU.is_ge, fill=0.0, base=0, pattern=[[1, P]],
                                        channel_multiplier=-1).then_inc(decay_ready, 1)
            pool.wait_ge(drained[7], DR["core"][7] + ML_HEADS)
            gains(3, g_mix_post[1:2, :], g_mlp_pre[1:2, :])

        @block.scalar
        def _(act):
            def copy(dst, src, scale=None):
                if scale is None:
                    return nc.scalar.activation(dst, src, ACT.Copy)
                return nc.scalar.activation(dst, src, ACT.Copy, scale=scale)

            steps = [0]

            def then(ins):
                steps[0] += 1
                ins.then_inc(act_done, 1)
                act.wait_ge(act_done, steps[0])

            def rms(dst, src, signal):
                then(nc.scalar.activation(junk[:, :], src, ACT.Square, scale=D ** -0.5, accum_out=dst))
                nc.scalar.activation(dst, dst, ACT.Sqrt, bias=col(C_EPS)).then_inc(signal, 1)

            def hi(c, half, first=False):
                act.wait_ge(raw_in[half], raw_count(c, half))
                if not first:
                    act.wait_ge(chunk_done, c - 1)
                for q in range(2):
                    copy(w_hi[half][:, q * 1024:(q + 1) * 1024], raw[half][:, q * 1024:(q + 1) * 1024]).then_inc(
                        hi_split, 1)

            def raw_count(c, half, ):
                return (c - half) * 8 + 16

            def norm_hi(stage, i0, t, b):
                for q in range(2):
                    bk = (t % 2) * 2 + q
                    act.wait_ge(tile_ready[bk], RD[stage][bk] + t // 2 + 1)
                    copy(aT_hi[:, 4 * q:4 * q + 4, t * P:(t + 1) * P],
                         bank[bk][:, :].rearrange("p (k t) -> p k t", k=4)).then_inc(aT_hi_ready, 1)

            act.wait_ge(pool_const, 1)
            for t in range(NT):
                act.wait_ge(x_in_sem[t], 16)
                rms(col(C_SSX + t), x[:, t, :], x_sq)
            hi(0, 0, first=True)
            norm_hi("norm0", 0, 0, 0)
            norm_hi("norm0", 0, 1, 0)
            hi(1, 1, first=True)
            norm_hi("norm0", 0, 2, 0)
            norm_hi("norm0", 0, 3, 0)
            act.wait_ge(small_f_ready, 1)
            copy(small_hi[:, :, :], small_f[:, :, :]).then_inc(small_hi_ready, 1)

            hi(2, 0)
            for j in range(4):
                weighted_ready(act, "latent", j, 0, CH["latent"] + 1)
                copy(lat_raw[:, j, :], bank[j][:, :]).then_inc(drained[j], 1)
            hi(3, 1)
            hi(4, 0)
            for j in range(4):
                weighted_ready(act, "bgate", j, 0, CH["bgate"] + 1)
                copy(b_conv[:, j, :], bank[j][:, :]).then_inc(drained[j], 1)
            act.wait_ge(angle_ready, 1)
            nc.scalar.activation(half_sin[:, :], ang[:, :], ACT.Sin, scale=0.5).then_inc(half_sin_ready, 1)
            nc.scalar.activation(turns[:, :], ang[:, :], ACT.Sin).then_inc(sin_raw_ready, 1)
            for n in range(2):
                act.wait_ge(tile_ready[5 + n], RD["sumsq"][5 + n] + 1)
                nc.scalar.activation(lat_rstd[:, n, :], bank[5 + n][:, :], ACT.Sqrt, bias=col(C_EPS),
                                     scale=1.0 / RANK).then_inc(drained[5 + n], 1)
            hi(5, 1)
            hi(6, 0)
            for j in range(4):
                weighted_ready(act, "cgate", j, 0, CH["cgate"] + 1)
                copy(c_conv[:, j, :], bank[j][:, :]).then_inc(drained[j], 1)
            for j in range(4):
                act.wait_ge(lat_f_ready, j + 1)
                copy(lat_hi[:, j, :], lat_f[:, j, :]).then_inc(lat_hi_ready, 1)
            hi(7, 1)

            def laid_out(c, half, parts):
                act.wait_ge(raw_in[half], raw_count(c, half))
                act.wait_ge(chunk_done, c - 1)
                for n, (dst, src) in enumerate(parts(w_hi[half], raw[half])):
                    ins = copy(dst, src)
                    if n == 0:
                        first = ins
                first.then_inc(hi_split, 1)
                ins.then_inc(hi_split, 1)

            laid_out(8, 0, uq_parts)
            act.wait_ge(chunk_done, CH["hconv"] + 2)
            for j in range(4):
                act.wait_ge(ya_f_ready, j + 1)
                copy(aT_hi[:, j, :], b_conv[:, j, :]).then_inc(ya_hi_ready, 1)
            laid_out(9, 1, ukv_parts)
            act.wait_ge(lat_ready, 4)
            for j in range(4):
                act.wait_ge(tile_ready[j], RD["uq"][j] + 1)
                copy(q_mla[0:NOPE, 2 * j, :], bank[j][0:64, :], ATT_SCALE)
                copy(q_mla[0:NOPE, 2 * j + 1, :], bank[j][64:128, :], ATT_SCALE).then_inc(drained[j], 1)
            hi(10, 0)
            for j in range(4):
                act.wait_ge(tile_ready[j], RD["ukv"][j] + 1)
                copy(k_mla[0:NOPE, 2 * j, :], bank[j][0:64, :])
                copy(k_mla[0:NOPE, 2 * j + 1, :], bank[j][64:128, :]).then_inc(drained[j], 1)
            for t in range(NT):
                weighted_ready(act, "ukv", 4 + t, 0, CH["ukv"])
                copy(v_mla[:, t, :], bank[4 + t][:, :]).then_inc(drained[4 + t], 1)
            hi(11, 1)
            def att_exp(u):
                qt, h = u // HEADS, u % HEADS
                kv = (qt + 1) * P
                act.wait_ge(nmax_ready, u + 1)
                if u >= 2:
                    act.wait_ge(tile_ready[2 + u % 2], RD["att"][2 + u % 2] + u // 2)
                nc.scalar.activation(probs[:, u % 2, 0:kv], bank[u % 2][:, 0:kv], ACT.Exp, bias=col(C_NMAX + u),
                                     accum_out=col(C_RSUM + u)).then_inc(drained[u % 2], 1)

            def att_T(u):
                qt = u // HEADS
                bk = 2 + u % 2
                act.wait_ge(tile_ready[bk], RD["att"][bk] + u // 2 + 1)
                if u >= 2:
                    act.wait_ge(pv_done, u - 1)
                copy(probsT[:, u % 2, 0:qt + 1, :], bank[bk][:, 0:(qt + 1) * P].rearrange(
                    "p (s t) -> p s t", t=P)).then_inc(drained[bk], 1)

            def yb_hi(qt):
                act.wait_ge(tile_ready[4 + qt], RD["att"][4 + qt] + 1)
                copy(aT_hi[:, 4:8, qt * P:(qt + 1) * P], bank[4 + qt][:, :].rearrange(
                    "p (k t) -> p k t", k=4)).then_inc(ya_hi_ready, 1)

            for u in range(NT * HEADS + 1):
                if u < NT * HEADS:
                    att_exp(u)
                if u >= 1:
                    att_T(u - 1)
                if u % HEADS == 4 and u > HEADS:
                    yb_hi(u // HEADS - 1)
            yb_hi(NT - 1)

            def rows_out(phase, rnd, chunk, dst):
                for t in range(NT):
                    weighted_ready(act, phase, 4 + t, rnd, chunk)
                    copy(dst(t), bank[4 + t][:, :]).then_inc(drained[4 + t], 1)

            def norm_stage(i, phase, next_chunk, last=False):
                for t in range(NT):
                    if t == 3 and next_chunk is not None:
                        hi(next_chunk, 0)
                    act.wait_ge(drained[4 + t], DR[phase][4 + t] + 2)
                    if t >= 2 and not last:
                        norm_hi(f"norm{i}", 0, t - 2, 0)
                    rms(col(C_SSY + t), y_acc[:, t, :], y_sq)
                    if not last:
                        act.wait_ge(x_new, NT * (i - 1) + t + 1)
                        rms(col(C_SSX + t), x[:, t, :], x_sq)
                if not last:
                    norm_hi(f"norm{i}", 0, 2, 0)
                    norm_hi(f"norm{i}", 0, 3, 0)

            def out_proj(i, phase):
                c = CH[phase]
                hi(c + 2, 0)
                rows_out(phase, 0, c + 1, lambda t: y_acc[:, t, 0:CW])
                hi(c + 3, 1)
                norm_stage(i, phase, c + 4)

            def mlp(l, i, next_chunk):
                for h in range(FH):
                    p1, p2 = f"w1{'ab'[h]}{l}", f"w2{'ab'[h]}{l}"
                    c1, c2 = CH[p1], CH[p2]
                    u0 = (l * FH + h) * 4 * FG
                    with act.Fori(0, FG) as g:
                        hi(g * 2 + (c1 + 1), 1)
                        hi(g * 2 + (c1 + 2), 0)
                        for j in range(4):
                            if j == 3:
                                act.wait_ge(chunk_done, g * 2 + (c1 + 2))
                            else:
                                act.wait_ge(tile_ready[j], g + (RD[p1][j] + 1))
                            act.wait_ge(u_sq, g * 4 + (u0 + j - 1 + 2))
                            nc.scalar.activation(relu[:, j % 2, :], bank[j][:, :], ACT.Relu).then_inc(drained[j], 1)
                            act.wait_ge(drained[j], g + (DR[p1][j] + 1))
                            nc.scalar.activation(uT_hi[:, bass.ds(g * 4 + j, 1), :].rearrange("p a t -> p (a t)"),
                                                 relu[:, j % 2, :], ACT.Square).then_inc(u_hi_ready, 1)
                    if h == 0:
                        with act.Fori(0, 2) as n:
                            for k in range(4):
                                hi(n * 4 + (c2 + k + 1), (k + 1) % 2)
                            for t in range(NT):
                                if t == 3:
                                    act.wait_ge(chunk_done, n * 4 + (c2 + 4))
                                else:
                                    act.wait_ge(tile_ready[4 + t], n + (RD[p2][4 + t] + 1))
                                copy(y_acc[:, t, bass.ds(n * CW, CW)], bank[4 + t][:, :]).then_inc(drained[4 + t], 1)
                    else:
                        for k in range(4):
                            hi(c2 + k + 1, (k + 1) % 2)
                        for k in range(4, 7):
                            hi(c2 + k + 1, (k + 1) % 2)
                        norm_stage(i, p2, next_chunk, last=next_chunk is None)

            out_proj(1, "out0")
            mlp(0, 2, CH["qk"])

            act.wait_ge(small_f_ready, 2)
            copy(small_hi[:, :, :], small_f[:, :, :]).then_inc(small_hi_ready, 1)
            act.wait_ge(gate_f, 1)
            then(nc.scalar.activation(e_row[:, :], abs_row[:, :], ACT.Exp, scale=-1.0))
            nc.scalar.activation(e_row[:, :], e_row[:, :], ACT.Ln, bias=1.0).then_inc(gate_ln, 1)
            c = CH["qk"]
            with act.Fori(0, 4) as g:
                hi(g * 2 + (c + 1), 1)
                hi(g * 2 + (c + 2), 0)
                for j in range(4):
                    if j == 3:
                        act.wait_ge(chunk_done, g * 2 + (c + 2))
                    else:
                        act.wait_ge(tile_ready[j], g + (RD["qk"][j] + 1))
                    copy(qk_ml[:, bass.ds(g * 4 + j, 1), :].rearrange("p a t -> p (a t)"),
                         bank[j][:, :]).then_inc(drained[j], 1)
            act.wait_ge(rows_ready, 1)
            c = CH["ogate"]
            for g in range(2):
                hi(c + 2 * g + 1, 1)
                hi(c + 2 * g + 2, 0)
                for j in range(4):
                    n = 4 * g + j
                    weighted_ready(act, "ogate", j, g, c + 2 * g + 1)
                    if n >= 2:
                        act.wait_ge(o_plus1, n - 1)
                    nc.scalar.activation(e_gate[:, n % 2, :], bank[j][:, :], ACT.Exp, scale=-1.0).then_inc(
                        drained[j], 1)
            c = CH["v"]
            for g in range(2):
                hi(c + 2 * g + 1, 1)
                hi(c + 2 * g + 2, 0)
                for t in range(NT):
                    weighted_ready(act, "v", 4 + t, g, c + 2 * g + 1)
                    copy(v_aug[:, t, 2 * g:2 * g + 2, 0:DH], bank[4 + t][:, :].rearrange(
                        "p (h d) -> p h d", h=2)).then_inc(drained[4 + t], 1)
            act.wait_ge(tile_ready[3], RD["core"][3] + 1)
            then(copy(ucol[:, :, :], bank[3][:, 0:4 * (len(PAIRS) + NT)].rearrange("p (c h) -> p c h", h=ML_HEADS)))
            nc.scalar.activation(ucol[:, len(PAIRS):, :], ucol[:, len(PAIRS):, :], ACT.Exp, scale=-1.0).then_inc(
                drained[3], 1)
            hi(CH["out1"] + 1, 1)
            act.wait_ge(o_ready, 8)
            posts = [(h, t) for h in range(ML_HEADS) for t in range(NT)]

            def post_sq(h, t):
                n = h * NT + t
                act.wait_ge(den_ready, n + 1)
                nc.scalar.activation(cell[:, t, h * DH:(h + 1) * DH], bank[4 + t][:, 0:DH], ACT.Square,
                                     scale=col(C_RDEN + 5 * (n % 4)),
                                     accum_out=col(C_RH + n)).then_inc(ssh_ready, 1)

            for h, s in posts:
                i = h * NT + s
                if s == 0:
                    act.wait_ge(tile_ready[0], RD["core"][0] + h + 1)
                if i >= 2:
                    act.wait_ge(wgt_ready, i - 1)
                for t in range(s, NT):
                    ins = nc.scalar.activation(decay[:, i % 2, t * P:(t + 1) * P], bank[0][:, t * P:(t + 1) * P],
                                               ACT.Exp, bias=ucol[:, PAIRS.index((s, t)), h:h + 1])
                ins.then_inc(decay_raw, 1)
                if i >= 2 and s != 1:
                    post_sq(*posts[i - 2])
                if i >= 2 and s == 0:
                    post_sq(*posts[i - 1])
            post_sq(*posts[-2])
            post_sq(*posts[-1])
            act.wait_ge(ssh_ready, 16)
            nc.scalar.activation(col(C_RH, 16), col(C_RH, 16), ACT.Sqrt, bias=col(C_EPS),
                                 scale=1.0 / DH).then_inc(rms_h_ready, 1)
            for f in range(8):
                act.wait_ge(drained[f % 4], DR["cellT"][f % 4] + f // 4 + 1)
                copy(aT_hi[:, f, :], cell_f[:, f % 2, :]).then_inc(cell_hi_ready, 1)
            out_proj(3, "out1")
            mlp(1, 4, None)

        @block.vector
        def _(dve):
            V = nc.vector
            steps = [0]

            def then(ins):
                steps[0] += 1
                ins.then_inc(dve_done, 1)
                dve.wait_ge(dve_done, steps[0])

            def lo(c, half):
                for q in range(2):
                    dve.wait_ge(hi_split, c * 2 + (q + 1))
                    ins = V.tensor_tensor(w_lo[half][:, q * 1024:(q + 1) * 1024], raw[half][:, q * 1024:(q + 1) * 1024],
                                          w_hi[half][:, q * 1024:(q + 1) * 1024].bitcast(fp32), ALU.subtract)
                ins.then_inc(lo_split, 1)

            def laid_out(c, half, parts):
                dve.wait_ge(hi_split, 2 * c + 2)
                hs = [h for h, _ in parts(w_hi[half], raw[half])]
                for h, (dst, src) in zip(hs, parts(w_lo[half], raw[half])):
                    ins = V.tensor_tensor(dst, src, h.bitcast(fp32), ALU.subtract)
                ins.then_inc(lo_split, 1)

            def norm_lo(stage, i0, t):
                for q in range(2):
                    bk = (t % 2) * 2 + q
                    dve.wait_ge(aT_hi_ready, i0 + 2 * t + q + 1)
                    dst = slice(t * P, (t + 1) * P)
                    V.tensor_tensor(aT_lo[:, 4 * q:4 * q + 4, dst], bank[bk][:, :].rearrange("p (k t) -> p k t", k=4),
                                    aT_hi[:, 4 * q:4 * q + 4, dst].bitcast(fp32), ALU.subtract).then_inc(drained[bk], 1)

            def pre_norm(i, t):
                dve.wait_ge(x_sq, NT * i + t + 1)
                then(V.reciprocal(col(C_RX + t), col(C_SSX + t)))
                if t >= 2:
                    dve.wait_ge(tile_ready[(t % 2) * 2 + 1], RD[f"norm{i}"][(t % 2) * 2 + 1] + 1)
                V.scalar_tensor_tensor(h_tok[:, t % 2, :], x[:, t, :], col(C_RX + t), g_pre[:, :], ALU.mult,
                                       ALU.mult).then_inc(h_ready, 1)

            dve.wait_ge(gain_in[0], 16)
            for t in range(NT):
                pre_norm(0, t)
                if t == 1:
                    lo(0, 0)
                if t >= 1:
                    norm_lo("norm0", 0, t - 1)
            lo(1, 1)
            norm_lo("norm0", 0, 3)
            dve.wait_ge(small_in[0], 16)
            V.tensor_copy(small_f[:, :, 0:32], small_raw[:, :, :])
            V.tensor_copy(small_f[:, :, 32:48], small_raw[:, :, 16:32])
            V.tensor_copy(small_f[:, :, 48:64], small_raw[:, :, 0:16]).then_inc(small_f_ready, 1)
            dve.wait_ge(small_hi_ready, 1)
            V.tensor_tensor(small_lo[:, :, :], small_f[:, :, :], small_hi[:, :, :].bitcast(fp32),
                            ALU.subtract).then_inc(small_ready, 1)
            lo(2, 0)
            for j in range(4):
                dve.wait_ge(drained[j], DR["latent"][j] + 1)
                V.tensor_tensor(lat_sq[:, j, :], lat_raw[:, j, :], lat_raw[:, j, :], ALU.mult).then_inc(lat_sq_ready, 1)
            lo(3, 1)
            dve.wait_ge(const_in, 16 * 7)
            dve.wait_ge(pos_in_sem, 16)
            dve.wait_ge(small_ready, 1)
            then(V.tensor_scalar(ang[:, :], pos_i[:, :], col(C_INV), None, ALU.mult))
            for period, parts in ((BIG, BIG_PARTS), (TWO_PI, PI_PARTS)):
                then(V.tensor_scalar(turns[:, :], ang[:, :], 1.0 / period, MAGIC, ALU.mult, ALU.add))
                then(V.tensor_scalar(turns[:, :], turns[:, :], MAGIC, None, ALU.subtract))
                for part in parts:
                    then(V.scalar_tensor_tensor(ang[:, :], turns[:, :], -part, ang[:, :], ALU.mult, ALU.add))
            V.tensor_scalar(ang[:, :], ang[:, :], PI_MAX, -PI_MAX, ALU.min, ALU.max).then_inc(angle_ready, 1)
            lo(4, 0)
            dve.wait_ge(half_sin_ready, 1)
            then(V.tensor_tensor(cos_t[:, :], half_sin[:, :], half_sin[:, :], ALU.mult))
            then(V.tensor_scalar(cos_t[:, :], cos_t[:, :], -2.0, 1.0, ALU.mult, ALU.add))
            dve.wait_ge(sin_raw_ready, 1)
            then(V.tensor_scalar(sin_t[:, :], turns[:, :], col(C_SIGN), None, ALU.mult))
            dve.wait_ge(tile_ready[4], RD["krope"][4] + 1)
            V.tensor_tensor(rot_a[NOPE:QK, :], bank[4][0:32, :], cos_t[0:32, :], ALU.mult)
            V.tensor_tensor(rot_b[NOPE:QK, :], bank[4][32:64, :], sin_t[32:64, :], ALU.mult).then_inc(drained[4], 1)
            for n in range(2):
                dve.wait_ge(drained[5 + n], DR["sumsq"][5 + n] + 1)
                then(V.reciprocal(lat_rstd[:, n, :], lat_rstd[:, n, :]))
            for j in range(4):
                V.scalar_tensor_tensor(lat_f[:, j, :], lat_raw[:, j, :], col((C_QG if j < 2 else C_KVG) + j % 2),
                                       lat_rstd[:, j // 2, :], ALU.mult, ALU.mult).then_inc(lat_f_ready, 1)
            lo(5, 1)
            lo(6, 0)
            for j in range(4):
                dve.wait_ge(lat_hi_ready, j + 1)
                V.tensor_tensor(lat_lo[:, j, :], lat_f[:, j, :], lat_hi[:, j, :].bitcast(fp32),
                                ALU.subtract).then_inc(lat_ready, 1)
            lo(7, 1)
            laid_out(8, 0, uq_parts)
            for j in range(4):
                weighted_ready(dve, "hconv", j, 0, CH["hconv"] + 1)
                V.tensor_tensor(u_conv[:, j, :], c_conv[:, j, :], bank[j][:, :], ALU.mult).then_inc(drained[j], 1)
            for j in range(4):
                def tap(w):
                    return col(C_CONV + 4 * w + j)
                if j == 0:
                    dve.wait_ge(drained[3], DR["hconv"][3] + 1)
                then(V.tensor_scalar(c_conv[:, j, :], u_conv[:, j, :], tap(2), None, ALU.mult))
                then(V.scalar_tensor_tensor(c_conv[:, j, 1:S], u_conv[:, j, 0:S - 1], tap(1), c_conv[:, j, 1:S],
                                            ALU.mult, ALU.add))
                then(V.scalar_tensor_tensor(c_conv[:, j, 2:S], u_conv[:, j, 0:S - 2], tap(0), c_conv[:, j, 2:S],
                                            ALU.mult, ALU.add))
                V.tensor_tensor(b_conv[:, j, :], b_conv[:, j, :], c_conv[:, j, :], ALU.mult).then_inc(ya_f_ready, 1)
            for j in range(4):
                dve.wait_ge(ya_hi_ready, j + 1)
                V.tensor_tensor(aT_lo[:, j, :], b_conv[:, j, :], aT_hi[:, j, :].bitcast(fp32),
                                ALU.subtract).then_inc(ya_ready, 1)
            laid_out(9, 1, ukv_parts)
            dve.wait_ge(k_rope_ready, HEADS)
            for n in range(2):
                dve.wait_ge(tile_ready[n], RD["uq"][n] + 2)
                V.scalar_tensor_tensor(rot_a[:, :], bank[n][:, :], ATT_SCALE, cos_t[:, :], ALU.mult,
                                       ALU.mult).then_inc(drained[n], 1)
                if n == 0:
                    dve.wait_ge(tile_ready[2], RD["uq"][2] + 2)
                else:
                    dve.wait_ge(chunk_done, CH["uq"] + 1)
                V.scalar_tensor_tensor(rot_b[:, :], bank[2 + n][:, :], ATT_SCALE, sin_t[:, :], ALU.mult,
                                       ALU.mult).then_inc(drained[2 + n], 1)
                dve.wait_ge(drained[n], DR["uq"][n] + 2)
                dve.wait_ge(drained[2 + n], DR["uq"][2 + n] + 2)
                for r in range(4):
                    ins = V.tensor_tensor(q_mla[NOPE:QK, 4 * n + r, :], rot_a[32 * r:32 * r + 32, :],
                                          rot_b[32 * r:32 * r + 32, :], ALU.add)
                ins.then_inc(q_rope_ready, 1)
                dve.wait_ge(q_rope_ready, n + 1)
            lo(10, 0)
            lo(11, 1)

            def att_max(u):
                qt, h = u // HEADS, u % HEADS
                kv = (qt + 1) * P
                dve.wait_ge(tile_ready[u % 2], RD["att"][u % 2] + u // 2 + 1)
                then(V.memset(bank[u % 2][0:CHUNK, kv - CHUNK:kv], NEG))
                V.tensor_reduce(col(C_NMAX + u), bank[u % 2][:, 0:kv], AX.X, ALU.max, negate=True).then_inc(
                    nmax_ready, 1)

            def att_norm(qt):
                u0 = qt * HEADS
                dve.wait_ge(pv_done, u0 + HEADS)
                then(V.reciprocal(col(C_RINV + u0, HEADS), col(C_RSUM + u0, HEADS)))
                V.tensor_tensor(y_acc[:, qt, 0:512].rearrange("p (h d) -> p h d", h=HEADS),
                                bank[4 + qt][:, :].rearrange("p (h d) -> p h d", h=HEADS),
                                col(C_RINV + u0, HEADS).unsqueeze(2).to_broadcast([P, HEADS, VD]),
                                ALU.mult).then_inc(drained[4 + qt], 1)

            def yb_lo(qt):
                dve.wait_ge(ya_hi_ready, 4 + qt + 1)
                V.tensor_tensor(aT_lo[:, 4:8, qt * P:(qt + 1) * P],
                                bank[4 + qt][:, :].rearrange("p (k t) -> p k t", k=4),
                                aT_hi[:, 4:8, qt * P:(qt + 1) * P].bitcast(fp32),
                                ALU.subtract).then_inc(drained[4 + qt], 1)

            for u in range(NT * HEADS):
                att_max(u)
                if u % HEADS == 2 and u > HEADS:
                    att_norm(u // HEADS - 1)
                if u % HEADS == 5 and u > HEADS:
                    yb_lo(u // HEADS - 1)
            att_norm(NT - 1)
            yb_lo(NT - 1)

            def norm_stage(i, phase, add, next_chunk, last=False):
                dve.wait_ge(final_gain_in if last else gain_in[i], 16 if last else 32)
                for t in range(NT):
                    if t == 3 and next_chunk is not None:
                        lo(next_chunk, 0)
                    weighted_ready(dve, phase, 4 + t, 1, CH[phase] + (8 if add else 4) - 1)
                    if add:
                        V.tensor_tensor(y_acc[:, t, CW:D], y_acc[:, t, CW:D], bank[4 + t][:, :],
                                        ALU.add).then_inc(drained[4 + t], 1)
                    else:
                        V.tensor_copy(y_acc[:, t, CW:D], bank[4 + t][:, :]).then_inc(drained[4 + t], 1)
                    if t >= 2 and not last:
                        norm_lo(f"norm{i}", 8 * i, t - 2)
                    dve.wait_ge(y_sq, NT * (i - 1) + t + 1)
                    then(V.reciprocal(col(C_RY + t), col(C_SSY + t)))
                    then(V.scalar_tensor_tensor(y_nrm[:, :], y_acc[:, t, :], col(C_RY + t), g_post[:, :], ALU.mult,
                                                ALU.mult))
                    V.tensor_tensor(x[:, t, :], x[:, t, :], y_nrm[:, :], ALU.add).then_inc(x_new, 1)
                    if not last:
                        pre_norm(i, t)
                if not last:
                    norm_lo(f"norm{i}", 8 * i, 2)
                    norm_lo(f"norm{i}", 8 * i, 3)

            def out_proj(i, phase):
                c = CH[phase]
                lo(c + 2, 0)
                lo(c + 3, 1)
                norm_stage(i, phase, False, c + 4)

            def mlp(l, i, next_chunk):
                for h in range(FH):
                    p1, p2 = f"w1{'ab'[h]}{l}", f"w2{'ab'[h]}{l}"
                    c1, c2 = CH[p1], CH[p2]
                    u0 = (l * FH + h) * 4 * FG
                    with dve.Fori(0, FG) as g:
                        lo(g * 2 + (c1 + 1), 1)
                        lo(g * 2 + (c1 + 2), 0)
                        for j in range(4):
                            dve.wait_ge(drained[j], g + (DR[p1][j] + 1))
                            V.tensor_tensor(usq[:, j % 2, :], relu[:, j % 2, :], relu[:, j % 2, :],
                                            ALU.mult).then_inc(u_sq, 1)
                            dve.wait_ge(u_sq, g * 4 + (u0 + j + 1 + 2))
                            dve.wait_ge(u_hi_ready, g * 4 + (u0 + j + 1))
                            V.tensor_tensor(uT_lo[:, bass.ds(g * 4 + j, 1), :].rearrange("p a t -> p (a t)"),
                                            usq[:, j % 2, :],
                                            uT_hi[:, bass.ds(g * 4 + j, 1), :].rearrange("p a t -> p (a t)").bitcast(
                                                fp32), ALU.subtract).then_inc(u_ready, 1)
                    if h == 0:
                        with dve.Fori(0, 2) as n:
                            for k in range(4):
                                lo(n * 4 + (c2 + k + 1), (k + 1) % 2)
                    else:
                        for k in range(4):
                            lo(c2 + k + 1, (k + 1) % 2)
                        for t in range(NT):
                            weighted_ready(dve, p2, 4 + t, 0, c2 + 3)
                            V.tensor_tensor(y_acc[:, t, 0:CW], y_acc[:, t, 0:CW], bank[4 + t][:, :],
                                            ALU.add).then_inc(drained[4 + t], 1)
                        for k in range(4, 7):
                            lo(c2 + k + 1, (k + 1) % 2)
                        norm_stage(i, p2, True, next_chunk, last=next_chunk is None)

            out_proj(1, "out0")
            V.memset(col(C_DEN), 0.0).then_inc(u_sq, 2)
            mlp(0, 2, CH["qk"])

            dve.wait_ge(small_in[1], 16)
            then(V.memset(small_f[:, :, :], 0.0))
            V.tensor_copy(small_f[:, :, 0:4], small_raw[:, :, 0:4])
            V.tensor_copy(small_f[:, :, 32:36], small_raw[:, :, 4:8]).then_inc(small_f_ready, 1)
            dve.wait_ge(small_hi_ready, 2)
            V.tensor_tensor(small_lo[:, :, :], small_f[:, :, :], small_hi[:, :, :].bitcast(fp32),
                            ALU.subtract).then_inc(small_ready, 1)
            dve.wait_ge(small_ready, 2)
            V.memset(zero_row[:, :], 0.0)
            dve.wait_ge(tile_ready[4], RD["gates"][4] + 1)
            V.tensor_scalar(row_i[:, :], bank[4][0:4, :], col(C_BI, 1, 4), None, ALU.add)
            V.tensor_scalar(row_f[:, :], bank[4][32:36, :], col(C_BF, 1, 4), None, ALU.add).then_inc(drained[4], 1)
            dve.wait_ge(drained[4], DR["gates"][4] + 1)
            V.scalar_tensor_tensor(abs_row[:, :], row_f[:, :], -1.0, row_f[:, :], ALU.mult, ALU.max).then_inc(gate_f, 1)
            lo(CH["qk"] + 1, 1)
            dve.wait_ge(gate_ln, 1)
            then(V.scalar_tensor_tensor(row_f[:, :], row_f[:, :], 0.0, e_row[:, :], ALU.min, ALU.subtract))
            V.tensor_tensor_scan(row_m[:, :], row_f[:, :], row_i[:, :], 0.0, ALU.add, ALU.max)
            for t in range(NT):
                ins = V.tensor_tensor_scan(row_b[:, t * P:(t + 1) * P], row_f[:, t * P:(t + 1) * P],
                                           zero_row[:, t * P:(t + 1) * P], 0.0, ALU.add, ALU.add)
            then(ins)
            then(V.tensor_tensor(row_i[:, :], row_i[:, :], row_b[:, :], ALU.subtract))
            then(V.tensor_tensor(row_f[:, :], row_b[:, :], row_m[:, :], ALU.subtract))
            V.memset(v_aug[:, :, :, DH:DH + 1], 1.0).then_inc(rows_ready, 1)
            lo(CH["qk"] + 2, 0)
            for k in range(2, 8):
                lo(CH["qk"] + k + 1, (k + 1) % 2)
            c = CH["ogate"]
            for g in range(2):
                lo(c + 2 * g + 1, 1)
                lo(c + 2 * g + 2, 0)
                for j in range(4):
                    n = 4 * g + j
                    dve.wait_ge(drained[j], DR["ogate"][j] + g + 1)
                    V.tensor_scalar(e_gate1[:, n % 2, :], e_gate[:, n % 2, :], 1.0, None, ALU.add).then_inc(o_plus1, 1)
                    dve.wait_ge(o_plus1, n + 1)
                    V.reciprocal(o_ml[:, n, :], e_gate1[:, n % 2, :]).then_inc(o_ready, 1)
            for t in range(1, NT):
                dve.wait_ge(row_step, t)
                V.tensor_scalar(row_i[:, 0:t * P], row_i[:, 0:t * P], row_b[:, t * P - 1:t * P], None,
                                ALU.add).then_inc(rows_ready, 1)
            c = CH["v"]
            for k in range(4):
                lo(c + k + 1, (k + 1) % 2)
            lo(CH["out1"] + 1, 1)

            posts = [(h, t) for h in range(ML_HEADS) for t in range(NT)]

            def den(h, t):
                n = h * NT + t
                dve.wait_ge(tile_ready[4 + t], RD["core"][4 + t] + h + 1)
                k = 5 * (n % 4)
                floor = ucol[:, len(PAIRS) + t, h:h + 1]
                then(V.tensor_scalar(col(C_DEN + k), bank[4 + t][:, DH:DH + 1], floor, None, ALU.max))
                then(V.scalar_tensor_tensor(col(C_DEN + k), bank[4 + t][:, DH:DH + 1], -1.0, col(C_DEN + k), ALU.mult,
                                            ALU.max))
                V.reciprocal(col(C_RDEN + k), col(C_DEN + k)).then_inc(den_ready, 1)

            def divide(h, t):
                n = h * NT + t
                dve.wait_ge(ssh_ready, n + 1)
                V.tensor_scalar(cell[:, t, h * DH:(h + 1) * DH], bank[4 + t][:, 0:DH], col(C_RDEN + 5 * (n % 4)),
                                None, ALU.mult).then_inc(drained[4 + t], 1)

            dve.wait_ge(drained[3], DR["core"][3] + 1)
            for i in range(ML_HEADS * NT + 1):
                if i < ML_HEADS * NT:
                    h, s = posts[i]
                    bk = 1 + i % 2
                    dve.wait_ge(tile_ready[bk], RD["core"][bk] + i // 2 + 1)
                    dve.wait_ge(decay_ready, i + 1)
                    V.scalar_tensor_tensor(wgtT[:, i % 2, s * P:S], bank[bk][:, s * P:S], ML_SCALE,
                                           decay[:, i % 2, s * P:S], ALU.mult, ALU.mult).then_inc(wgt_ready, 1)
                if 1 <= i <= ML_HEADS * NT:
                    den(*posts[i - 1])
                if i >= 2 and i % NT != 1:
                    divide(*posts[i - 2])
                if i >= 2 and i % NT == 0:
                    divide(*posts[i - 1])
            dve.wait_ge(rms_h_ready, 1)
            then(V.reciprocal(col(C_RH, 16), col(C_RH, 16)))
            for h, t in posts:
                part = cell[:, t, h * DH:(h + 1) * DH]
                V.tensor_scalar(part, part, col(C_RH + h * NT + t), None, ALU.mult).then_inc(cell_ready, 1)

            for f in range(8):
                bk = f % 4
                dve.wait_ge(tile_ready[bk], RD["cellT"][bk] + f // 4 + 1)
                V.scalar_tensor_tensor(cell_f[:, f % 2, :], bank[bk][:, :], col(C_HEAD + f), o_ml[:, f, :], ALU.mult,
                                       ALU.mult).then_inc(drained[bk], 1)
                dve.wait_ge(cell_hi_ready, f + 1)
                V.tensor_tensor(aT_lo[:, f, :], cell_f[:, f % 2, :], aT_hi[:, f, :].bitcast(fp32),
                                ALU.subtract).then_inc(ya_ready, 1)
            out_proj(3, "out1")
            mlp(1, 4, None)

        @block.tensor
        def _(pe):
            def mm3(dst, st_hi, st_lo, mv_hi, mv_lo, start, stop):
                nc.tensor.matmul(dst, st_lo, mv_hi, start=start, stop=False)
                nc.tensor.matmul(dst, st_hi, mv_lo, start=False, stop=False)
                return nc.tensor.matmul(dst, st_hi, mv_hi, start=False, stop=stop)

            def w(half, kt, cols_):
                v = [z[half][:, :].rearrange("p (k f) -> p k f", k=CK)[:, kt, cols_] for z in (w_hi, w_lo)]
                return v

            def columns(phase, c0, rnd, loop_rnd=None):
                for kc in range(2):
                    pe.wait_ge(lo_split, c0 + (kc + 1))
                    for j in range(4):
                        if kc == 0:
                            pe.wait_ge(drained[j], rnd + DR[phase][j])
                        for kt in range(CK):
                            k = kc * CK + kt
                            wh, wl = w(kc, kt, slice(j * P, (j + 1) * P))
                            ins = mm3(bank[j][:, :], wh, wl, aT_hi[:, k, :], aT_lo[:, k, :], k == 0, k == KT - 1)
                        if j == 3:
                            ins.then_inc(chunk_done, 1)
                        elif kc == 1:
                            ins.then_inc(tile_ready[j], 1)

            def rows(phase, c0, rnd, nk, lhs_hi, lhs_lo, lhs_ready=None, norm=None, tail=False):
                def tile(kc, t):
                    if kc == 0 and t >= 0:
                        pe.wait_ge(drained[4 + t], rnd + DR[phase][4 + t])
                    for kt in range(CK):
                        k = kc * CK + kt
                        wh, wl = w(kc % 2, kt, slice(0, CW))
                        ts = slice(t * P, (t + 1) * P)
                        ins = mm3(bank[4 + t][:, :], lhs_hi[:, k, ts], lhs_lo[:, k, ts], wh, wl, k == 0,
                                  k == nk * CK - 1)
                    if t == 3:
                        ins.then_inc(chunk_done, 1)
                    elif kc == nk - 1:
                        ins.then_inc(tile_ready[4 + t], 1)

                for kc in range(nk - 2 if tail else nk):
                    pe.wait_ge(lo_split, c0 + (kc + 1))
                    if lhs_ready is not None:
                        lhs_ready(kc)
                    for t in range(NT):
                        tile(kc, t)
                if tail:
                    for kc in (nk - 2, nk - 1):
                        pe.wait_ge(lo_split, c0 + (kc + 1))
                        if lhs_ready is not None:
                            lhs_ready(kc)
                    for t in range(NT):
                        tile(nk - 2, t)
                        tile(nk - 1, t)
                        if t >= 2 and norm is not None:
                            norm_T(norm, t - 2)
                    if norm is not None:
                        norm_T(norm, 2)
                        norm_T(norm, 3)

            def norm_T(i, t):
                pe.wait_ge(h_ready, NT * i + t + 1)
                for q in range(2):
                    bk = (t % 2) * 2 + q
                    n = DR[f"norm{i}"][bk] + t // 2
                    if n:
                        pe.wait_ge(drained[bk], n)
                    for k in range(4):
                        f = (4 * q + k) * P
                        ins = nc.tensor.transpose(bank[bk][:, k * P:(k + 1) * P], h_tok[:, t % 2, f:f + P], ident[:, :])
                    ins.then_inc(tile_ready[bk], 1)

            def norm_done(i):
                for bk in range(4):
                    pe.wait_ge(drained[bk], DR[f"norm{i}"][bk] + 2)

            pe.wait_ge(pool_const, 1)
            for t in range(NT):
                norm_T(0, t)
            norm_done(0)
            columns("latent", CH["latent"], 0)
            pe.wait_ge(small_ready, 1)
            for k in range(KT):
                ins = mm3(bank[4][0:64, :], small_hi[:, k, :], small_lo[:, k, :], aT_hi[:, k, :], aT_lo[:, k, :],
                          k == 0, k == KT - 1)
            ins.then_inc(tile_ready[4], 1)
            columns("bgate", CH["bgate"], 0)
            for n in range(2):
                pe.wait_ge(lat_sq_ready, 2 * n + 2)
                nc.tensor.matmul(bank[5 + n][:, :], ones[:, :], lat_sq[:, 2 * n, :], start=True, stop=False)
                nc.tensor.matmul(bank[5 + n][:, :], ones[:, :], lat_sq[:, 2 * n + 1, :], start=False,
                                 stop=True).then_inc(tile_ready[5 + n], 1)
            columns("cgate", CH["cgate"], 0)
            columns("hconv", CH["hconv"], 0)

            def w2(half, k, c_):
                return [z[half][:, :].rearrange("p (k f) -> p k f", k=2)[:, k, c_] for z in (w_hi, w_lo)]

            pe.wait_ge(lo_split, CH["uq"] + 1)
            pe.wait_ge(lat_ready, 4)
            for rnd in range(2):
                for j in range(4):
                    pe.wait_ge(drained[j], DR["uq"][j] + rnd)
                    for k in range(2):
                        wh, wl = w2(0, k, slice((4 * rnd + j) * P, (4 * rnd + j + 1) * P))
                        ins = mm3(bank[j][:, :], wh, wl, lat_hi[:, k, :], lat_lo[:, k, :], k == 0, k == 1)
                    ins.then_inc(chunk_done if rnd == 1 and j == 3 else tile_ready[j], 1)
            pe.wait_ge(lo_split, CH["ukv"] + 1)
            for j in range(4):
                pe.wait_ge(drained[j], DR["ukv"][j])
                for k in range(2):
                    wh, wl = w2(1, k, slice(j * P, (j + 1) * P))
                    ins = mm3(bank[j][:, :], wh, wl, lat_hi[:, 2 + k, :], lat_lo[:, 2 + k, :], k == 0, k == 1)
                ins.then_inc(tile_ready[j], 1)
            for t in range(NT):
                for k in range(2):
                    wh, wl = w2(1, k, slice(512, 1024))
                    ts = slice(t * P, (t + 1) * P)
                    ins = mm3(bank[4 + t][:, :], lat_hi[:, 2 + k, ts], lat_lo[:, 2 + k, ts], wh, wl, k == 0, k == 1)
                ins.then_inc(chunk_done if t == 3 else tile_ready[4 + t], 1)

            def scores(u):
                qt, h = u // HEADS, u % HEADS
                pe.wait_ge(drained[u % 2], DR["att"][u % 2] + u // 2)
                nc.tensor.matmul(bank[u % 2][:, 0:(qt + 1) * P], q_mla[:, h, qt * P:(qt + 1) * P],
                                 k_mla[:, h, 0:(qt + 1) * P], start=True, stop=True).then_inc(tile_ready[u % 2], 1)

            def turn(u):
                qt, bk = u // HEADS, 2 + u % 2
                pe.wait_ge(drained[u % 2], DR["att"][u % 2] + u // 2 + 1)
                pe.wait_ge(drained[bk], DR["att"][bk] + u // 2)
                for s in range(qt + 1):
                    ins = nc.tensor.transpose(bank[bk][:, s * P:(s + 1) * P], probs[:, u % 2, s * P:(s + 1) * P],
                                              ident[:, :])
                ins.then_inc(tile_ready[bk], 1)

            def values(u):
                qt, h, bk = u // HEADS, u % HEADS, 2 + u % 2
                pe.wait_ge(drained[bk], DR["att"][bk] + u // 2 + 1)
                if h == 0:
                    pe.wait_ge(drained[4 + qt], DR["att"][4 + qt])
                for s in range(qt + 1):
                    ins = nc.tensor.matmul(bank[4 + qt][:, h * VD:(h + 1) * VD], probsT[:, u % 2, s, :],
                                           v_mla[:, s, h * VD:(h + 1) * VD], start=(s == 0), stop=(s == qt))
                ins.then_inc(pv_done, 1)

            def yb_T(qt):
                pe.wait_ge(drained[4 + qt], DR["att"][4 + qt] + 1)
                for k in range(4):
                    ins = nc.tensor.transpose(bank[4 + qt][:, k * P:(k + 1) * P], y_acc[:, qt, k * P:(k + 1) * P],
                                              ident[:, :])
                ins.then_inc(tile_ready[4 + qt], 1)

            pe.wait_ge(q_rope_ready, 2)
            pe.wait_ge(k_rope_ready, HEADS)
            for j in range(4):
                pe.wait_ge(drained[j], DR["ukv"][j] + 1)
                pe.wait_ge(drained[4 + j], DR["ukv"][4 + j] + 1)
            units = NT * HEADS
            scores(0)
            for u in range(units + 1):
                if u + 1 < units:
                    scores(u + 1)
                if u < units:
                    turn(u)
                if u >= 1:
                    values(u - 1)
                if u % HEADS == 3 and u > HEADS:
                    yb_T(u // HEADS - 1)
            yb_T(NT - 1)

            def out_proj(i, phase, ready):
                c = CH[phase]
                rows(phase, c, 0, 2, aT_hi, aT_lo, lhs_ready=ready)
                rows(phase, c + 2, 1, 2, aT_hi, aT_lo, norm=i, tail=True)

            def out0_ready(kc):
                if kc == 0:
                    pe.wait_ge(ya_ready, 4)
                else:
                    for qt in range(NT):
                        pe.wait_ge(drained[4 + qt], DR["att"][4 + qt] + 2)

            def mlp(l, i):
                for h in range(FH):
                    p1, p2 = f"w1{'ab'[h]}{l}", f"w2{'ab'[h]}{l}"
                    c1, c2 = CH[p1], CH[p2]
                    u0 = (l * FH + h) * 4 * FG
                    with pe.Fori(0, FG) as g:
                        columns(p1, g * 2 + c1, g)

                    def u_tiles(kc):
                        pe.wait_ge(u_ready, u0 + 4 * kc + 4)

                    if h == 0:
                        with pe.Fori(0, 2) as n:
                            rows(p2, n * 4 + c2, n, 4, uT_hi, uT_lo, lhs_ready=u_tiles)
                    else:
                        rows(p2, c2, 0, 4, uT_hi, uT_lo, lhs_ready=u_tiles)
                        rows(p2, c2 + 4, 1, 4, uT_hi, uT_lo, norm=i, tail=True)

            out_proj(1, "out0", out0_ready)
            norm_done(1)
            mlp(0, 2)
            norm_done(2)

            pe.wait_ge(small_ready, 2)
            pe.wait_ge(drained[4], DR["gates"][4])
            for k in range(KT):
                ins = mm3(bank[4][0:64, :], small_hi[:, k, :], small_lo[:, k, :], aT_hi[:, k, :], aT_lo[:, k, :],
                          k == 0, k == KT - 1)
            ins.then_inc(tile_ready[4], 1)
            with pe.Fori(0, 4) as g:
                columns("qk", g * 2 + CH["qk"], g)
            for g in range(2):
                columns("ogate", CH["ogate"] + 2 * g, g)
            pe.wait_ge(drained[3], DR["core"][3])
            for t in range(NT):
                pe.wait_ge(rows_ready, t + 1)
                for s in range(t + 1):
                    n = PAIRS.index((s, t))
                    ins = nc.tensor.transpose(bank[3][:, 4 * n:4 * n + 4], row_i[:, s * P:(s + 1) * P],
                                              ident[0:4, 0:4])
                if t < NT - 1:
                    ins.then_inc(row_step, 1)
            for t in range(NT):
                n = len(PAIRS) + t
                ins = nc.tensor.transpose(bank[3][:, 4 * n:4 * n + 4], row_m[:, t * P:(t + 1) * P], ident[0:4, 0:4])
            ins.then_inc(tile_ready[3], 1)
            for g in range(2):
                rows("v", CH["v"] + 2 * g, g, 2, aT_hi, aT_lo)
            pe.wait_ge(sel_ready, 1)
            for t in range(NT):
                pe.wait_ge(drained[4 + t], DR["v"][4 + t] + 2)

            def ml_row(h):
                if h == 0:
                    pe.wait_ge(drained[0], DR["core"][0])
                else:
                    pe.wait_ge(decay_raw, h * NT)
                nc.tensor.matmul(bank[0][:, :], head_sel[:, h * P:(h + 1) * P], row_f[:, :], start=True,
                                 stop=True).then_inc(tile_ready[0], 1)

            def ml_scores(i):
                h, s = i // NT, i % NT
                bk = 1 + i % 2
                if i >= 2:
                    pe.wait_ge(wgt_ready, i - 1)
                else:
                    pe.wait_ge(drained[bk], DR["core"][bk])
                for k in range(2):
                    ins = nc.tensor.matmul(bank[bk][:, s * P:S], qk_ml[:, 8 + 2 * h + k, s * P:(s + 1) * P],
                                           qk_ml[:, 2 * h + k, s * P:S], start=(k == 0), stop=(k == 1))
                ins.then_inc(tile_ready[bk], 1)

            def ml_values(i):
                h, s = i // NT, i % NT
                pe.wait_ge(wgt_ready, i + 1)
                for t in range(s, NT):
                    if s == 0:
                        pe.wait_ge(drained[4 + t], DR["core"][4 + t] + h)
                    ins = nc.tensor.matmul(bank[4 + t][:, 0:DH + 1], wgtT[:, i % 2, t * P:(t + 1) * P],
                                           v_aug[:, s, h, :], start=(s == 0), stop=(s == t))
                    if t == s:
                        ins.then_inc(tile_ready[4 + t], 1)

            n_ml = ML_HEADS * NT
            ml_row(0)
            ml_scores(0)
            for i in range(n_ml):
                if i + 1 < n_ml:
                    if (i + 1) % NT == 0:
                        ml_row((i + 1) // NT)
                    ml_scores(i + 1)
                ml_values(i)
            for f in range(8):
                bk = f % 4
                pe.wait_ge(cell_ready, NT * (f // 2) + NT)
                if f >= 4:
                    pe.wait_ge(drained[bk], DR["cellT"][bk] + f // 4)
                for t in range(NT):
                    ins = nc.tensor.transpose(bank[bk][:, t * P:(t + 1) * P], cell[:, t, f * P:(f + 1) * P], ident[:, :])
                ins.then_inc(tile_ready[bk], 1)

            def out1_ready(kc):
                pe.wait_ge(ya_ready, 4 + 4 * kc + 4)

            out_proj(3, "out1", out1_ready)
            norm_done(3)
            mlp(1, None)


_INS = ["x", "positions", "norm_mix_pre", "norm_mix_post", "norm_mlp_pre", "norm_mlp_post", "hyb_w_in", "conv_w",
        "mla_q_norm", "mla_kv_norm", "mla_w_uq", "mla_w_ukv", "hyb_w_out", "ml_w_in", "ml_b_i", "ml_b_f",
        "ml_head_norm", "ml_w_out", "mlp_w1", "mlp_w2"]
_FLAT = {"x", "hyb_w_in", "conv_w", "mla_w_uq", "mla_w_ukv", "hyb_w_out", "ml_w_in", "ml_w_out"}


def kernel(**inputs):
    import numpy as _np
    import concourse.bacc as _bacc
    from concourse import mybir as _mybir
    from concourse.bass_utils import run_bass_kernel_spmd as _run

    nc = _bacc.Bacc("TRN2", target_bir_lowering=False, num_devices=1)
    arrays, args = {}, []

    def give(name, a):
        arrays[f"in_{name}_dram"] = a
        args.append(nc.dram_tensor(f"in_{name}_dram", a.shape, _mybir.dt.from_np(a.dtype), kind="ExternalInput").ap())

    for name in _INS:
        a = _np.ascontiguousarray(inputs[name])
        if name in _FLAT:
            a = a[0]
        give(name, a)
    half = ROPE // 2
    inv = _np.float32(10000.0) ** (-_np.arange(half, dtype=_np.float32) / _np.float32(half))
    sign = _np.where(_np.arange(P) % ROPE < half, -1.0, 1.0).astype(_np.float32)
    give("rope_const", _np.stack([_np.tile(inv, P // half), sign], axis=1))
    args.append(nc.dram_tensor("out_dram", (S, D), _mybir.dt.float32, kind="ExternalOutput").ap())
    trunk(nc, *args)
    r = _run(nc, [arrays], core_ids=[0])
    return r.results[0]["out_dram"].reshape(1, S, D)
```

```python
import concourse.bass as bass
from concourse import mybir
from contextlib import ExitStack

P = 128
D, S, DFF = 1024, 512, 4096
EPS = 1e-6
NT = S // P
KT = D // P
CW = 512
CK = 4
HEADS, NOPE, ROPE, VD = 8, 64, 32, 64
QK = NOPE + ROPE
RANK = 256
ML_HEADS, DH = 4, 256
CHUNK = 64
ATT_SCALE = float(QK) ** -0.5
ML_SCALE = float(DH) ** -0.5
NEG = -3.0e38
FH = 2
FG = DFF // FH // CW
PAIRS = [(s, t) for t in range(NT) for s in range(t + 1)]
FAR = [(s, t) for s, t in PAIRS if s < t]

MAGIC = 12582912.0
BIG = 25735.927018207585
BIG_PARTS = (25600.0, 136.0, BIG - 25736.0)
TWO_PI = 6.283185307179586
C2 = 0.0019350051879882812
PI_PARTS = (6.28125, C2, TWO_PI - 6.28125 - C2)
PI_MAX = 3.1415925


def build_schedule():
    a, b, none, every = (1, 1, 1, 1, 0, 0, 0, 0), (0, 0, 0, 0, 1, 1, 1, 1), (0,) * 8, (1,) * 8
    aw, bw = (1, 1, 1, 0, 0, 0, 0, 0), (0, 0, 0, 0, 1, 1, 1, 0)

    def times(u, n):
        return tuple(n * x for x in u)

    def plus(u, v):
        return tuple(x + y for x, y in zip(u, v))

    mlp = [("w1a", times(a, FG), times(aw, FG), 2 * FG), ("w2a", times(b, 2), times(bw, 2), 8),
           ("w1b", times(a, FG), times(aw, FG), 2 * FG), ("w2b", times(b, 2), times(bw, 2), 8)]
    phases = [
        ("norm0", every, every, 0),
        ("latent", a, aw, 2),
        ("krope", (0, 0, 0, 0, 1, 0, 0, 0), (0, 0, 0, 0, 1, 0, 0, 0), 0),
        ("cgate", a, aw, 2),
        ("sumsq", (0, 0, 0, 0, 0, 1, 1, 0), (0, 0, 0, 0, 0, 1, 1, 0), 0),
        ("hconv", a, aw, 2),
        ("bgate", a, aw, 2),
        ("uq", times(a, 2), plus(a, aw), 1),
        ("ukv", plus(a, b), plus(a, bw), 1),
        ("att", (16, 16, 16, 16, 2, 2, 2, 2), (16, 16, 16, 16, 1, 1, 1, 1), 0),
        ("out0", times(b, 2), times(bw, 2), 4),
        ("norm1", every, every, 0),
        *[(n + "0", u, v, c) for n, u, v, c in mlp],
        ("norm2", every, every, 0),
        ("gates", (0, 0, 0, 0, 2, 0, 0, 0), (0, 0, 0, 0, 2, 0, 0, 0), 0),
        ("qk", times(a, 4), times(aw, 4), 8),
        ("ogate", times(a, 2), times(aw, 2), 4),
        ("v", times(b, 2), times(bw, 2), 4),
        ("core", (0, 0, 0, 0, 4, 4, 4, 4), (4, 8, 8, 0, 4, 4, 4, 4), 0),
        ("cellT", times(a, 2), times(a, 2), 0),
        ("out1", times(b, 2), times(bw, 2), 4),
        ("norm3", every, every, 0),
        *[(n + "1", u, v, c) for n, u, v, c in mlp],
    ]
    drains, readies, chunks = {}, {}, {}
    d, r, c = none, none, 0
    for name, uses, ready, n in phases:
        drains[name], readies[name], chunks[name] = d, r, c
        d, r, c = plus(d, uses), plus(r, ready), c + n
    return drains, readies, chunks


def trunk(nc, x_in, pos_in, g_mix_pre, g_mix_post, g_mlp_pre, g_mlp_post, w_hyb, conv_w, q_gain, kv_gain,
          w_uq, w_ukv, w_hyb_out, w_ml, ml_bi, ml_bf, head_gain, w_ml_out, w_mlp1, w_mlp2, rope_const, out):
    fp32, f32r, i32 = mybir.dt.float32, mybir.dt.float32r, mybir.dt.int32
    ACT, ALU, AX = mybir.ActivationFunctionType, mybir.AluOpType, mybir.AxisListType
    DR, RD, CH = build_schedule()

    with ExitStack() as ctx:
        base = 16512
        assert nc.sbuf_base <= base

        def at(name, offset, shape, dt=fp32):
            return nc.alloc_sbuf_tensor_at(name, shape, dt, offset=base + offset)

        def sem(name):
            return ctx.enter_context(nc.semaphore(name))

        o = 0
        x = at("x", o, [P, NT, D]); o += 16384
        Y = o; o += 16512
        y_acc = at("y_acc", Y, [P, NT, D])
        lat_hi = at("lat_hi", Y, [P, 4, S], f32r)
        lat_lo = at("lat_lo", Y + 8192, [P, 4, S], f32r)
        v_aug = at("v_aug", Y, [P, NT, ML_HEADS, DH + 1])
        aT_hi = at("aT_hi", o, [P, KT, S], f32r); o += 16384
        aT_lo = at("aT_lo", o, [P, KT, S], f32r); o += 16384
        raw = [at(f"raw{i}", o + 8192 * i, [P, CK * CW]) for i in range(2)]; o += 16384
        w_hi = [at(f"w_hi{i}", o + 16384 * i, [P, CK * CW], f32r) for i in range(2)]
        w_lo = [at(f"w_lo{i}", o + 16384 * i + 8192, [P, CK * CW], f32r) for i in range(2)]; o += 32768
        A = o; o += 65536
        uT_hi = at("uT_hi", A, [P, DFF // FH // P, S], f32r)
        uT_lo = at("uT_lo", A + 32768, [P, DFF // FH // P, S], f32r)
        q_mla = at("q_mla", A, [QK, HEADS, S])
        k_mla = at("k_mla", A + 16384, [QK, HEADS, S])
        v_mla = at("v_mla", A + 32768, [P, NT, HEADS * VD])
        probs = at("probs", A + 40960, [P, 2, S])
        probsT = at("probsT", A + 45056, [P, 2, NT, P])
        b_conv = at("b_conv", A + 49152, [P, 4, S])
        c_conv = at("c_conv", A + 57344, [P, 4, S])
        lat_raw = at("lat_raw", A, [P, 4, S])
        lat_sq = at("lat_sq", A + 8192, [P, 4, S])
        lat_rstd = at("lat_rstd", A + 40960, [P, 2, S])
        lat_f = at("lat_f", A + 32768, [P, 4, S])
        u_conv = at("u_conv", A + 40960, [P, 4, S])
        qk_ml = at("qk_ml", A, [P, 16, S])
        o_ml = at("o_ml", A + 32768, [P, 8, S])
        cell = at("cell", A + 49152, [P, NT, D])
        g_post = at("g_post", o, [P, D]); o += 4096
        g_pre = at("g_pre", o, [P, D]); o += 4096
        head_sel = at("head_sel", o - 4096, [ML_HEADS, ML_HEADS * P])
        H = o; o += 8192
        h_tok = at("h_tok", H, [P, 2, D])
        cos_t = at("cos_t", H, [P, S])
        sin_t = at("sin_t", H + 2048, [P, S])
        rot_a = at("rot_a", H + 4096, [P, S])
        rot_b = at("rot_b", H + 6144, [P, S])
        row_i = at("row_i", H, [ML_HEADS, S])
        row_f = at("row_f", H + 2048, [ML_HEADS, S])
        row_b = at("row_b", H + 4096, [ML_HEADS, S])
        row_m = at("row_m", H + 6144, [ML_HEADS, S])
        R = o; o += 8192
        relu = at("relu", R, [P, 2, S])
        usq = at("usq", R + 4096, [P, 2, S])
        junk = at("junk", R, [P, D])
        y_gain = at("y_gain", R + 4096, [P, 2, CW])
        pos_i = at("pos_i", R, [P, S], i32)
        ang = at("ang", R + 2048, [P, S])
        turns = at("turns", R + 4096, [P, S])
        half_sin = at("half_sin", R + 6144, [P, S])
        e_row = at("e_row", R, [ML_HEADS, S])
        zero_row = at("zero_row", R + 2048, [ML_HEADS, S])
        abs_row = at("abs_row", R + 4096, [ML_HEADS, S])
        row_far = at("row_far", R + 4096, [ML_HEADS, len(FAR) * P])
        decay = at("decay", R, [P, 2, S])
        wgtT = at("wgtT", R + 4096, [P, 2, S])
        cell_f = at("cell_f", R, [P, 2, S])
        small_hi = at("small_hi", o, [P, KT, 64], f32r); o += 2048
        small_lo = at("small_lo", o, [P, KT, 64], f32r); o += 2048
        small_f = at("small_f", R + 6144, [P, KT, 64])
        small_raw = at("small_raw", o, [P, KT, 32]); o += 1024
        ident = at("ident", o, [P, P]); o += 512
        ones = at("ones", o, [P, P]); o += 512
        ucol = at("ucol", o, [P, len(PAIRS) + NT, ML_HEADS]); o += 256
        cols = at("cols", o, [P, 192]); o += 768
        assert base + o <= nc.sbuf_usable_end

        def col(i, n=1, p=P):
            return cols[0:p, i:i + n]

        C_QG, C_KVG, C_CONV, C_HEAD, C_INV, C_SIGN, C_BI, C_BF = 0, 2, 4, 16, 24, 25, 26, 27
        C_SSY, C_RY, C_SSX, C_RX = 28, 32, 36, 40
        C_EPS, C_SS0 = 44, 180
        C_BIAS = 184
        C_NMAX, C_RSUM, C_RINV = 48, 80, 112
        C_DEN, C_RDEN, C_RH = 144, 145, 164

        bank = [ctx.enter_context(nc.psum_tensor(f"bank{i}", [P, S], fp32)) for i in range(8)]

        raw_in = [sem(f"raw_in{i}") for i in range(2)]
        hi_split = sem("hi_split")
        lo_split = sem("lo_split")
        chunk_done = sem("chunk_done")
        tile_ready = [sem(f"tile_ready{i}") for i in range(8)]
        drained = [sem(f"drained{i}") for i in range(8)]
        x_in_sem = [sem(f"x_in{i}") for i in range(NT)]
        const_in = sem("const_in")
        small_in = [sem(f"small_in{i}") for i in range(2)]
        pos_in_sem = sem("pos_in")
        gain_in = [sem(f"gain_in{i}") for i in range(4)]
        final_gain_in = sem("final_gain_in")
        pool_const = sem("pool_const")
        pool_step = sem("pool_step")
        dve_done = sem("dve_done")
        act_done = sem("act_done")
        y0_sq = sem("y0_sq")
        y1_sq = sem("y1_sq")
        y0_gained = sem("y0_gained")
        y1_gained = sem("y1_gained")
        y_bias = sem("y_bias")
        y_sq = sem("y_sq")
        x_sq = sem("x_sq")
        x_new = sem("x_new")
        h_ready = sem("h_ready")
        aT_hi_ready = sem("aT_hi_ready")
        aT_ready = sem("aT_ready")
        small_f_ready = sem("small_f_ready")
        small_hi_ready = sem("small_hi_ready")
        small_ready = sem("small_ready")
        lat_copied = sem("lat_copied")
        lat_sq_ready = sem("lat_sq_ready")
        lat_f_ready = sem("lat_f_ready")
        lat_hi_ready = sem("lat_hi_ready")
        lat_ready = sem("lat_ready")
        angle_ready = sem("angle_ready")
        half_sin_ready = sem("half_sin_ready")
        sin_raw_ready = sem("sin_raw_ready")
        k_rope_ready = sem("k_rope_ready")
        ya_f_ready = sem("ya_f_ready")
        ya_hi_ready = sem("ya_hi_ready")
        ya_ready = sem("ya_ready")
        q_rope_ready = sem("q_rope_ready")
        nmax_ready = sem("nmax_ready")
        yb_f_ready = sem("yb_f_ready")
        u_sq = sem("u_sq")
        u_hi_ready = sem("u_hi_ready")
        u_ready = sem("u_ready")
        gate_f = sem("gate_f")
        gate_ln = sem("gate_ln")
        rows_ready = sem("rows_ready")
        row_step = sem("row_step")
        ucol_ready = sem("ucol_ready")
        v_ones = sem("v_ones")
        o_ready = sem("o_ready")
        o_plus1 = sem("o_plus1")
        decay_raw = sem("decay_raw")
        decay_ready = sem("decay_ready")
        wgt_ready = sem("wgt_ready")
        den_ready = sem("den_ready")
        rms_h_ready = sem("rms_h_ready")
        cell_ready = sem("cell_ready")
        ssh_ready = sem("ssh_ready")
        cell_hi_ready = sem("cell_hi_ready")
        sel_ready = sem("sel_ready")
        pv_done = sem("pv_done")
        out_sem = sem("out_stored")

        block = ctx.enter_context(nc.Block())

        def uq_parts(dst, src):
            d = dst[:, :].rearrange("p (k f) -> p k f", k=2)
            s = src[:, 0:2 * HEADS * QK].rearrange("p (k h f) -> p k h f", k=2, h=HEADS)
            half = ROPE // 2
            for k in range(2):
                yield d[:, k, 0:512].rearrange("p (h f) -> p h f", h=HEADS), s[:, k, :, 0:NOPE]
                yield d[:, k, 512:768].rearrange("p (h f) -> p h f", h=HEADS), s[:, k, :, NOPE:QK]
                swap = d[:, k, 768:1024].rearrange("p (h f) -> p h f", h=HEADS)
                yield swap[:, :, 0:half], s[:, k, :, NOPE + half:QK]
                yield swap[:, :, half:ROPE], s[:, k, :, NOPE:NOPE + half]

        def ukv_parts(dst, src):
            d = dst[:, :].rearrange("p (k f) -> p k f", k=2)
            s = src[:, :].rearrange("p (k h f) -> p k h f", k=2, h=HEADS)
            for k in range(2):
                for n in range(2):
                    yield (d[:, k, n * 512:(n + 1) * 512].rearrange("p (h f) -> p h f", h=HEADS),
                           s[:, k, :, n * 64:(n + 1) * 64])

        def weighted_ready(eng, phase, b, rnd, chunk):
            if b in (3, 7):
                eng.wait_ge(chunk_done, chunk + 1)
            else:
                eng.wait_ge(tile_ready[b], RD[phase][b] + rnd + 1)

        @block.sync
        def _(sp):
            def load(c, half, src, k=CK, first=False):
                if not first:
                    sp.wait_ge(lo_split, c - 1)
                sp.dma_start(raw[half][:, 0:k * src.shape[-1]].rearrange("p (k f) -> p k f", k=k),
                             src.rearrange("(k p) f -> p k f", p=P)).then_inc(raw_in[half], 16)

            def gains(i, post, pre):
                sp.wait_ge(h_ready, NT * i)
                sp.dma_start(g_post[:, :], post.to_broadcast([P, D])).then_inc(gain_in[i], 16)
                sp.dma_start(g_pre[:, :], pre.to_broadcast([P, D])).then_inc(gain_in[i], 16)

            c = CH["latent"]
            for t in range(NT):
                sp.dma_start(x[:, t, :], x_in[t * P:(t + 1) * P, :]).then_inc(x_in_sem[t], 16)
                if t == 0:
                    sp.dma_start(g_pre[:, :], g_mix_pre[0:1, :].to_broadcast([P, D])).then_inc(gain_in[0], 16)
                if t == 1:
                    load(c, 0, w_hyb[0:CW, 1536:2048], first=True)
            load(c + 1, 1, w_hyb[CW:2 * CW, 1536:2048], first=True)
            sp.dma_start(small_raw[:, :, :], w_hyb[:, 2048:2080].rearrange("(k p) f -> p k f", p=P)).then_inc(
                small_in[0], 16)
            with nc.allow_non_contiguous_dma(reason="a few KiB of per-feature constants"):
                for dst, src in ((col(C_QG, 2), q_gain.rearrange("a (j p) -> p (a j)", p=P)),
                                 (col(C_KVG, 2), kv_gain.rearrange("a (j p) -> p (a j)", p=P)),
                                 (col(C_HEAD, 8), head_gain.rearrange("a (j p) -> p (a j)", p=P)),
                                 (col(C_INV, 2), rope_const[:, :]),
                                 (col(C_BI, 1, ML_HEADS), ml_bi.rearrange("a h -> h a")),
                                 (col(C_BF, 1, ML_HEADS), ml_bf.rearrange("a h -> h a"))):
                    sp.dma_start(dst, src).then_inc(const_in, 16)
                sp.dma_start(col(C_CONV, 12).rearrange("p (w j) -> p w j", w=3),
                             conv_w.rearrange("w (j p) -> p w j", p=P)).then_inc(const_in, 16)
            sp.wait_ge(x_sq, NT)
            sp.dma_start(pos_i[:, :], pos_in[0:1, :].to_broadcast([P, S])).then_inc(pos_in_sem, 16)
            for phase, col0 in (("cgate", 512), ("hconv", 1024), ("bgate", 0)):
                for kc in range(2):
                    load(CH[phase] + kc, kc, w_hyb[kc * CW:(kc + 1) * CW, col0:col0 + CW])
            load(CH["uq"], 0, w_uq, k=2)
            load(CH["ukv"], 1, w_ukv, k=2)

            def load_out(phase, w):
                for n in range(2):
                    for kc in range(2):
                        load(CH[phase] + 2 * n + kc, kc, w[kc * CW:(kc + 1) * CW, n * CW:(n + 1) * CW])

            load_out("out0", w_hyb_out)

            def load_mlp(l, stage_gains):
                for h in range(FH):
                    c1, c2 = CH[f"w1{'ab'[h]}{l}"], CH[f"w2{'ab'[h]}{l}"]
                    with sp.Fori(0, FG) as g:
                        for kc in range(2):
                            load(g * 2 + (c1 + kc), kc, w_mlp1[l, kc * CW:(kc + 1) * CW,
                                                              bass.ds(g * CW + h * FG * CW, CW)])
                    if h == 0:
                        stage_gains()
                    with sp.Fori(0, 2) as n:
                        for kc in range(4):
                            row = h * (DFF // FH) + kc * CW
                            load(n * 4 + (c2 + kc), kc % 2, w_mlp2[l, row:row + CW, bass.ds(n * CW, CW)])

            def gains_1():
                gains(2, g_mlp_post[0:1, :], g_mix_pre[1:2, :])

            load_mlp(0, gains_1)
            sp.wait_ge(small_f_ready, 1)
            sp.dma_start(small_raw[:, :, 0:8], w_ml[:, 4096:4104].rearrange("(k p) f -> p k f", p=P)).then_inc(
                small_in[1], 16)
            with sp.Fori(0, 4) as g:
                for kc in range(2):
                    load(g * 2 + (CH["qk"] + kc), kc, w_ml[kc * CW:(kc + 1) * CW, bass.ds(g * CW, CW)])
            with sp.Fori(0, 2) as g:
                for kc in range(2):
                    load(g * 2 + (CH["ogate"] + kc), kc, w_ml[kc * CW:(kc + 1) * CW, bass.ds(g * CW + 3072, CW)])
            with sp.Fori(0, 2) as g:
                for kc in range(2):
                    load(g * 2 + (CH["v"] + kc), kc, w_ml[kc * CW:(kc + 1) * CW, bass.ds(g * CW + 2048, CW)])
            load_out("out1", w_ml_out)

            def gains_3():
                sp.wait_ge(h_ready, NT * 4)
                sp.dma_start(g_post[:, :], g_mlp_post[1:2, :].to_broadcast([P, D])).then_inc(final_gain_in, 16)

            load_mlp(1, gains_3)
            for t in range(NT):
                sp.wait_ge(x_new, NT * 3 + t + 1)
                sp.dma_start(out[t * P:(t + 1) * P, :], x[:, t, :]).then_inc(out_sem, 16)
            sp.wait_ge(out_sem, 16 * NT)

        @block.gpsimd
        def _(pool):
            def gains(i, post, pre):
                pool.wait_ge(h_ready, NT * i)
                pool.dma_start(g_post[:, :], post.to_broadcast([P, D])).then_inc(gain_in[i], 16)
                pool.dma_start(g_pre[:, :], pre.to_broadcast([P, D])).then_inc(gain_in[i], 16)

            nc.gpsimd.memset(col(C_EPS), EPS)
            nc.gpsimd.memset(ones[:, :], 1.0).then_inc(pool_step, 1)
            pool.wait_ge(pool_step, 1)
            nc.gpsimd.affine_select(out=ident[:, :], in_=ones[:, :], compare_op=ALU.is_equal, fill=0.0, base=0,
                                    pattern=[[-1, P]], channel_multiplier=1).then_inc(pool_const, 1)
            gains(1, g_mix_post[0:1, :], g_mlp_pre[0:1, :])
            pool.wait_ge(drained[4], DR["krope"][4] + 1)
            for h in range(HEADS):
                nc.gpsimd.tensor_tensor(k_mla[NOPE:QK, h, :], rot_a[NOPE:QK, :], rot_b[NOPE:QK, :],
                                        ALU.add).then_inc(k_rope_ready, 1)

            def y1_gain(i, phase):
                for t in range(NT):
                    pool.wait_ge(drained[4 + t], DR[phase][4 + t] + 2)
                    if t >= 2:
                        pool.wait_ge(x_new, NT * (i - 1) + t - 1)
                    nc.gpsimd.tensor_tensor(y_gain[:, t % 2, :], y_acc[:, t, CW:D], g_post[:, CW:D],
                                            ALU.mult).then_inc(y1_gained, 1)

            y1_gain(2, "w2b0")
            pool.wait_ge(h_ready, NT * 3)
            nc.gpsimd.memset(head_sel[:, :], 1.0).then_inc(pool_step, 1)
            pool.wait_ge(pool_step, 2)
            nc.gpsimd.affine_select(out=head_sel[:, :].rearrange("p (h j) -> p h j", h=ML_HEADS),
                                    in_=head_sel[:, :].rearrange("p (h j) -> p h j", h=ML_HEADS),
                                    compare_op=ALU.is_equal, fill=0.0, base=0,
                                    pattern=[[-1, ML_HEADS], [0, P]], channel_multiplier=1).then_inc(sel_ready, 1)
            for i in range(ML_HEADS * NT):
                s = i % NT
                pool.wait_ge(decay_raw, i + 1)
                nc.gpsimd.affine_select(out=decay[:, i % 2, s * P:(s + 1) * P], in_=decay[:, i % 2, s * P:(s + 1) * P],
                                        compare_op=ALU.is_ge, fill=0.0, base=0, pattern=[[1, P]],
                                        channel_multiplier=-1).then_inc(decay_ready, 1)
            pool.wait_ge(drained[7], DR["core"][7] + ML_HEADS)
            gains(3, g_mix_post[1:2, :], g_mlp_pre[1:2, :])
            y1_gain(4, "w2b1")

        @block.scalar
        def _(act):
            def copy(dst, src, scale=None):
                if scale is None:
                    return nc.scalar.activation(dst, src, ACT.Copy)
                return nc.scalar.activation(dst, src, ACT.Copy, scale=scale)

            steps = [0]

            def then(ins):
                steps[0] += 1
                ins.then_inc(act_done, 1)
                act.wait_ge(act_done, steps[0])

            def rms(dst, src, signal):
                then(nc.scalar.activation(junk[:, :], src, ACT.Square, scale=D ** -0.5, accum_out=dst))
                nc.scalar.activation(dst, dst, ACT.Sqrt, bias=col(C_EPS)).then_inc(signal, 1)

            def hi(c, half, first=False):
                act.wait_ge(raw_in[half], raw_count(c, half))
                if not first:
                    act.wait_ge(chunk_done, c - 1)
                for q in range(2):
                    copy(w_hi[half][:, q * 1024:(q + 1) * 1024], raw[half][:, q * 1024:(q + 1) * 1024]).then_inc(
                        hi_split, 1)

            def raw_count(c, half, ):
                return (c - half) * 8 + 16

            def norm_hi(stage, t):
                for q in range(2):
                    bk = 2 * t + q
                    act.wait_ge(tile_ready[bk], RD[stage][bk] + 1)
                    copy(aT_hi[:, 4 * q:4 * q + 4, t * P:(t + 1) * P],
                         bank[bk][:, :].rearrange("p (k t) -> p k t", k=4)).then_inc(aT_hi_ready, 1)

            act.wait_ge(pool_const, 1)
            then(nc.scalar.activation(col(C_RX), col(C_EPS), ACT.Sqrt))
            for t in (0, 1):
                act.wait_ge(x_in_sem[t], 16)
                rms(col(C_SSX + t), x[:, t, :], x_sq)
            hi(0, 0, first=True)
            norm_hi("norm0", 0)
            norm_hi("norm0", 1)
            for t in (2, 3):
                act.wait_ge(x_in_sem[t], 16)
                rms(col(C_SSX + t), x[:, t, :], x_sq)
            hi(1, 1, first=True)
            norm_hi("norm0", 2)
            norm_hi("norm0", 3)
            act.wait_ge(small_f_ready, 1)
            copy(small_hi[:, :, :], small_f[:, :, :]).then_inc(small_hi_ready, 1)

            c = CH["cgate"]
            hi(c, 0)
            for j in range(4):
                weighted_ready(act, "latent", j, 0, CH["latent"] + 1)
                copy(lat_raw[:, j, :], bank[j][:, :]).then_inc(drained[j], 1)
            hi(c + 1, 1)
            hi(c + 2, 0)
            act.wait_ge(angle_ready, 1)
            nc.scalar.activation(half_sin[:, :], ang[:, :], ACT.Sin, scale=0.5).then_inc(half_sin_ready, 1)
            nc.scalar.activation(turns[:, :], ang[:, :], ACT.Sin).then_inc(sin_raw_ready, 1)
            for n in range(2):
                act.wait_ge(tile_ready[5 + n], RD["sumsq"][5 + n] + 1)
                nc.scalar.activation(lat_rstd[:, n, :], bank[5 + n][:, :], ACT.Sqrt, bias=col(C_EPS),
                                     scale=1.0 / RANK).then_inc(drained[5 + n], 1)
            for j in range(4):
                weighted_ready(act, "cgate", j, 0, CH["cgate"] + 1)
                copy(c_conv[:, j, :], bank[j][:, :]).then_inc(drained[j], 1)
            hi(c + 3, 1)
            for j in range(4):
                act.wait_ge(lat_f_ready, j + 1)
                copy(lat_hi[:, j, :], lat_f[:, j, :]).then_inc(lat_hi_ready, 1)
            hi(c + 4, 0)
            hi(c + 5, 1)

            def laid_out(c, half, parts):
                act.wait_ge(raw_in[half], raw_count(c, half))
                act.wait_ge(chunk_done, c - 1)
                for n, (dst, src) in enumerate(parts(w_hi[half], raw[half])):
                    ins = copy(dst, src)
                    if n == 0:
                        first = ins
                first.then_inc(hi_split, 1)
                ins.then_inc(hi_split, 1)

            laid_out(CH["uq"], 0, uq_parts)
            laid_out(CH["ukv"], 1, ukv_parts)
            for j in range(4):
                act.wait_ge(drained[j], DR["bgate"][j] + 1)
                copy(aT_hi[:, j, :], b_conv[:, j, :]).then_inc(ya_hi_ready, 1)
            act.wait_ge(lat_ready, 4)
            for j in range(4):
                act.wait_ge(tile_ready[j], RD["uq"][j] + 1)
                copy(q_mla[0:NOPE, 2 * j, :], bank[j][0:64, :], ATT_SCALE)
                copy(q_mla[0:NOPE, 2 * j + 1, :], bank[j][64:128, :], ATT_SCALE).then_inc(drained[j], 1)
            hi(CH["out0"], 0)
            for j in range(4):
                act.wait_ge(tile_ready[j], RD["ukv"][j] + 1)
                copy(k_mla[0:NOPE, 2 * j, :], bank[j][0:64, :])
                copy(k_mla[0:NOPE, 2 * j + 1, :], bank[j][64:128, :]).then_inc(drained[j], 1)
            for t in range(NT):
                weighted_ready(act, "ukv", 4 + t, 0, CH["ukv"])
                if t == 0:
                    then(nc.scalar.activation(col(C_RX), col(C_EPS), ACT.Exp))
                copy(v_mla[:, t, :], bank[4 + t][:, :]).then_inc(drained[4 + t], 1)
            def att_exp(u):
                qt, h = u // HEADS, u % HEADS
                kv = (qt + 1) * P
                act.wait_ge(nmax_ready, u + 1)
                if u >= 2:
                    act.wait_ge(tile_ready[2 + u % 2], RD["att"][2 + u % 2] + u // 2)
                nc.scalar.activation(probs[:, u % 2, 0:kv], bank[u % 2][:, 0:kv], ACT.Exp, bias=col(C_NMAX + u),
                                     accum_out=col(C_RSUM + u)).then_inc(drained[u % 2], 1)

            def att_T(u):
                qt = u // HEADS
                bk = 2 + u % 2
                act.wait_ge(tile_ready[bk], RD["att"][bk] + u // 2 + 1)
                if u >= 2:
                    act.wait_ge(pv_done, u - 1)
                copy(probsT[:, u % 2, 0:qt + 1, :], bank[bk][:, 0:(qt + 1) * P].rearrange(
                    "p (s t) -> p s t", t=P)).then_inc(drained[bk], 1)

            def yb_hi(qt):
                act.wait_ge(tile_ready[4 + qt], RD["att"][4 + qt] + 1)
                copy(aT_hi[:, 4:8, qt * P:(qt + 1) * P], bank[4 + qt][:, :].rearrange(
                    "p (k t) -> p k t", k=4)).then_inc(ya_hi_ready, 1)

            for u in range(NT * HEADS + 1):
                if u < NT * HEADS:
                    att_exp(u)
                if u >= 1:
                    att_T(u - 1)
                if u == 2:
                    hi(CH["out0"] + 1, 1)
                if u % HEADS == 4 and u > HEADS:
                    yb_hi(u // HEADS - 1)
            yb_hi(NT - 1)

            def y0_squares(i, phase):
                for t in range(NT):
                    act.wait_ge(drained[4 + t], DR[phase][4 + t] + 1)
                    if t:
                        act.wait_ge(y0_sq, NT * (i - 1) + t)
                    nc.scalar.activation(junk[:, 0:CW], y_acc[:, t, 0:CW], ACT.Square, scale=D ** -0.5,
                                         accum_out=col(C_SS0 + t)).then_inc(y0_sq, 1)

            def norm_stage(i, phase, add, next_chunk, last=False):
                def y_rms(t):
                    if add:
                        act.wait_ge(drained[4 + t], DR[phase][4 + t] + 2)
                        y1 = y_acc[:, t, CW:D]
                    else:
                        weighted_ready(act, phase, 4 + t, 1, CH[phase] + 3)
                        y1 = bank[4 + t][:, :]
                    nc.scalar.activation(junk[:, 0:CW], y1, ACT.Square, scale=D ** -0.5,
                                         accum_out=col(C_SSY + t)).then_inc(y1_sq, 1)
                    act.wait_ge(y1_sq, NT * (i - 1) + t + 1)
                    nc.scalar.activation(col(C_SSY + t), col(C_SSY + t), ACT.Sqrt,
                                         bias=col(C_BIAS + t)).then_inc(y_sq, 1)

                def x_rms(t):
                    act.wait_ge(x_new, NT * (i - 1) + t + 1)
                    rms(col(C_SSX + t), x[:, t, :], x_sq)

                act.wait_ge(y_bias, i)
                if last:
                    for t in range(NT):
                        y_rms(t)
                    return
                y_rms(0)
                for t in (0, 1):
                    if t == 0 and not add:
                        y_rms(1)
                    x_rms(t)
                    if t == 0 and add:
                        y_rms(1)
                norm_hi(f"norm{i}", 0)
                hi(next_chunk, 0)
                norm_hi(f"norm{i}", 1)
                y_rms(2)
                if not add:
                    y_rms(3)
                hi(next_chunk + 1, 1)
                x_rms(2)
                if add:
                    y_rms(3)
                norm_hi(f"norm{i}", 2)
                x_rms(3)
                norm_hi(f"norm{i}", 3)

            def out_proj(i, phase):
                c = CH[phase]
                hi(c + 2, 0)
                for t in range(NT):
                    if t == 3:
                        hi(c + 3, 1)
                    weighted_ready(act, phase, 4 + t, 0, c + 1)
                    copy(y_acc[:, t, 0:CW], bank[4 + t][:, :]).then_inc(drained[4 + t], 1)
                y0_squares(i, phase)
                norm_stage(i, phase, False, c + 4)

            def mlp(l, i, next_chunk):
                for h in range(FH):
                    p1, p2 = f"w1{'ab'[h]}{l}", f"w2{'ab'[h]}{l}"
                    c1, c2 = CH[p1], CH[p2]
                    u0 = (l * FH + h) * 4 * FG

                    def group(g):
                        hi(g * 2 + (c1 + 2), 0)
                        for j in range(4):
                            if j == 3:
                                act.wait_ge(chunk_done, g * 2 + (c1 + 2))
                            else:
                                act.wait_ge(tile_ready[j], g + (RD[p1][j] + 1))
                            act.wait_ge(u_sq, g * 4 + (u0 + j - 1 + 2))
                            nc.scalar.activation(relu[:, j % 2, :], bank[j][:, :], ACT.Relu).then_inc(drained[j], 1)
                            act.wait_ge(drained[j], g + (DR[p1][j] + 1))
                            nc.scalar.activation(uT_hi[:, bass.ds(g * 4 + j, 1), :].rearrange("p a t -> p (a t)"),
                                                 relu[:, j % 2, :], ACT.Square).then_inc(u_hi_ready, 1)

                    if h == 0:
                        group(0)
                    with act.Fori(1 - h, FG) as g:
                        hi(g * 2 + (c1 + 1), 1)
                        group(g)
                    if h == 0:
                        with act.Fori(0, 2) as n:
                            for k in range(4):
                                hi(n * 4 + (c2 + k + 1), (k + 1) % 2)
                            for t in range(NT):
                                if t == 3:
                                    act.wait_ge(chunk_done, n * 4 + (c2 + 4))
                                else:
                                    act.wait_ge(tile_ready[4 + t], n + (RD[p2][4 + t] + 1))
                                copy(y_acc[:, t, bass.ds(n * CW, CW)], bank[4 + t][:, :]).then_inc(drained[4 + t], 1)
                    else:
                        for k in range(4):
                            hi(c2 + k + 1, (k + 1) % 2)
                        hi(c2 + 5, 1)
                        y0_squares(i, p2)
                        hi(c2 + 6, 0)
                        hi(c2 + 7, 1)
                        norm_stage(i, p2, True, next_chunk, last=next_chunk is None)

            out_proj(1, "out0")
            mlp(0, 2, CH["qk"])

            c = CH["qk"]

            def qk_group(g):
                hi(g * 2 + (c + 2), 0)
                for j in range(4):
                    if j == 3:
                        act.wait_ge(chunk_done, g * 2 + (c + 2))
                    else:
                        act.wait_ge(tile_ready[j], g + (RD["qk"][j] + 1))
                    copy(qk_ml[:, bass.ds(g * 4 + j, 1), :].rearrange("p a t -> p (a t)"),
                         bank[j][:, :]).then_inc(drained[j], 1)

            act.wait_ge(small_f_ready, 2)
            copy(small_hi[:, :, :], small_f[:, :, :]).then_inc(small_hi_ready, 1)
            qk_group(0)
            hi(c + 3, 1)
            act.wait_ge(gate_f, 1)
            then(nc.scalar.activation(e_row[:, :], abs_row[:, :], ACT.Exp, scale=-1.0))
            nc.scalar.activation(e_row[:, :], e_row[:, :], ACT.Ln, bias=1.0).then_inc(gate_ln, 1)
            qk_group(1)
            act.wait_ge(tile_ready[4], RD["gates"][4] + 2)
            then(copy(ucol[:, :, :], bank[4][:, 0:4 * (len(PAIRS) + NT)].rearrange("p (c h) -> p c h", h=ML_HEADS)))
            nc.scalar.activation(ucol[:, len(PAIRS):, :], ucol[:, len(PAIRS):, :], ACT.Exp, scale=-1.0).then_inc(
                drained[4], 1)
            with act.Fori(2, 4) as g:
                hi(g * 2 + (c + 1), 1)
                qk_group(g)
            c = CH["ogate"]
            for g in range(2):
                hi(c + 2 * g + 1, 1)
                hi(c + 2 * g + 2, 0)
                for j in range(4):
                    weighted_ready(act, "ogate", j, g, c + 2 * g + 1)
                    nc.scalar.activation(o_ml[:, 4 * g + j, :], bank[j][:, :], ACT.Sigmoid).then_inc(drained[j], 1)
            act.wait_ge(rows_ready, 1)
            act.wait_ge(drained[4], DR["gates"][4] + 2)

            def decays(i):
                h, s = i // NT, i % NT
                if s == 0:
                    act.wait_ge(tile_ready[0], RD["core"][0] + h + 1)
                if i >= 2:
                    act.wait_ge(wgt_ready, i - 1)
                for t in range(s, NT):
                    ins = nc.scalar.activation(decay[:, i % 2, t * P:(t + 1) * P], bank[0][:, t * P:(t + 1) * P],
                                               ACT.Exp, bias=ucol[:, PAIRS.index((s, t)), h:h + 1])
                ins.then_inc(decay_raw, 1)

            c = CH["v"]
            for g in range(2):
                hi(c + 2 * g + 1, 1)
                hi(c + 2 * g + 2, 0)
                if g == 1:
                    decays(0)
                    decays(1)
                for t in range(NT):
                    weighted_ready(act, "v", 4 + t, g, c + 2 * g + 1)
                    copy(v_aug[:, t, 2 * g:2 * g + 2, 0:DH], bank[4 + t][:, :].rearrange(
                        "p (h d) -> p h d", h=2)).then_inc(drained[4 + t], 1)
            posts = [(h, t) for h in range(ML_HEADS) for t in range(NT)]

            def post_sq(h, t):
                n = h * NT + t
                act.wait_ge(den_ready, n + 1)
                nc.scalar.activation(cell[:, t, h * DH:(h + 1) * DH], bank[4 + t][:, 0:DH], ACT.Square,
                                     scale=col(C_RDEN + 5 * (n % 4)),
                                     accum_out=col(C_RH + n)).then_inc(ssh_ready, 1)

            for h, s in posts:
                i = h * NT + s
                if i >= 2:
                    decays(i)
                if i == 2:
                    hi(CH["out1"] + 1, 1)
                if i >= 2 and s != 1:
                    post_sq(*posts[i - 2])
                if i >= 2 and s == 0:
                    post_sq(*posts[i - 1])
            post_sq(*posts[-2])
            post_sq(*posts[-1])
            act.wait_ge(ssh_ready, 16)
            nc.scalar.activation(col(C_RH, 16), col(C_RH, 16), ACT.Sqrt, bias=col(C_EPS),
                                 scale=1.0 / DH).then_inc(rms_h_ready, 1)
            for f in range(8):
                act.wait_ge(drained[f % 4], DR["cellT"][f % 4] + f // 4 + 1)
                copy(aT_hi[:, f, :], cell_f[:, f % 2, :]).then_inc(cell_hi_ready, 1)
            out_proj(3, "out1")
            mlp(1, 4, None)

        @block.vector
        def _(dve):
            V = nc.vector
            steps = [0]

            def then(ins):
                steps[0] += 1
                ins.then_inc(dve_done, 1)
                dve.wait_ge(dve_done, steps[0])

            def lo(c, half):
                for q in range(2):
                    dve.wait_ge(hi_split, c * 2 + (q + 1))
                    ins = V.tensor_tensor(w_lo[half][:, q * 1024:(q + 1) * 1024], raw[half][:, q * 1024:(q + 1) * 1024],
                                          w_hi[half][:, q * 1024:(q + 1) * 1024].bitcast(fp32), ALU.subtract)
                ins.then_inc(lo_split, 1)

            def laid_out(c, half, parts):
                dve.wait_ge(hi_split, 2 * c + 2)
                hs = [h for h, _ in parts(w_hi[half], raw[half])]
                for h, (dst, src) in zip(hs, parts(w_lo[half], raw[half])):
                    ins = V.tensor_tensor(dst, src, h.bitcast(fp32), ALU.subtract)
                ins.then_inc(lo_split, 1)

            def norm_lo(i, t):
                for q in range(2):
                    bk = 2 * t + q
                    dve.wait_ge(aT_hi_ready, 2 * (NT * i + t) + q + 1)
                    dst = slice(t * P, (t + 1) * P)
                    V.tensor_tensor(aT_lo[:, 4 * q:4 * q + 4, dst], bank[bk][:, :].rearrange("p (k t) -> p k t", k=4),
                                    aT_hi[:, 4 * q:4 * q + 4, dst].bitcast(fp32), ALU.subtract).then_inc(drained[bk], 1)

            def pre_norm(i, t):
                dve.wait_ge(x_sq, NT * i + t + 1)
                then(V.reciprocal(col(C_RX + t), col(C_SSX + t)))
                if t >= 2:
                    dve.wait_ge(tile_ready[2 * t - 3], RD[f"norm{i}"][2 * t - 3] + 1)
                V.scalar_tensor_tensor(h_tok[:, t % 2, :], x[:, t, :], col(C_RX + t), g_pre[:, :], ALU.mult,
                                       ALU.mult).then_inc(h_ready, 1)

            dve.wait_ge(gain_in[0], 16)
            pre_norm(0, 0)
            pre_norm(0, 1)
            lo(0, 0)
            norm_lo(0, 0)
            norm_lo(0, 1)
            pre_norm(0, 2)
            pre_norm(0, 3)
            lo(1, 1)
            norm_lo(0, 2)
            norm_lo(0, 3)
            dve.wait_ge(small_in[0], 16)
            V.tensor_copy(small_f[:, :, 0:32], small_raw[:, :, :])
            V.tensor_copy(small_f[:, :, 32:48], small_raw[:, :, 16:32])
            V.tensor_copy(small_f[:, :, 48:64], small_raw[:, :, 0:16]).then_inc(small_f_ready, 1)
            dve.wait_ge(small_hi_ready, 1)
            V.tensor_tensor(small_lo[:, :, :], small_f[:, :, :], small_hi[:, :, :].bitcast(fp32),
                            ALU.subtract).then_inc(small_ready, 1)
            lo(2, 0)
            for j in range(4):
                dve.wait_ge(drained[j], DR["latent"][j] + 1)
                V.tensor_tensor(lat_sq[:, j, :], lat_raw[:, j, :], lat_raw[:, j, :], ALU.mult).then_inc(lat_sq_ready, 1)
            lo(3, 1)
            dve.wait_ge(const_in, 16 * 7)
            dve.wait_ge(pos_in_sem, 16)
            dve.wait_ge(small_ready, 1)
            then(V.tensor_scalar(ang[:, :], pos_i[:, :], col(C_INV), None, ALU.mult))
            for period, parts in ((BIG, BIG_PARTS), (TWO_PI, PI_PARTS)):
                then(V.tensor_scalar(turns[:, :], ang[:, :], 1.0 / period, MAGIC, ALU.mult, ALU.add))
                then(V.tensor_scalar(turns[:, :], turns[:, :], MAGIC, None, ALU.subtract))
                for part in parts:
                    then(V.scalar_tensor_tensor(ang[:, :], turns[:, :], -part, ang[:, :], ALU.mult, ALU.add))
            V.tensor_scalar(ang[:, :], ang[:, :], PI_MAX, -PI_MAX, ALU.min, ALU.max).then_inc(angle_ready, 1)
            lo(4, 0)
            dve.wait_ge(half_sin_ready, 1)
            then(V.tensor_tensor(cos_t[:, :], half_sin[:, :], half_sin[:, :], ALU.mult))
            then(V.tensor_scalar(cos_t[:, :], cos_t[:, :], -2.0, 1.0, ALU.mult, ALU.add))
            dve.wait_ge(sin_raw_ready, 1)
            then(V.tensor_scalar(sin_t[:, :], turns[:, :], col(C_SIGN), None, ALU.mult))
            dve.wait_ge(tile_ready[4], RD["krope"][4] + 1)
            V.tensor_tensor(rot_a[NOPE:QK, :], bank[4][0:32, :], cos_t[0:32, :], ALU.mult)
            V.tensor_tensor(rot_b[NOPE:QK, :], bank[4][32:64, :], sin_t[32:64, :], ALU.mult).then_inc(drained[4], 1)
            for n in range(2):
                dve.wait_ge(drained[5 + n], DR["sumsq"][5 + n] + 1)
                then(V.reciprocal(lat_rstd[:, n, :], lat_rstd[:, n, :]))
            for j in range(4):
                V.scalar_tensor_tensor(lat_f[:, j, :], lat_raw[:, j, :], col((C_QG if j < 2 else C_KVG) + j % 2),
                                       lat_rstd[:, j // 2, :], ALU.mult, ALU.mult).then_inc(lat_f_ready, 1)
            lo(CH["hconv"] + 1, 1)
            for j in range(4):
                dve.wait_ge(lat_hi_ready, j + 1)
                V.tensor_tensor(lat_lo[:, j, :], lat_f[:, j, :], lat_hi[:, j, :].bitcast(fp32),
                                ALU.subtract).then_inc(lat_ready, 1)
            lo(CH["bgate"], 0)
            for j in range(4):
                weighted_ready(dve, "hconv", j, 0, CH["hconv"] + 1)
                V.tensor_tensor(u_conv[:, j, :], c_conv[:, j, :], bank[j][:, :], ALU.mult).then_inc(drained[j], 1)
            lo(CH["bgate"] + 1, 1)
            dve.wait_ge(drained[3], DR["hconv"][3] + 1)
            for j in range(4):
                def tap(w):
                    return col(C_CONV + 4 * w + j)
                then(V.tensor_scalar(c_conv[:, j, :], u_conv[:, j, :], tap(2), None, ALU.mult))
                then(V.scalar_tensor_tensor(c_conv[:, j, 1:S], u_conv[:, j, 0:S - 1], tap(1), c_conv[:, j, 1:S],
                                            ALU.mult, ALU.add))
                then(V.scalar_tensor_tensor(c_conv[:, j, 2:S], u_conv[:, j, 0:S - 2], tap(0), c_conv[:, j, 2:S],
                                            ALU.mult, ALU.add))
            laid_out(CH["uq"], 0, uq_parts)
            for j in range(4):
                weighted_ready(dve, "bgate", j, 0, CH["bgate"] + 1)
                V.tensor_tensor(b_conv[:, j, :], c_conv[:, j, :], bank[j][:, :], ALU.mult).then_inc(drained[j], 1)
            laid_out(CH["ukv"], 1, ukv_parts)
            dve.wait_ge(k_rope_ready, HEADS)
            for n in range(2):
                dve.wait_ge(tile_ready[n], RD["uq"][n] + 2)
                V.scalar_tensor_tensor(rot_a[:, :], bank[n][:, :], ATT_SCALE, cos_t[:, :], ALU.mult,
                                       ALU.mult).then_inc(drained[n], 1)
                if n == 0:
                    dve.wait_ge(tile_ready[2], RD["uq"][2] + 2)
                else:
                    dve.wait_ge(chunk_done, CH["uq"] + 1)
                V.scalar_tensor_tensor(rot_b[:, :], bank[2 + n][:, :], ATT_SCALE, sin_t[:, :], ALU.mult,
                                       ALU.mult).then_inc(drained[2 + n], 1)
                dve.wait_ge(drained[n], DR["uq"][n] + 2)
                dve.wait_ge(drained[2 + n], DR["uq"][2 + n] + 2)
                for r in range(4):
                    ins = V.tensor_tensor(q_mla[NOPE:QK, 4 * n + r, :], rot_a[32 * r:32 * r + 32, :],
                                          rot_b[32 * r:32 * r + 32, :], ALU.add)
                ins.then_inc(q_rope_ready, 1)
                dve.wait_ge(q_rope_ready, n + 1)
            lo(CH["out0"], 0)

            def att_max(u):
                qt, h = u // HEADS, u % HEADS
                kv = (qt + 1) * P
                dve.wait_ge(tile_ready[u % 2], RD["att"][u % 2] + u // 2 + 1)
                then(V.memset(bank[u % 2][0:CHUNK, kv - CHUNK:kv], NEG))
                V.tensor_reduce(col(C_NMAX + u), bank[u % 2][:, 0:kv], AX.X, ALU.max, negate=True).then_inc(
                    nmax_ready, 1)

            def att_norm(qt):
                u0 = qt * HEADS
                dve.wait_ge(pv_done, u0 + HEADS)
                then(V.reciprocal(col(C_RINV + u0, HEADS), col(C_RSUM + u0, HEADS)))
                V.tensor_tensor(y_acc[:, qt, 0:512].rearrange("p (h d) -> p h d", h=HEADS),
                                bank[4 + qt][:, :].rearrange("p (h d) -> p h d", h=HEADS),
                                col(C_RINV + u0, HEADS).unsqueeze(2).to_broadcast([P, HEADS, VD]),
                                ALU.mult).then_inc(drained[4 + qt], 1)

            def yb_lo(qt):
                dve.wait_ge(ya_hi_ready, 4 + qt + 1)
                V.tensor_tensor(aT_lo[:, 4:8, qt * P:(qt + 1) * P],
                                bank[4 + qt][:, :].rearrange("p (k t) -> p k t", k=4),
                                aT_hi[:, 4:8, qt * P:(qt + 1) * P].bitcast(fp32),
                                ALU.subtract).then_inc(drained[4 + qt], 1)

            for u in range(NT * HEADS):
                att_max(u)
                if u == 4:
                    lo(CH["out0"] + 1, 1)
                    for j in range(4):
                        dve.wait_ge(ya_hi_ready, j + 1)
                        V.tensor_tensor(aT_lo[:, j, :], b_conv[:, j, :], aT_hi[:, j, :].bitcast(fp32),
                                        ALU.subtract).then_inc(ya_ready, 1)
                if u % HEADS == 2 and u > HEADS:
                    att_norm(u // HEADS - 1)
                if u % HEADS == 5 and u > HEADS:
                    yb_lo(u // HEADS - 1)
            att_norm(NT - 1)
            yb_lo(NT - 1)

            def y0_gain(i, last=False):
                dve.wait_ge(final_gain_in if last else gain_in[i], 16 if last else 32)
                for t in range(NT):
                    dve.wait_ge(y0_sq, NT * (i - 1) + t + 1)
                    V.tensor_tensor(y_acc[:, t, 0:CW], y_acc[:, t, 0:CW], g_post[:, 0:CW], ALU.mult).then_inc(
                        y0_gained, 1)
                V.tensor_scalar(col(C_BIAS, NT), col(C_SS0, NT), EPS, None, ALU.add).then_inc(y_bias, 1)

            def norm_stage(i, phase, add, next_chunk, last=False):
                def y_last(t):
                    if add:
                        weighted_ready(dve, phase, 4 + t, 1, CH[phase] + 7)
                        V.tensor_tensor(y_acc[:, t, CW:D], y_acc[:, t, CW:D], bank[4 + t][:, :],
                                        ALU.add).then_inc(drained[4 + t], 1)
                    else:
                        dve.wait_ge(y1_sq, NT * (i - 1) + t + 1)
                        V.tensor_tensor(y_gain[:, t % 2, :], bank[4 + t][:, :], g_post[:, CW:D],
                                        ALU.mult).then_inc(drained[4 + t], 1)

                def x_add(t):
                    n = NT * (i - 1) + t
                    if add:
                        dve.wait_ge(y1_gained, NT * (i // 2 - 1) + t + 1)
                    else:
                        dve.wait_ge(drained[4 + t], DR[phase][4 + t] + 2)
                    dve.wait_ge(y_sq, n + 1)
                    then(V.reciprocal(col(C_RY + t), col(C_SSY + t)))
                    V.scalar_tensor_tensor(x[:, t, 0:CW], y_acc[:, t, 0:CW], col(C_RY + t), x[:, t, 0:CW], ALU.mult,
                                           ALU.add)
                    V.scalar_tensor_tensor(x[:, t, CW:D], y_gain[:, t % 2, :], col(C_RY + t), x[:, t, CW:D], ALU.mult,
                                           ALU.add).then_inc(x_new, 1)

                dve.wait_ge(y0_gained, NT * i)
                y_last(0)
                if last:
                    for t in range(NT):
                        x_add(t)
                        if t < NT - 1:
                            y_last(t + 1)
                    return
                x_add(0)
                y_last(1)
                pre_norm(i, 0)
                x_add(1)
                norm_lo(i, 0)
                pre_norm(i, 1)
                if add:
                    y_last(2)
                lo(next_chunk, 0)
                norm_lo(i, 1)
                if not add:
                    y_last(2)
                x_add(2)
                y_last(3)
                pre_norm(i, 2)
                lo(next_chunk + 1, 1)
                x_add(3)
                norm_lo(i, 2)
                pre_norm(i, 3)
                norm_lo(i, 3)

            def out_proj(i, phase):
                c = CH[phase]
                lo(c + 2, 0)
                lo(c + 3, 1)
                y0_gain(i)
                norm_stage(i, phase, False, c + 4)

            def mlp(l, i, next_chunk):
                for h in range(FH):
                    p1, p2 = f"w1{'ab'[h]}{l}", f"w2{'ab'[h]}{l}"
                    c1, c2 = CH[p1], CH[p2]
                    u0 = (l * FH + h) * 4 * FG

                    def group(g):
                        lo(g * 2 + (c1 + 2), 0)
                        for j in range(4):
                            dve.wait_ge(drained[j], g + (DR[p1][j] + 1))
                            V.tensor_tensor(usq[:, j % 2, :], relu[:, j % 2, :], relu[:, j % 2, :],
                                            ALU.mult).then_inc(u_sq, 1)
                            dve.wait_ge(u_sq, g * 4 + (u0 + j + 1 + 2))
                            dve.wait_ge(u_hi_ready, g * 4 + (u0 + j + 1))
                            V.tensor_tensor(uT_lo[:, bass.ds(g * 4 + j, 1), :].rearrange("p a t -> p (a t)"),
                                            usq[:, j % 2, :],
                                            uT_hi[:, bass.ds(g * 4 + j, 1), :].rearrange("p a t -> p (a t)").bitcast(
                                                fp32), ALU.subtract).then_inc(u_ready, 1)

                    if h == 0:
                        group(0)
                    with dve.Fori(1 - h, FG) as g:
                        lo(g * 2 + (c1 + 1), 1)
                        group(g)
                    if h == 0:
                        with dve.Fori(0, 2) as n:
                            for k in range(4):
                                lo(n * 4 + (c2 + k + 1), (k + 1) % 2)
                    else:
                        for k in range(4):
                            lo(c2 + k + 1, (k + 1) % 2)
                        for t in range(NT):
                            weighted_ready(dve, p2, 4 + t, 0, c2 + 3)
                            V.tensor_tensor(y_acc[:, t, 0:CW], y_acc[:, t, 0:CW], bank[4 + t][:, :],
                                            ALU.add).then_inc(drained[4 + t], 1)
                        lo(c2 + 5, 1)
                        lo(c2 + 6, 0)
                        lo(c2 + 7, 1)
                        y0_gain(i, last=next_chunk is None)
                        norm_stage(i, p2, True, next_chunk, last=next_chunk is None)

            out_proj(1, "out0")
            V.memset(col(C_DEN), 0.0).then_inc(u_sq, 2)
            mlp(0, 2, CH["qk"])

            dve.wait_ge(small_in[1], 16)
            then(V.memset(small_f[:, :, :], 0.0))
            V.tensor_copy(small_f[:, :, 0:4], small_raw[:, :, 0:4])
            V.tensor_copy(small_f[:, :, 32:36], small_raw[:, :, 4:8]).then_inc(small_f_ready, 1)
            dve.wait_ge(small_hi_ready, 2)
            V.tensor_tensor(small_lo[:, :, :], small_f[:, :, :], small_hi[:, :, :].bitcast(fp32),
                            ALU.subtract).then_inc(small_ready, 1)
            dve.wait_ge(small_ready, 2)
            V.memset(zero_row[:, :], 0.0)
            lo(CH["qk"] + 2, 0)
            lo(CH["qk"] + 3, 1)
            dve.wait_ge(tile_ready[4], RD["gates"][4] + 1)
            V.tensor_scalar(row_i[:, :], bank[4][0:4, :], col(C_BI, 1, 4), None, ALU.add)
            V.tensor_scalar(row_f[:, :], bank[4][32:36, :], col(C_BF, 1, 4), None, ALU.add).then_inc(drained[4], 1)
            dve.wait_ge(drained[4], DR["gates"][4] + 1)
            V.scalar_tensor_tensor(abs_row[:, :], row_f[:, :], -1.0, row_f[:, :], ALU.mult, ALU.max).then_inc(gate_f, 1)
            dve.wait_ge(gate_ln, 1)
            then(V.scalar_tensor_tensor(row_f[:, :], row_f[:, :], 0.0, e_row[:, :], ALU.min, ALU.subtract))
            V.tensor_tensor_scan(row_m[:, :], row_f[:, :], row_i[:, :], 0.0, ALU.add, ALU.max)
            for t in range(NT):
                ins = V.tensor_tensor_scan(row_b[:, t * P:(t + 1) * P], row_f[:, t * P:(t + 1) * P],
                                           zero_row[:, t * P:(t + 1) * P], 0.0, ALU.add, ALU.add)
            then(ins)
            then(V.tensor_tensor(row_i[:, :], row_i[:, :], row_b[:, :], ALU.subtract))
            then(V.tensor_tensor(row_f[:, :], row_b[:, :], row_m[:, :], ALU.subtract))
            for t in range(1, NT):
                at_t = FAR.index((0, t)) * P
                total = row_b[:, t * P - 1:t * P]
                if t > 1:
                    before = FAR.index((0, t - 1)) * P
                    V.tensor_scalar(row_far[:, at_t:at_t + (t - 1) * P], row_far[:, before:before + (t - 1) * P], total,
                                    None, ALU.add)
                ins = V.tensor_scalar(row_far[:, at_t + (t - 1) * P:at_t + t * P], row_i[:, (t - 1) * P:t * P], total,
                                      None, ALU.add)
                if t < NT - 1:
                    then(ins)
            ins.then_inc(rows_ready, 1)
            V.memset(v_aug[:, :, :, DH:DH + 1], 1.0).then_inc(v_ones, 1)
            for k in range(3, 8):
                lo(CH["qk"] + k + 1, (k + 1) % 2)
            c = CH["ogate"]
            for k in range(4):
                lo(c + k + 1, (k + 1) % 2)
            c = CH["v"]
            for k in range(4):
                lo(c + k + 1, (k + 1) % 2)

            posts = [(h, t) for h in range(ML_HEADS) for t in range(NT)]

            def den(h, t):
                n = h * NT + t
                dve.wait_ge(tile_ready[4 + t], RD["core"][4 + t] + h + 1)
                k = 5 * (n % 4)
                floor = ucol[:, len(PAIRS) + t, h:h + 1]
                then(V.tensor_scalar(col(C_DEN + k), bank[4 + t][:, DH:DH + 1], floor, None, ALU.max))
                then(V.scalar_tensor_tensor(col(C_DEN + k), bank[4 + t][:, DH:DH + 1], -1.0, col(C_DEN + k), ALU.mult,
                                            ALU.max))
                V.reciprocal(col(C_RDEN + k), col(C_DEN + k)).then_inc(den_ready, 1)

            def divide(h, t):
                n = h * NT + t
                dve.wait_ge(ssh_ready, n + 1)
                V.tensor_scalar(cell[:, t, h * DH:(h + 1) * DH], bank[4 + t][:, 0:DH], col(C_RDEN + 5 * (n % 4)),
                                None, ALU.mult).then_inc(drained[4 + t], 1)

            for i in range(ML_HEADS * NT + 1):
                if i == 3:
                    lo(CH["out1"] + 1, 1)
                if i < ML_HEADS * NT:
                    h, s = posts[i]
                    bk = 1 + i % 2
                    dve.wait_ge(tile_ready[bk], RD["core"][bk] + i // 2 + 1)
                    dve.wait_ge(decay_ready, i + 1)
                    V.scalar_tensor_tensor(wgtT[:, i % 2, s * P:S], bank[bk][:, s * P:S], ML_SCALE,
                                           decay[:, i % 2, s * P:S], ALU.mult, ALU.mult).then_inc(wgt_ready, 1)
                if 1 <= i <= ML_HEADS * NT:
                    den(*posts[i - 1])
                if i >= 2 and i % NT != 1:
                    divide(*posts[i - 2])
                if i >= 2 and i % NT == 0:
                    divide(*posts[i - 1])
            dve.wait_ge(rms_h_ready, 1)
            then(V.reciprocal(col(C_RH, 16), col(C_RH, 16)))
            for h, t in posts:
                part = cell[:, t, h * DH:(h + 1) * DH]
                V.tensor_scalar(part, part, col(C_RH + h * NT + t), None, ALU.mult).then_inc(cell_ready, 1)

            for f in range(8):
                bk = f % 4
                dve.wait_ge(drained[bk], DR["ogate"][bk] + 2)
                dve.wait_ge(tile_ready[bk], RD["cellT"][bk] + f // 4 + 1)
                V.scalar_tensor_tensor(cell_f[:, f % 2, :], bank[bk][:, :], col(C_HEAD + f), o_ml[:, f, :], ALU.mult,
                                       ALU.mult).then_inc(drained[bk], 1)
                dve.wait_ge(cell_hi_ready, f + 1)
                V.tensor_tensor(aT_lo[:, f, :], cell_f[:, f % 2, :], aT_hi[:, f, :].bitcast(fp32),
                                ALU.subtract).then_inc(ya_ready, 1)
            out_proj(3, "out1")
            mlp(1, 4, None)

        @block.tensor
        def _(pe):
            def mm3(dst, st_hi, st_lo, mv_hi, mv_lo, start, stop):
                nc.tensor.matmul(dst, st_lo, mv_hi, start=start, stop=False)
                nc.tensor.matmul(dst, st_hi, mv_lo, start=False, stop=False)
                return nc.tensor.matmul(dst, st_hi, mv_hi, start=False, stop=stop)

            def w(half, kt, cols_):
                v = [z[half][:, :].rearrange("p (k f) -> p k f", k=CK)[:, kt, cols_] for z in (w_hi, w_lo)]
                return v

            def columns(phase, c0, rnd, loop_rnd=None):
                for kc in range(2):
                    pe.wait_ge(lo_split, c0 + (kc + 1))
                    for j in range(4):
                        if kc == 0:
                            pe.wait_ge(drained[j], rnd + DR[phase][j])
                        for kt in range(CK):
                            k = kc * CK + kt
                            wh, wl = w(kc, kt, slice(j * P, (j + 1) * P))
                            ins = mm3(bank[j][:, :], wh, wl, aT_hi[:, k, :], aT_lo[:, k, :], k == 0, k == KT - 1)
                        if j == 3:
                            ins.then_inc(chunk_done, 1)
                        elif kc == 1:
                            ins.then_inc(tile_ready[j], 1)

            def rows(phase, c0, rnd, nk, lhs_hi, lhs_lo, lhs_ready=None, norm=None, tail=False):
                def tile(kc, t):
                    if kc == 0 and t >= 0:
                        pe.wait_ge(drained[4 + t], rnd + DR[phase][4 + t])
                    for kt in range(CK):
                        k = kc * CK + kt
                        wh, wl = w(kc % 2, kt, slice(0, CW))
                        ts = slice(t * P, (t + 1) * P)
                        ins = mm3(bank[4 + t][:, :], lhs_hi[:, k, ts], lhs_lo[:, k, ts], wh, wl, k == 0,
                                  k == nk * CK - 1)
                    if t == 3:
                        ins.then_inc(chunk_done, 1)
                    elif kc == nk - 1:
                        ins.then_inc(tile_ready[4 + t], 1)

                for kc in range(nk - 2 if tail else nk):
                    pe.wait_ge(lo_split, c0 + (kc + 1))
                    if lhs_ready is not None:
                        lhs_ready(kc)
                    for t in range(NT):
                        tile(kc, t)
                if tail:
                    for t0 in (0, 2):
                        for kc in (nk - 2, nk - 1):
                            if t0 == 0:
                                pe.wait_ge(lo_split, c0 + (kc + 1))
                                if lhs_ready is not None:
                                    lhs_ready(kc)
                            for t in (t0, t0 + 1):
                                tile(kc, t)
                                if norm is not None and (kc, t) == (nk - 2, 3):
                                    norm_T(norm, 0)
                                if norm is not None and (kc, t) == (nk - 1, 2):
                                    norm_T(norm, 1)

            def norm_T(i, t):
                pe.wait_ge(h_ready, NT * i + t + 1)
                for q in range(2):
                    bk = 2 * t + q
                    n = DR[f"norm{i}"][bk]
                    if n:
                        pe.wait_ge(drained[bk], n)
                    for k in range(4):
                        f = (4 * q + k) * P
                        ins = nc.tensor.transpose(bank[bk][:, k * P:(k + 1) * P], h_tok[:, t % 2, f:f + P], ident[:, :])
                    ins.then_inc(tile_ready[bk], 1)

            def columns_halves(phase, i):
                c0 = CH[phase]
                for part in range(2):
                    for bk in range(4 * part, 4 * part + 4):
                        pe.wait_ge(drained[bk], DR[f"norm{i}"][bk] + 1)
                    ts = slice(part * S // 2, (part + 1) * S // 2)
                    for kc in range(2):
                        if part == 0:
                            pe.wait_ge(lo_split, c0 + kc + 1)
                        for j in range(4):
                            for kt in range(CK):
                                k = kc * CK + kt
                                wh, wl = w(kc, kt, slice(j * P, (j + 1) * P))
                                ins = mm3(bank[j][:, ts], wh, wl, aT_hi[:, k, ts], aT_lo[:, k, ts], k == 0,
                                          k == KT - 1)
                            if part == 1 and j == 3:
                                ins.then_inc(chunk_done, 1)
                            elif part == 1 and kc == 1:
                                ins.then_inc(tile_ready[j], 1)
                            if part == 0 and j == 2:
                                norm_T(i, 2 + kc)

            pe.wait_ge(pool_const, 1)
            norm_T(0, 0)
            norm_T(0, 1)
            columns_halves("latent", 0)
            pe.wait_ge(small_ready, 1)
            for k in range(KT):
                ins = mm3(bank[4][0:64, :], small_hi[:, k, :], small_lo[:, k, :], aT_hi[:, k, :], aT_lo[:, k, :],
                          k == 0, k == KT - 1)
            ins.then_inc(tile_ready[4], 1)
            columns("cgate", CH["cgate"], 0)
            for n in range(2):
                pe.wait_ge(lat_sq_ready, 2 * n + 2)
                nc.tensor.matmul(bank[5 + n][:, :], ones[:, :], lat_sq[:, 2 * n, :], start=True, stop=False)
                nc.tensor.matmul(bank[5 + n][:, :], ones[:, :], lat_sq[:, 2 * n + 1, :], start=False,
                                 stop=True).then_inc(tile_ready[5 + n], 1)
            columns("hconv", CH["hconv"], 0)
            columns("bgate", CH["bgate"], 0)

            def w2(half, k, c_):
                return [z[half][:, :].rearrange("p (k f) -> p k f", k=2)[:, k, c_] for z in (w_hi, w_lo)]

            pe.wait_ge(lo_split, CH["uq"] + 1)
            pe.wait_ge(lat_ready, 4)
            for rnd in range(2):
                for j in range(4):
                    pe.wait_ge(drained[j], DR["uq"][j] + rnd)
                    for k in range(2):
                        wh, wl = w2(0, k, slice((4 * rnd + j) * P, (4 * rnd + j + 1) * P))
                        ins = mm3(bank[j][:, :], wh, wl, lat_hi[:, k, :], lat_lo[:, k, :], k == 0, k == 1)
                    ins.then_inc(chunk_done if rnd == 1 and j == 3 else tile_ready[j], 1)
            pe.wait_ge(lo_split, CH["ukv"] + 1)
            for j in range(4):
                pe.wait_ge(drained[j], DR["ukv"][j])
                for k in range(2):
                    wh, wl = w2(1, k, slice(j * P, (j + 1) * P))
                    ins = mm3(bank[j][:, :], wh, wl, lat_hi[:, 2 + k, :], lat_lo[:, 2 + k, :], k == 0, k == 1)
                ins.then_inc(tile_ready[j], 1)
            for t in range(NT):
                for k in range(2):
                    wh, wl = w2(1, k, slice(512, 1024))
                    ts = slice(t * P, (t + 1) * P)
                    ins = mm3(bank[4 + t][:, :], lat_hi[:, 2 + k, ts], lat_lo[:, 2 + k, ts], wh, wl, k == 0, k == 1)
                ins.then_inc(chunk_done if t == 3 else tile_ready[4 + t], 1)

            def scores(u):
                qt, h = u // HEADS, u % HEADS
                pe.wait_ge(drained[u % 2], DR["att"][u % 2] + u // 2)
                nc.tensor.matmul(bank[u % 2][:, 0:(qt + 1) * P], q_mla[:, h, qt * P:(qt + 1) * P],
                                 k_mla[:, h, 0:(qt + 1) * P], start=True, stop=True).then_inc(tile_ready[u % 2], 1)

            def turn(u):
                qt, bk = u // HEADS, 2 + u % 2
                pe.wait_ge(drained[u % 2], DR["att"][u % 2] + u // 2 + 1)
                pe.wait_ge(drained[bk], DR["att"][bk] + u // 2)
                for s in range(qt + 1):
                    ins = nc.tensor.transpose(bank[bk][:, s * P:(s + 1) * P], probs[:, u % 2, s * P:(s + 1) * P],
                                              ident[:, :])
                ins.then_inc(tile_ready[bk], 1)

            def values(u):
                qt, h, bk = u // HEADS, u % HEADS, 2 + u % 2
                pe.wait_ge(drained[bk], DR["att"][bk] + u // 2 + 1)
                if h == 0:
                    pe.wait_ge(drained[4 + qt], DR["att"][4 + qt])
                for s in range(qt + 1):
                    ins = nc.tensor.matmul(bank[4 + qt][:, h * VD:(h + 1) * VD], probsT[:, u % 2, s, :],
                                           v_mla[:, s, h * VD:(h + 1) * VD], start=(s == 0), stop=(s == qt))
                ins.then_inc(pv_done, 1)

            def yb_T(qt):
                pe.wait_ge(drained[4 + qt], DR["att"][4 + qt] + 1)
                for k in range(4):
                    ins = nc.tensor.transpose(bank[4 + qt][:, k * P:(k + 1) * P], y_acc[:, qt, k * P:(k + 1) * P],
                                              ident[:, :])
                ins.then_inc(tile_ready[4 + qt], 1)

            pe.wait_ge(q_rope_ready, 2)
            pe.wait_ge(k_rope_ready, HEADS)
            for j in range(4):
                pe.wait_ge(drained[j], DR["ukv"][j] + 1)
                pe.wait_ge(drained[4 + j], DR["ukv"][4 + j] + 1)
            units = NT * HEADS
            scores(0)
            for u in range(units + 1):
                if u + 1 < units:
                    scores(u + 1)
                if u < units:
                    turn(u)
                if u >= 1:
                    values(u - 1)
                if u % HEADS == 3 and u > HEADS:
                    yb_T(u // HEADS - 1)
            yb_T(NT - 1)

            def out_proj(i, phase, ready):
                c = CH[phase]
                rows(phase, c, 0, 2, aT_hi, aT_lo, lhs_ready=ready)
                rows(phase, c + 2, 1, 2, aT_hi, aT_lo, norm=i, tail=True)

            def out0_ready(kc):
                if kc == 0:
                    pe.wait_ge(ya_ready, 4)
                else:
                    for qt in range(NT):
                        pe.wait_ge(drained[4 + qt], DR["att"][4 + qt] + 2)

            def mlp(l, i):
                for h in range(FH):
                    p1, p2 = f"w1{'ab'[h]}{l}", f"w2{'ab'[h]}{l}"
                    c1, c2 = CH[p1], CH[p2]
                    u0 = (l * FH + h) * 4 * FG
                    if h == 0:
                        columns_halves(p1, i - 1)
                    with pe.Fori(1 - h, FG) as g:
                        columns(p1, g * 2 + c1, g)

                    def u_tiles(kc):
                        pe.wait_ge(u_ready, u0 + 4 * kc + 4)

                    if h == 0:
                        with pe.Fori(0, 2) as n:
                            rows(p2, n * 4 + c2, n, 4, uT_hi, uT_lo, lhs_ready=u_tiles)
                    else:
                        rows(p2, c2, 0, 4, uT_hi, uT_lo, lhs_ready=u_tiles)
                        rows(p2, c2 + 4, 1, 4, uT_hi, uT_lo, norm=i if i < 4 else None, tail=True)

            out_proj(1, "out0", out0_ready)
            mlp(0, 2)
            columns_halves("qk", 2)

            pe.wait_ge(small_ready, 2)
            pe.wait_ge(drained[4], DR["gates"][4])
            for k in range(KT):
                ins = mm3(bank[4][0:64, :], small_hi[:, k, :], small_lo[:, k, :], aT_hi[:, k, :], aT_lo[:, k, :],
                          k == 0, k == KT - 1)
            ins.then_inc(tile_ready[4], 1)
            columns("qk", CH["qk"] + 2, 1)
            pe.wait_ge(rows_ready, 1)
            pe.wait_ge(drained[4], DR["gates"][4] + 1)
            for n, (s, t) in enumerate(PAIRS):
                row, r = (row_i, s) if s == t else (row_far, FAR.index((s, t)))
                nc.tensor.transpose(bank[4][:, 4 * n:4 * n + 4], row[:, r * P:(r + 1) * P], ident[0:4, 0:4])
            for t in range(NT):
                n = len(PAIRS) + t
                ins = nc.tensor.transpose(bank[4][:, 4 * n:4 * n + 4], row_m[:, t * P:(t + 1) * P], ident[0:4, 0:4])
            ins.then_inc(tile_ready[4], 1)
            with pe.Fori(2, 4) as g:
                columns("qk", g * 2 + CH["qk"], g)
            for g in range(2):
                columns("ogate", CH["ogate"] + 2 * g, g)
            rows("v", CH["v"], 0, 2, aT_hi, aT_lo)
            pe.wait_ge(sel_ready, 1)
            for bk in range(4):
                pe.wait_ge(drained[bk], DR["qk"][bk] + 4)

            def ml_row(h):
                if h == 0:
                    pe.wait_ge(drained[0], DR["core"][0])
                else:
                    pe.wait_ge(decay_raw, h * NT)
                nc.tensor.matmul(bank[0][:, :], head_sel[:, h * P:(h + 1) * P], row_f[:, :], start=True,
                                 stop=True).then_inc(tile_ready[0], 1)

            def ml_scores(i):
                h, s = i // NT, i % NT
                bk = 1 + i % 2
                if i >= 2:
                    pe.wait_ge(wgt_ready, i - 1)
                else:
                    pe.wait_ge(drained[bk], DR["core"][bk])
                for k in range(2):
                    ins = nc.tensor.matmul(bank[bk][:, s * P:S], qk_ml[:, 8 + 2 * h + k, s * P:(s + 1) * P],
                                           qk_ml[:, 2 * h + k, s * P:S], start=(k == 0), stop=(k == 1))
                ins.then_inc(tile_ready[bk], 1)

            def ml_values(i):
                h, s = i // NT, i % NT
                pe.wait_ge(wgt_ready, i + 1)
                for t in range(s, NT):
                    if s == 0:
                        pe.wait_ge(drained[4 + t], DR["core"][4 + t] + h)
                    ins = nc.tensor.matmul(bank[4 + t][:, 0:DH + 1], wgtT[:, i % 2, t * P:(t + 1) * P],
                                           v_aug[:, s, h, :], start=(s == 0), stop=(s == t))
                    if t == s:
                        ins.then_inc(tile_ready[4 + t], 1)

            n_ml = ML_HEADS * NT
            ml_row(0)
            ml_scores(0)
            rows("v", CH["v"] + 2, 1, 2, aT_hi, aT_lo)
            for t in range(NT):
                pe.wait_ge(drained[4 + t], DR["v"][4 + t] + 2)
            pe.wait_ge(v_ones, 1)
            for i in range(n_ml):
                if i + 1 < n_ml:
                    if (i + 1) % NT == 0:
                        ml_row((i + 1) // NT)
                    ml_scores(i + 1)
                ml_values(i)
            for f in range(8):
                bk = f % 4
                pe.wait_ge(cell_ready, NT * (f // 2) + NT)
                if f >= 4:
                    pe.wait_ge(drained[bk], DR["cellT"][bk] + f // 4)
                for t in range(NT):
                    ins = nc.tensor.transpose(bank[bk][:, t * P:(t + 1) * P], cell[:, t, f * P:(f + 1) * P], ident[:, :])
                ins.then_inc(tile_ready[bk], 1)

            def out1_ready(kc):
                pe.wait_ge(ya_ready, 4 + 4 * kc + 4)

            out_proj(3, "out1", out1_ready)
            mlp(1, 4)


_INS = ["x", "positions", "norm_mix_pre", "norm_mix_post", "norm_mlp_pre", "norm_mlp_post", "hyb_w_in", "conv_w",
        "mla_q_norm", "mla_kv_norm", "mla_w_uq", "mla_w_ukv", "hyb_w_out", "ml_w_in", "ml_b_i", "ml_b_f",
        "ml_head_norm", "ml_w_out", "mlp_w1", "mlp_w2"]
_FLAT = {"x", "hyb_w_in", "conv_w", "mla_w_uq", "mla_w_ukv", "hyb_w_out", "ml_w_in", "ml_w_out"}


def kernel(**inputs):
    import numpy as _np
    import concourse.bacc as _bacc
    from concourse import mybir as _mybir
    from concourse.bass_utils import run_bass_kernel_spmd as _run

    nc = _bacc.Bacc("TRN2", target_bir_lowering=False, num_devices=1)
    arrays, args = {}, []

    def give(name, a):
        arrays[f"in_{name}_dram"] = a
        args.append(nc.dram_tensor(f"in_{name}_dram", a.shape, _mybir.dt.from_np(a.dtype), kind="ExternalInput").ap())

    for name in _INS:
        a = _np.ascontiguousarray(inputs[name])
        if name in _FLAT:
            a = a[0]
        give(name, a)
    half = ROPE // 2
    inv = _np.float32(10000.0) ** (-_np.arange(half, dtype=_np.float32) / _np.float32(half))
    sign = _np.where(_np.arange(P) % ROPE < half, -1.0, 1.0).astype(_np.float32)
    give("rope_const", _np.stack([_np.tile(inv, P // half), sign], axis=1))
    args.append(nc.dram_tensor("out_dram", (S, D), _mybir.dt.float32, kind="ExternalOutput").ap())
    trunk(nc, *args)
    r = _run(nc, [arrays], core_ids=[0])
    return r.results[0]["out_dram"].reshape(1, S, D)
```

```python
import concourse.bass as bass
from concourse import mybir
from contextlib import ExitStack

P = 128
D, S, DFF = 1024, 512, 4096
EPS = 1e-6
NT = S // P
KT = D // P
CW = 512
CK = 4
HEADS, NOPE, ROPE, VD = 8, 64, 32, 64
QK = NOPE + ROPE
RANK = 256
ML_HEADS, DH = 4, 256
CHUNK = 64
ATT_SCALE = float(QK) ** -0.5
ML_SCALE = float(DH) ** -0.5
NEG = -3.0e38
FH = 2
FG = DFF // FH // CW
PAIRS = [(s, t) for t in range(NT) for s in range(t + 1)]
FAR = [(s, t) for s, t in PAIRS if s < t]

MAGIC = 12582912.0
BIG = 25735.927018207585
BIG_PARTS = (25600.0, 136.0, BIG - 25736.0)
TWO_PI = 6.283185307179586
C2 = 0.0019350051879882812
PI_PARTS = (6.28125, C2, TWO_PI - 6.28125 - C2)
PI_MAX = 3.1415925


def build_schedule():
    a, b, none, every = (1, 1, 1, 1, 0, 0, 0, 0), (0, 0, 0, 0, 1, 1, 1, 1), (0,) * 8, (1,) * 8
    aw, bw = (1, 1, 1, 0, 0, 0, 0, 0), (0, 0, 0, 0, 1, 1, 1, 0)

    def times(u, n):
        return tuple(n * x for x in u)

    def plus(u, v):
        return tuple(x + y for x, y in zip(u, v))

    mlp = [("w1a", times(a, FG), times(aw, FG), 2 * FG), ("w2a", times(b, 2), times(bw, 2), 8),
           ("w1b", times(a, FG), times(aw, FG), 2 * FG), ("w2b", times(b, 2), times(bw, 2), 8)]
    phases = [
        ("norm0", every, every, 0),
        ("latent", a, aw, 2),
        ("krope", (0, 0, 0, 0, 1, 0, 0, 0), (0, 0, 0, 0, 1, 0, 0, 0), 0),
        ("cgate", a, aw, 2),
        ("sumsq", (0, 0, 0, 0, 0, 1, 1, 0), (0, 0, 0, 0, 0, 1, 1, 0), 0),
        ("hconv", a, aw, 2),
        ("bgate", a, aw, 2),
        ("uq", times(a, 2), plus(a, aw), 1),
        ("ukv", plus(a, b), plus(aw, b), 1),
        ("att", (16, 16, 16, 16, 2, 2, 2, 2), (16, 16, 16, 16, 1, 1, 1, 1), 0),
        ("out0", times(b, 2), times(bw, 2), 4),
        ("norm1", every, every, 0),
        *[(n + "0", u, v, c) for n, u, v, c in mlp],
        ("norm2", every, every, 0),
        ("gates", (0, 0, 0, 0, 2, 0, 0, 0), (0, 0, 0, 0, 2, 0, 0, 0), 0),
        ("qk", times(a, 4), times(aw, 4), 8),
        ("ogate", times(a, 2), times(aw, 2), 4),
        ("v", times(b, 2), times(bw, 2), 4),
        ("core", (0, 0, 0, 0, 4, 4, 4, 4), (4, 8, 8, 0, 4, 4, 4, 4), 0),
        ("cellT", times(a, 2), times(a, 2), 0),
        ("out1", times(b, 2), times(bw, 2), 4),
        ("norm3", every, every, 0),
        *[(n + "1", u, v, c) for n, u, v, c in mlp],
    ]
    drains, readies, chunks = {}, {}, {}
    d, r, c = none, none, 0
    for name, uses, ready, n in phases:
        drains[name], readies[name], chunks[name] = d, r, c
        d, r, c = plus(d, uses), plus(r, ready), c + n
    return drains, readies, chunks


def trunk(nc, x_in, pos_in, g_mix_pre, g_mix_post, g_mlp_pre, g_mlp_post, w_hyb, conv_w, q_gain, kv_gain,
          w_uq, w_ukv, w_hyb_out, w_ml, ml_bi, ml_bf, head_gain, w_ml_out, w_mlp1, w_mlp2, rope_const, out):
    fp32, f32r, i32 = mybir.dt.float32, mybir.dt.float32r, mybir.dt.int32
    ACT, ALU, AX = mybir.ActivationFunctionType, mybir.AluOpType, mybir.AxisListType
    DR, RD, CH = build_schedule()

    with ExitStack() as ctx:
        base = 16512
        assert nc.sbuf_base <= base

        def at(name, offset, shape, dt=fp32):
            return nc.alloc_sbuf_tensor_at(name, shape, dt, offset=base + offset)

        def sem(name):
            return ctx.enter_context(nc.semaphore(name))

        o = 0
        x = at("x", o, [P, NT, D]); o += 16384
        Y = o; o += 16512
        y_acc = at("y_acc", Y, [P, NT, D])
        lat_hi = at("lat_hi", Y, [P, 4, S], f32r)
        lat_lo = at("lat_lo", Y + 8192, [P, 4, S], f32r)
        v_aug = at("v_aug", Y, [P, NT, ML_HEADS, DH + 1])
        aT_hi = at("aT_hi", o, [P, KT, S], f32r); o += 16384
        aT_lo = at("aT_lo", o, [P, KT, S], f32r); o += 16384
        raw = [at(f"raw{i}", o + 8192 * i, [P, CK * CW]) for i in range(2)]; o += 16384
        w_hi = [at(f"w_hi{i}", o + 16384 * i, [P, CK * CW], f32r) for i in range(2)]
        w_lo = [at(f"w_lo{i}", o + 16384 * i + 8192, [P, CK * CW], f32r) for i in range(2)]; o += 32768
        A = o; o += 65536
        uT_hi = at("uT_hi", A, [P, DFF // FH // P, S], f32r)
        uT_lo = at("uT_lo", A + 32768, [P, DFF // FH // P, S], f32r)
        q_mla = at("q_mla", A, [QK, HEADS, S])
        k_mla = at("k_mla", A + 16384, [QK, HEADS, S])
        v_mla = at("v_mla", A + 32768, [P, NT, HEADS * VD])
        probs = at("probs", A + 40960, [P, 2, S])
        probsT = at("probsT", A + 45056, [P, 2, NT, P])
        b_conv = at("b_conv", A + 49152, [P, 4, S])
        c_conv = at("c_conv", A + 57344, [P, 4, S])
        lat_raw = at("lat_raw", A, [P, 4, S])
        lat_sq = at("lat_sq", A + 8192, [P, 4, S])
        lat_rstd = at("lat_rstd", A + 40960, [P, 2, S])
        lat_f = at("lat_f", A + 32768, [P, 4, S])
        u_conv = at("u_conv", A + 40960, [P, 4, S])
        qk_ml = at("qk_ml", A, [P, 16, S])
        o_ml = at("o_ml", A + 32768, [P, 8, S])
        cell = at("cell", A + 49152, [P, NT, D])
        g_post = at("g_post", o, [P, D]); o += 4096
        g_pre = at("g_pre", o, [P, D]); o += 4096
        head_sel = at("head_sel", o - 4096, [ML_HEADS, ML_HEADS * P])
        head_sel_r = at("head_sel_r", o - 2048, [ML_HEADS, ML_HEADS * P], f32r)
        H = o; o += 8192
        h_tok = at("h_tok", H, [P, 2, D])
        cos_t = at("cos_t", H, [P, S])
        sin_t = at("sin_t", H + 2048, [P, S])
        rot_a = at("rot_a", H + 4096, [P, S])
        rot_b = at("rot_b", H + 6144, [P, S])
        row_i = at("row_i", H, [ML_HEADS, S])
        row_f = at("row_f", H + 2048, [ML_HEADS, S])
        row_b = at("row_b", H + 4096, [ML_HEADS, S])
        row_m = at("row_m", H + 6144, [ML_HEADS, S])
        R = o; o += 8192
        relu = at("relu", R, [P, 2, S])
        usq = at("usq", R + 4096, [P, 2, S])
        junk = at("junk", R, [P, D])
        y_gain = at("y_gain", R + 4096, [P, 2, CW])
        pos_i = at("pos_i", R, [P, S], i32)
        ang = at("ang", R + 2048, [P, S])
        turns = at("turns", R + 4096, [P, S])
        half_sin = at("half_sin", R + 6144, [P, S])
        e_row = at("e_row", R, [ML_HEADS, S])
        zero_row = at("zero_row", R + 2048, [ML_HEADS, S])
        abs_row = at("abs_row", R + 4096, [ML_HEADS, S])
        row_far = at("row_far", R + 4096, [ML_HEADS, len(FAR) * P])
        decay = at("decay", R, [P, 2, S])
        wgtT = at("wgtT", R + 4096, [P, 2, S])
        cell_f = at("cell_f", R, [P, 2, S])
        small_hi = at("small_hi", o, [P, KT, 64], f32r); o += 2048
        small_lo = at("small_lo", o, [P, KT, 64], f32r); o += 2048
        row_f_hi = at("row_f_hi", o - 4096, [ML_HEADS, S], f32r)
        row_f_lo = at("row_f_lo", o - 2048, [ML_HEADS, S], f32r)
        small_f = at("small_f", R + 6144, [P, KT, 64])
        small_raw = at("small_raw", o, [P, KT, 32]); o += 1024
        ident = at("ident", o, [P, P]); o += 512
        ones = at("ones", o, [P, P]); o += 512
        ucol = at("ucol", o, [P, len(PAIRS) + NT, ML_HEADS]); o += 256
        cols = at("cols", o, [P, 192]); o += 768
        assert base + o <= nc.sbuf_usable_end

        def col(i, n=1, p=P):
            return cols[0:p, i:i + n]

        C_QG, C_KVG, C_CONV, C_HEAD, C_INV, C_SIGN, C_BI, C_BF = 0, 2, 4, 16, 24, 25, 26, 27
        C_SSY, C_RY, C_SSX, C_RX = 28, 32, 36, 40
        C_EPS, C_SS0 = 44, 180
        C_BIAS = 184
        C_NMAX, C_RSUM, C_RINV = 48, 80, 112
        C_DEN, C_RDEN, C_RH = 144, 145, 164

        bank = [ctx.enter_context(nc.psum_tensor(f"bank{i}", [P, S], fp32)) for i in range(8)]

        raw_in = [sem(f"raw_in{i}") for i in range(2)]
        hi_split = sem("hi_split")
        lo_split = sem("lo_split")
        lo_first_done = sem("lo_first_done")
        chunk_done = sem("chunk_done")
        tile_ready = [sem(f"tile_ready{i}") for i in range(8)]
        drained = [sem(f"drained{i}") for i in range(8)]
        x_in_sem = [sem(f"x_in{i}") for i in range(NT)]
        const_in = sem("const_in")
        small_in = [sem(f"small_in{i}") for i in range(2)]
        pos_in_sem = sem("pos_in")
        gain_in = [sem(f"gain_in{i}") for i in range(4)]
        final_gain_in = sem("final_gain_in")
        pool_const = sem("pool_const")
        pool_step = sem("pool_step")
        dve_done = sem("dve_done")
        act_done = sem("act_done")
        y0_sq = sem("y0_sq")
        y1_sq = sem("y1_sq")
        y0_gained = sem("y0_gained")
        y1_gained = sem("y1_gained")
        y_bias = sem("y_bias")
        y_sq = sem("y_sq")
        x_sq = sem("x_sq")
        x_first = sem("x_first")
        x_new = sem("x_new")
        h_ready = sem("h_ready")
        aT_hi_ready = sem("aT_hi_ready")
        small_f_ready = sem("small_f_ready")
        small_hi_ready = sem("small_hi_ready")
        small_ready = sem("small_ready")
        lat_sq_ready = sem("lat_sq_ready")
        lat_sq_added = sem("lat_sq_added")
        lat_f_ready = sem("lat_f_ready")
        lat_hi_ready = sem("lat_hi_ready")
        lat_ready = sem("lat_ready")
        angle_ready = sem("angle_ready")
        half_sin_ready = sem("half_sin_ready")
        sin_raw_ready = sem("sin_raw_ready")
        k_rope_ready = sem("k_rope_ready")
        ya_hi_ready = sem("ya_hi_ready")
        ya_ready = sem("ya_ready")
        q_rope_ready = sem("q_rope_ready")
        nmax_ready = sem("nmax_ready")
        u_sq = sem("u_sq")
        u_hi_ready = sem("u_hi_ready")
        u_ready = sem("u_ready")
        gate_f = sem("gate_f")
        gate_ln = sem("gate_ln")
        rows_ready = sem("rows_ready")
        sel_r_ready = sem("sel_r_ready")
        row_hi_ready = sem("row_hi_ready")
        row_lo_ready = sem("row_lo_ready")
        v_ones = sem("v_ones")
        decay_raw = sem("decay_raw")
        decay_ready = sem("decay_ready")
        wgt_ready = sem("wgt_ready")
        den_ready = sem("den_ready")
        rms_h_ready = sem("rms_h_ready")
        cell_ready = sem("cell_ready")
        ssh_ready = sem("ssh_ready")
        cell_hi_ready = sem("cell_hi_ready")
        sel_ready = sem("sel_ready")
        pv_done = sem("pv_done")
        out_sem = sem("out_stored")

        block = ctx.enter_context(nc.Block())

        def uq_parts(dst, src):
            d = dst[:, :].rearrange("p (k f) -> p k f", k=2)
            s = src[:, 0:2 * HEADS * QK].rearrange("p (k h f) -> p k h f", k=2, h=HEADS)
            half = ROPE // 2
            for k in range(2):
                yield d[:, k, 0:512].rearrange("p (h f) -> p h f", h=HEADS), s[:, k, :, 0:NOPE]
                yield d[:, k, 512:768].rearrange("p (h f) -> p h f", h=HEADS), s[:, k, :, NOPE:QK]
                swap = d[:, k, 768:1024].rearrange("p (h f) -> p h f", h=HEADS)
                yield swap[:, :, 0:half], s[:, k, :, NOPE + half:QK]
                yield swap[:, :, half:ROPE], s[:, k, :, NOPE:NOPE + half]

        def ukv_parts(dst, src):
            d = dst[:, :].rearrange("p (k f) -> p k f", k=2)
            s = src[:, :].rearrange("p (k h f) -> p k h f", k=2, h=HEADS)
            for k in range(2):
                for n in range(2):
                    yield (d[:, k, n * 512:(n + 1) * 512].rearrange("p (h f) -> p h f", h=HEADS),
                           s[:, k, :, n * 64:(n + 1) * 64])

        def weighted_ready(eng, phase, b, rnd, chunk):
            if b in (3, 7):
                eng.wait_ge(chunk_done, chunk + 1)
            else:
                eng.wait_ge(tile_ready[b], RD[phase][b] + rnd + 1)

        @block.sync
        def _(sp):
            def load(c, half, src, k=CK, first=False):
                if not first:
                    sp.wait_ge(lo_split, c - 1)
                sp.dma_start(raw[half][:, 0:k * src.shape[-1]].rearrange("p (k f) -> p k f", k=k),
                             src.rearrange("(k p) f -> p k f", p=P)).then_inc(raw_in[half], 16)

            def gains(i, post, pre):
                sp.wait_ge(h_ready, NT * i)
                sp.dma_start(g_post[:, :], post.to_broadcast([P, D])).then_inc(gain_in[i], 16)
                sp.dma_start(g_pre[:, :], pre.to_broadcast([P, D])).then_inc(gain_in[i], 16)

            c = CH["latent"]
            for t in range(NT):
                sp.dma_start(x[:, t, :], x_in[t * P:(t + 1) * P, :]).then_inc(x_in_sem[t], 16)
                if t == 0:
                    sp.dma_start(g_pre[:, :], g_mix_pre[0:1, :].to_broadcast([P, D])).then_inc(gain_in[0], 16)
                if t == 1:
                    load(c, 0, w_hyb[0:CW, 1536:2048], first=True)
            load(c + 1, 1, w_hyb[CW:2 * CW, 1536:2048], first=True)
            sp.dma_start(small_raw[:, :, :], w_hyb[:, 2048:2080].rearrange("(k p) f -> p k f", p=P)).then_inc(
                small_in[0], 16)
            with nc.allow_non_contiguous_dma(reason="a few KiB of per-feature constants"):
                for dst, src in ((col(C_QG, 2), q_gain.rearrange("a (j p) -> p (a j)", p=P)),
                                 (col(C_KVG, 2), kv_gain.rearrange("a (j p) -> p (a j)", p=P)),
                                 (col(C_HEAD, 8), head_gain.rearrange("a (j p) -> p (a j)", p=P)),
                                 (col(C_INV, 2), rope_const[:, :]),
                                 (col(C_BI, 1, ML_HEADS), ml_bi.rearrange("a h -> h a")),
                                 (col(C_BF, 1, ML_HEADS), ml_bf.rearrange("a h -> h a"))):
                    sp.dma_start(dst, src).then_inc(const_in, 16)
                sp.dma_start(col(C_CONV, 12).rearrange("p (w j) -> p w j", w=3),
                             conv_w.rearrange("w (j p) -> p w j", p=P)).then_inc(const_in, 16)
            sp.wait_ge(x_sq, NT)
            sp.dma_start(pos_i[:, :], pos_in[0:1, :].to_broadcast([P, S])).then_inc(pos_in_sem, 16)
            for phase, col0 in (("cgate", 512), ("hconv", 1024), ("bgate", 0)):
                for kc in range(2):
                    load(CH[phase] + kc, kc, w_hyb[kc * CW:(kc + 1) * CW, col0:col0 + CW])
            load(CH["uq"], 0, w_uq, k=2)
            load(CH["ukv"], 1, w_ukv, k=2)

            def load_out(phase, w):
                for n in range(2):
                    for kc in range(2):
                        load(CH[phase] + 2 * n + kc, kc, w[kc * CW:(kc + 1) * CW, n * CW:(n + 1) * CW])

            load_out("out0", w_hyb_out)

            def load_mlp(l, stage_gains):
                for h in range(FH):
                    c1, c2 = CH[f"w1{'ab'[h]}{l}"], CH[f"w2{'ab'[h]}{l}"]
                    with sp.Fori(0, FG) as g:
                        for kc in range(2):
                            load(g * 2 + (c1 + kc), kc, w_mlp1[l, kc * CW:(kc + 1) * CW,
                                                              bass.ds(g * CW + h * FG * CW, CW)])
                    if h == 0:
                        stage_gains()
                    with sp.Fori(0, 2) as n:
                        for kc in range(4):
                            row = h * (DFF // FH) + kc * CW
                            load(n * 4 + (c2 + kc), kc % 2, w_mlp2[l, row:row + CW, bass.ds(n * CW, CW)])

            def gains_1():
                gains(2, g_mlp_post[0:1, :], g_mix_pre[1:2, :])

            load_mlp(0, gains_1)
            sp.wait_ge(small_f_ready, 1)
            sp.dma_start(small_raw[:, :, 0:8], w_ml[:, 4096:4104].rearrange("(k p) f -> p k f", p=P)).then_inc(
                small_in[1], 16)
            with sp.Fori(0, 4) as g:
                for kc in range(2):
                    load(g * 2 + (CH["qk"] + kc), kc, w_ml[kc * CW:(kc + 1) * CW, bass.ds(g * CW, CW)])
            with sp.Fori(0, 2) as g:
                for kc in range(2):
                    load(g * 2 + (CH["ogate"] + kc), kc, w_ml[kc * CW:(kc + 1) * CW, bass.ds(g * CW + 3072, CW)])
            with sp.Fori(0, 2) as g:
                for kc in range(2):
                    load(g * 2 + (CH["v"] + kc), kc, w_ml[kc * CW:(kc + 1) * CW, bass.ds(g * CW + 2048, CW)])
            load_out("out1", w_ml_out)

            def gains_3():
                sp.wait_ge(h_ready, NT * 4)
                sp.dma_start(g_post[:, :], g_mlp_post[1:2, :].to_broadcast([P, D])).then_inc(final_gain_in, 16)

            load_mlp(1, gains_3)
            for t in range(NT):
                for n, ready in enumerate((x_first, x_new)):
                    sp.wait_ge(ready, (NT * 3 if n else 0) + t + 1)
                    sp.dma_start(out[t * P:(t + 1) * P, n * CW:(n + 1) * CW],
                                 x[:, t, n * CW:(n + 1) * CW]).then_inc(out_sem, 16)
            sp.wait_ge(out_sem, 16 * NT * 2)

        @block.gpsimd
        def _(pool):
            def gains(i, post, pre):
                pool.wait_ge(h_ready, NT * i)
                pool.dma_start(g_post[:, :], post.to_broadcast([P, D])).then_inc(gain_in[i], 16)
                pool.dma_start(g_pre[:, :], pre.to_broadcast([P, D])).then_inc(gain_in[i], 16)

            nc.gpsimd.memset(col(C_EPS), EPS)
            nc.gpsimd.memset(ones[:, :], 1.0).then_inc(pool_step, 1)
            pool.wait_ge(pool_step, 1)
            nc.gpsimd.affine_select(out=ident[:, :], in_=ones[:, :], compare_op=ALU.is_equal, fill=0.0, base=0,
                                    pattern=[[-1, P]], channel_multiplier=1).then_inc(pool_const, 1)
            gains(1, g_mix_post[0:1, :], g_mlp_pre[0:1, :])
            for n in range(2):
                pool.wait_ge(lat_sq_ready, 2 * n + 2)
                nc.gpsimd.tensor_tensor(lat_sq[:, 2 * n, :], lat_sq[:, 2 * n, :], lat_sq[:, 2 * n + 1, :],
                                        ALU.add).then_inc(lat_sq_added, 1)
            pool.wait_ge(lat_sq_added, 2)
            pool.wait_ge(drained[4], DR["krope"][4] + 1)
            for h in range(HEADS):
                nc.gpsimd.tensor_tensor(k_mla[NOPE:QK, h, :], rot_a[NOPE:QK, :], rot_b[NOPE:QK, :],
                                        ALU.add).then_inc(k_rope_ready, 1)

            def lo_second(c, half, n):
                pool.wait_ge(hi_split, c * 2 + 2)
                for q in range(2):
                    part = slice(1024 + q * 512, 1536 + q * 512)
                    if q == 1:
                        pool.wait_ge(lo_first_done, n)
                    ins = nc.gpsimd.tensor_tensor(w_lo[half][:, part], raw[half][:, part],
                                                  w_hi[half][:, part].bitcast(fp32), ALU.subtract)
                ins.then_inc(lo_split, 1)

            def y1_gain(i, phase, tiles):
                for t in tiles:
                    pool.wait_ge(drained[4 + t], DR[phase][4 + t] + 2)
                    if t >= 2:
                        pool.wait_ge(x_new, NT * (i - 1) + t - 1)
                    nc.gpsimd.tensor_tensor(y_gain[:, t % 2, :], y_acc[:, t, CW:D], g_post[:, CW:D],
                                            ALU.mult).then_inc(y1_gained, 1)

            for kc in range(2):
                lo_second(CH["w1a0"] + kc, kc, kc + 1)
            y1_gain(2, "w2b0", (0, 1))
            lo_second(CH["qk"], 0, 3)
            y1_gain(2, "w2b0", (2,))
            lo_second(CH["qk"] + 1, 1, 4)
            y1_gain(2, "w2b0", (3,))
            pool.wait_ge(h_ready, NT * 3)
            nc.gpsimd.memset(head_sel[:, :], 1.0).then_inc(pool_step, 1)
            pool.wait_ge(pool_step, 2)
            nc.gpsimd.affine_select(out=head_sel[:, :].rearrange("p (h j) -> p h j", h=ML_HEADS),
                                    in_=head_sel[:, :].rearrange("p (h j) -> p h j", h=ML_HEADS),
                                    compare_op=ALU.is_equal, fill=0.0, base=0,
                                    pattern=[[-1, ML_HEADS], [0, P]], channel_multiplier=1).then_inc(sel_ready, 1)
            for i in range(ML_HEADS * NT):
                s = i % NT
                pool.wait_ge(decay_raw, i + 1)
                nc.gpsimd.affine_select(out=decay[:, i % 2, s * P:(s + 1) * P], in_=decay[:, i % 2, s * P:(s + 1) * P],
                                        compare_op=ALU.is_ge, fill=0.0, base=0, pattern=[[1, P]],
                                        channel_multiplier=-1).then_inc(decay_ready, 1)
            pool.wait_ge(drained[7], DR["core"][7] + ML_HEADS)
            gains(3, g_mix_post[1:2, :], g_mlp_pre[1:2, :])
            for kc in range(2):
                lo_second(CH["w1a1"] + kc, kc, kc + 5)

        @block.scalar
        def _(act):
            def copy(dst, src, scale=None):
                if scale is None:
                    return nc.scalar.activation(dst, src, ACT.Copy)
                return nc.scalar.activation(dst, src, ACT.Copy, scale=scale)

            steps = [0]

            def then(ins):
                steps[0] += 1
                ins.then_inc(act_done, 1)
                act.wait_ge(act_done, steps[0])

            def rms(dst, src, signal):
                then(nc.scalar.activation(junk[:, :], src, ACT.Square, scale=D ** -0.5, accum_out=dst))
                nc.scalar.activation(dst, dst, ACT.Sqrt, bias=col(C_EPS)).then_inc(signal, 1)

            def hi(c, half, first=False, parts=(0, 1)):
                act.wait_ge(raw_in[half], raw_count(c, half))
                if not first:
                    act.wait_ge(chunk_done, c - 1)
                for q in parts:
                    copy(w_hi[half][:, q * 1024:(q + 1) * 1024], raw[half][:, q * 1024:(q + 1) * 1024]).then_inc(
                        hi_split, 1)

            def raw_count(c, half, ):
                return (c - half) * 8 + 16

            def norm_hi(stage, t):
                for q in range(2):
                    bk = 2 * t + q
                    act.wait_ge(tile_ready[bk], RD[stage][bk] + 1)
                    copy(aT_hi[:, 4 * q:4 * q + 4, t * P:(t + 1) * P],
                         bank[bk][:, :].rearrange("p (k t) -> p k t", k=4)).then_inc(aT_hi_ready, 1)

            act.wait_ge(pool_const, 1)
            then(nc.scalar.activation(col(C_RX), col(C_EPS), ACT.Sqrt))
            for t in (0, 1):
                act.wait_ge(x_in_sem[t], 16)
                rms(col(C_SSX + t), x[:, t, :], x_sq)
            norm_hi("norm0", 0)
            hi(0, 0, first=True)
            norm_hi("norm0", 1)
            for t in (2, 3):
                act.wait_ge(x_in_sem[t], 16)
                rms(col(C_SSX + t), x[:, t, :], x_sq)
            hi(1, 1, first=True)
            norm_hi("norm0", 2)
            norm_hi("norm0", 3)
            act.wait_ge(small_f_ready, 1)
            copy(small_hi[:, :, :], small_f[:, :, :]).then_inc(small_hi_ready, 1)

            c = CH["cgate"]
            hi(c, 0)
            for j in range(4):
                weighted_ready(act, "latent", j, 0, CH["latent"] + 1)
                copy(lat_raw[:, j, :], bank[j][:, :]).then_inc(drained[j], 1)
            hi(c + 1, 1)
            hi(c + 2, 0)
            act.wait_ge(angle_ready, 1)
            nc.scalar.activation(half_sin[:, :], ang[:, :], ACT.Sin, scale=0.5).then_inc(half_sin_ready, 1)
            nc.scalar.activation(turns[:, :], ang[:, :], ACT.Sin).then_inc(sin_raw_ready, 1)
            for j in range(4):
                weighted_ready(act, "cgate", j, 0, CH["cgate"] + 1)
                copy(c_conv[:, j, :], bank[j][:, :]).then_inc(drained[j], 1)
            for n in range(2):
                act.wait_ge(tile_ready[5 + n], RD["sumsq"][5 + n] + 1)
                nc.scalar.activation(lat_rstd[:, n, :], bank[5 + n][:, :], ACT.Sqrt, bias=col(C_EPS),
                                     scale=1.0 / RANK).then_inc(drained[5 + n], 1)
            hi(c + 3, 1)
            for j in range(4):
                act.wait_ge(lat_f_ready, j + 1)
                copy(lat_hi[:, j, :], lat_f[:, j, :]).then_inc(lat_hi_ready, 1)
            hi(c + 4, 0)
            hi(c + 5, 1)

            def laid_out(c, half, parts):
                act.wait_ge(raw_in[half], raw_count(c, half))
                act.wait_ge(chunk_done, c - 1)
                for n, (dst, src) in enumerate(parts(w_hi[half], raw[half])):
                    ins = copy(dst, src)
                    if n == 0:
                        first = ins
                first.then_inc(hi_split, 1)
                ins.then_inc(hi_split, 1)

            laid_out(CH["uq"], 0, uq_parts)
            laid_out(CH["ukv"], 1, ukv_parts)
            for j in range(4):
                act.wait_ge(drained[j], DR["bgate"][j] + 1)
                copy(aT_hi[:, j, :], b_conv[:, j, :]).then_inc(ya_hi_ready, 1)
            act.wait_ge(lat_ready, 4)
            for j in range(4):
                act.wait_ge(tile_ready[j], RD["uq"][j] + 1)
                copy(q_mla[0:NOPE, 2 * j, :], bank[j][0:64, :], ATT_SCALE)
                copy(q_mla[0:NOPE, 2 * j + 1, :], bank[j][64:128, :], ATT_SCALE).then_inc(drained[j], 1)
            then(nc.scalar.activation(col(C_RX), col(C_EPS), ACT.Exp))
            for t in range(NT):
                act.wait_ge(tile_ready[4 + t], RD["ukv"][4 + t] + 1)
                copy(v_mla[:, t, :], bank[4 + t][:, :]).then_inc(drained[4 + t], 1)
            for j in range(4):
                weighted_ready(act, "ukv", j, 0, CH["ukv"])
                copy(k_mla[0:NOPE, 2 * j, :], bank[j][0:64, :])
                copy(k_mla[0:NOPE, 2 * j + 1, :], bank[j][64:128, :]).then_inc(drained[j], 1)
            def att_exp(u):
                qt, h = u // HEADS, u % HEADS
                kv = (qt + 1) * P
                act.wait_ge(nmax_ready, u + 1)
                if u >= 2:
                    act.wait_ge(tile_ready[(u - 2) % 4], RD["att"][(u - 2) % 4] + 2 * ((u - 2) // 4) + 2)
                nc.scalar.activation(probs[:, u % 2, 0:kv], bank[u % 4][:, 0:kv], ACT.Exp, bias=col(C_NMAX + u),
                                     accum_out=col(C_RSUM + u)).then_inc(drained[u % 4], 1)

            def att_T(u):
                qt = u // HEADS
                bk = u % 4
                act.wait_ge(tile_ready[bk], RD["att"][bk] + 2 * (u // 4) + 2)
                if u >= 2:
                    act.wait_ge(pv_done, u - 1)
                copy(probsT[:, u % 2, 0:qt + 1, :], bank[bk][:, 0:(qt + 1) * P].rearrange(
                    "p (s t) -> p s t", t=P)).then_inc(drained[bk], 1)

            def yb_hi(qt):
                act.wait_ge(tile_ready[4 + qt], RD["att"][4 + qt] + 1)
                copy(aT_hi[:, 4:8, qt * P:(qt + 1) * P], bank[4 + qt][:, :].rearrange(
                    "p (k t) -> p k t", k=4)).then_inc(ya_hi_ready, 1)

            for u in range(NT * HEADS + 1):
                if u < NT * HEADS:
                    att_exp(u)
                if u >= 1:
                    att_T(u - 1)
                if u in (16, 18):
                    hi(CH["out0"], 0, parts=((u - 16) // 2,))
                if u in (20, 22):
                    hi(CH["out0"] + 1, 1, parts=((u - 20) // 2,))
                if u % HEADS == 4 and u > HEADS:
                    yb_hi(u // HEADS - 1)
            yb_hi(NT - 1)

            def y0_squares(i, phase):
                for t in range(NT):
                    act.wait_ge(drained[4 + t], DR[phase][4 + t] + 1)
                    if t:
                        act.wait_ge(y0_sq, NT * (i - 1) + t)
                    nc.scalar.activation(junk[:, 0:CW], y_acc[:, t, 0:CW], ACT.Square, scale=D ** -0.5,
                                         accum_out=col(C_SS0 + t)).then_inc(y0_sq, 1)

            def norm_stage(i, phase, add, next_chunk, last=False):
                def y_rms(t):
                    if add:
                        act.wait_ge(drained[4 + t], DR[phase][4 + t] + 2)
                        y1 = y_acc[:, t, CW:D]
                    else:
                        weighted_ready(act, phase, 4 + t, 1, CH[phase] + 3)
                        y1 = bank[4 + t][:, :]
                    nc.scalar.activation(junk[:, 0:CW], y1, ACT.Square, scale=D ** -0.5,
                                         accum_out=col(C_SSY + t)).then_inc(y1_sq, 1)
                    act.wait_ge(y1_sq, NT * (i - 1) + t + 1)
                    nc.scalar.activation(col(C_SSY + t), col(C_SSY + t), ACT.Sqrt,
                                         bias=col(C_BIAS + t)).then_inc(y_sq, 1)

                def x_rms(t):
                    act.wait_ge(x_new, NT * (i - 1) + t + 1)
                    rms(col(C_SSX + t), x[:, t, :], x_sq)

                act.wait_ge(y_bias, i)
                if last:
                    for t in range(NT):
                        y_rms(t)
                    return
                y_rms(0)
                for t in (0, 1):
                    if t == 0 and not add:
                        y_rms(1)
                    x_rms(t)
                    if t == 0 and add:
                        y_rms(1)
                norm_hi(f"norm{i}", 0)
                hi(next_chunk, 0)
                norm_hi(f"norm{i}", 1)
                y_rms(2)
                if not add:
                    y_rms(3)
                hi(next_chunk + 1, 1)
                x_rms(2)
                if add:
                    y_rms(3)
                norm_hi(f"norm{i}", 2)
                x_rms(3)
                norm_hi(f"norm{i}", 3)

            def out_proj(i, phase):
                c = CH[phase]
                hi(c + 2, 0)
                for t in range(NT):
                    if t == 3:
                        hi(c + 3, 1)
                    weighted_ready(act, phase, 4 + t, 0, c + 1)
                    copy(y_acc[:, t, 0:CW], bank[4 + t][:, :]).then_inc(drained[4 + t], 1)
                y0_squares(i, phase)
                norm_stage(i, phase, False, c + 4)

            def mlp(l, i, next_chunk):
                for h in range(FH):
                    p1, p2 = f"w1{'ab'[h]}{l}", f"w2{'ab'[h]}{l}"
                    c1, c2 = CH[p1], CH[p2]
                    u0 = (l * FH + h) * 4 * FG

                    def group(g):
                        hi(g * 2 + (c1 + 2), 0)
                        for j in range(4):
                            if j == 3:
                                act.wait_ge(chunk_done, g * 2 + (c1 + 2))
                            else:
                                act.wait_ge(tile_ready[j], g + (RD[p1][j] + 1))
                            act.wait_ge(u_sq, g * 4 + (u0 + j - 1 + 2))
                            nc.scalar.activation(relu[:, j % 2, :], bank[j][:, :], ACT.Relu).then_inc(drained[j], 1)
                            act.wait_ge(drained[j], g + (DR[p1][j] + 1))
                            nc.scalar.activation(uT_hi[:, bass.ds(g * 4 + j, 1), :].rearrange("p a t -> p (a t)"),
                                                 relu[:, j % 2, :], ACT.Square).then_inc(u_hi_ready, 1)

                    if h == 0:
                        group(0)
                    with act.Fori(1 - h, FG) as g:
                        hi(g * 2 + (c1 + 1), 1)
                        group(g)
                    if h == 0:
                        with act.Fori(0, 2) as n:
                            for k in range(4):
                                hi(n * 4 + (c2 + k + 1), (k + 1) % 2)
                            for t in range(NT):
                                if t == 3:
                                    act.wait_ge(chunk_done, n * 4 + (c2 + 4))
                                else:
                                    act.wait_ge(tile_ready[4 + t], n + (RD[p2][4 + t] + 1))
                                copy(y_acc[:, t, bass.ds(n * CW, CW)], bank[4 + t][:, :]).then_inc(drained[4 + t], 1)
                    else:
                        for k in range(4):
                            hi(c2 + k + 1, (k + 1) % 2)
                        hi(c2 + 5, 1)
                        y0_squares(i, p2)
                        hi(c2 + 6, 0)
                        hi(c2 + 7, 1)
                        norm_stage(i, p2, True, next_chunk, last=next_chunk is None)

            out_proj(1, "out0")
            mlp(0, 2, CH["qk"])

            c = CH["qk"]

            def qk_group(g):
                hi(g * 2 + (c + 2), 0)
                for j in range(4):
                    if j == 3:
                        act.wait_ge(chunk_done, g * 2 + (c + 2))
                    else:
                        act.wait_ge(tile_ready[j], g + (RD["qk"][j] + 1))
                    copy(qk_ml[:, bass.ds(g * 4 + j, 1), :].rearrange("p a t -> p (a t)"),
                         bank[j][:, :]).then_inc(drained[j], 1)

            act.wait_ge(small_f_ready, 2)
            copy(small_hi[:, :, :], small_f[:, :, :]).then_inc(small_hi_ready, 1)
            qk_group(0)
            hi(c + 3, 1)
            act.wait_ge(gate_f, 1)
            then(nc.scalar.activation(e_row[:, :], abs_row[:, :], ACT.Exp, scale=-1.0))
            nc.scalar.activation(e_row[:, :], e_row[:, :], ACT.Ln, bias=1.0).then_inc(gate_ln, 1)
            qk_group(1)
            act.wait_ge(sel_ready, 1)
            copy(head_sel_r[:, :], head_sel[:, :]).then_inc(sel_r_ready, 1)
            act.wait_ge(rows_ready, 1)
            copy(row_f_hi[:, :], row_f[:, :]).then_inc(row_hi_ready, 1)
            act.wait_ge(tile_ready[4], RD["gates"][4] + 2)
            then(copy(ucol[:, :, :], bank[4][:, 0:4 * (len(PAIRS) + NT)].rearrange("p (c h) -> p c h", h=ML_HEADS)))
            nc.scalar.activation(ucol[:, len(PAIRS):, :], ucol[:, len(PAIRS):, :], ACT.Exp, scale=-1.0).then_inc(
                drained[4], 1)
            with act.Fori(2, 4) as g:
                hi(g * 2 + (c + 1), 1)
                qk_group(g)
            c = CH["ogate"]
            for g in range(2):
                hi(c + 2 * g + 1, 1)
                hi(c + 2 * g + 2, 0)
                for j in range(4):
                    weighted_ready(act, "ogate", j, g, c + 2 * g + 1)
                    nc.scalar.activation(o_ml[:, 4 * g + j, :], bank[j][:, :], ACT.Sigmoid).then_inc(drained[j], 1)
            act.wait_ge(rows_ready, 1)
            act.wait_ge(drained[4], DR["gates"][4] + 2)

            def decays(i):
                h, s = i // NT, i % NT
                if s == 0:
                    act.wait_ge(tile_ready[0], RD["core"][0] + h + 1)
                if i >= 2:
                    act.wait_ge(wgt_ready, i - 1)
                for t in range(s, NT):
                    ins = nc.scalar.activation(decay[:, i % 2, t * P:(t + 1) * P], bank[0][:, t * P:(t + 1) * P],
                                               ACT.Exp, bias=ucol[:, PAIRS.index((s, t)), h:h + 1])
                ins.then_inc(decay_raw, 1)

            c = CH["v"]
            for g in range(2):
                hi(c + 2 * g + 1, 1)
                hi(c + 2 * g + 2, 0)
                if g == 1:
                    decays(0)
                    decays(1)
                for t in range(NT):
                    weighted_ready(act, "v", 4 + t, g, c + 2 * g + 1)
                    copy(v_aug[:, t, 2 * g:2 * g + 2, 0:DH], bank[4 + t][:, :].rearrange(
                        "p (h d) -> p h d", h=2)).then_inc(drained[4 + t], 1)
            posts = [(h, t) for h in range(ML_HEADS) for t in range(NT)]

            def post_sq(h, t):
                n = h * NT + t
                act.wait_ge(den_ready, n + 1)
                nc.scalar.activation(cell[:, t, h * DH:(h + 1) * DH], bank[4 + t][:, 0:DH], ACT.Square,
                                     scale=col(C_RDEN + 5 * (n % 4)),
                                     accum_out=col(C_RH + n)).then_inc(ssh_ready, 1)

            def h_rms(h0, h1):
                act.wait_ge(ssh_ready, NT * h1)
                c = col(C_RH + NT * h0, NT * (h1 - h0))
                nc.scalar.activation(c, c, ACT.Sqrt, bias=col(C_EPS), scale=1.0 / DH).then_inc(rms_h_ready, 1)

            for h, s in posts:
                i = h * NT + s
                if i >= 2:
                    decays(i)
                if i == 2:
                    hi(CH["out1"] + 1, 1)
                if i == len(posts) - 1:
                    h_rms(0, 3)
                if i >= 2 and s != 1:
                    post_sq(*posts[i - 2])
                if i >= 2 and s == 0:
                    post_sq(*posts[i - 1])
            for f in range(8):
                if f == 4:
                    post_sq(*posts[-2])
                    post_sq(*posts[-1])
                    h_rms(3, 4)
                act.wait_ge(drained[f % 4], DR["cellT"][f % 4] + f // 4 + 1)
                copy(aT_hi[:, f, :], cell_f[:, f % 2, :]).then_inc(cell_hi_ready, 1)
            out_proj(3, "out1")
            mlp(1, 4, None)

        @block.vector
        def _(dve):
            V = nc.vector
            steps = [0]

            def then(ins):
                steps[0] += 1
                ins.then_inc(dve_done, 1)
                dve.wait_ge(dve_done, steps[0])

            def lo(c, half):
                for q in range(2):
                    dve.wait_ge(hi_split, c * 2 + (q + 1))
                    ins = V.tensor_tensor(w_lo[half][:, q * 1024:(q + 1) * 1024], raw[half][:, q * 1024:(q + 1) * 1024],
                                          w_hi[half][:, q * 1024:(q + 1) * 1024].bitcast(fp32), ALU.subtract)
                ins.then_inc(lo_split, 1)

            def lo_first(c, half):
                dve.wait_ge(hi_split, c * 2 + 1)
                V.tensor_tensor(w_lo[half][:, 0:1024], raw[half][:, 0:1024], w_hi[half][:, 0:1024].bitcast(fp32),
                                ALU.subtract).then_inc(lo_first_done, 1)

            def laid_out(c, half, parts):
                dve.wait_ge(hi_split, 2 * c + 2)
                hs = [h for h, _ in parts(w_hi[half], raw[half])]
                for h, (dst, src) in zip(hs, parts(w_lo[half], raw[half])):
                    ins = V.tensor_tensor(dst, src, h.bitcast(fp32), ALU.subtract)
                ins.then_inc(lo_split, 1)

            def norm_lo(i, t):
                for q in range(2):
                    bk = 2 * t + q
                    dve.wait_ge(aT_hi_ready, 2 * (NT * i + t) + q + 1)
                    dst = slice(t * P, (t + 1) * P)
                    V.tensor_tensor(aT_lo[:, 4 * q:4 * q + 4, dst], bank[bk][:, :].rearrange("p (k t) -> p k t", k=4),
                                    aT_hi[:, 4 * q:4 * q + 4, dst].bitcast(fp32), ALU.subtract).then_inc(drained[bk], 1)

            def pre_norm(i, t):
                dve.wait_ge(x_sq, NT * i + t + 1)
                then(V.reciprocal(col(C_RX + t), col(C_SSX + t)))
                if t >= 2:
                    dve.wait_ge(tile_ready[2 * t - 3], RD[f"norm{i}"][2 * t - 3] + 1)
                V.scalar_tensor_tensor(h_tok[:, t % 2, :], x[:, t, :], col(C_RX + t), g_pre[:, :], ALU.mult,
                                       ALU.mult).then_inc(h_ready, 1)

            dve.wait_ge(gain_in[0], 16)
            pre_norm(0, 0)
            pre_norm(0, 1)
            norm_lo(0, 0)
            lo(0, 0)
            norm_lo(0, 1)
            pre_norm(0, 2)
            pre_norm(0, 3)
            lo(1, 1)
            norm_lo(0, 2)
            norm_lo(0, 3)
            dve.wait_ge(small_in[0], 16)
            V.tensor_copy(small_f[:, :, 0:32], small_raw[:, :, :])
            V.tensor_copy(small_f[:, :, 32:48], small_raw[:, :, 16:32])
            V.tensor_copy(small_f[:, :, 48:64], small_raw[:, :, 0:16]).then_inc(small_f_ready, 1)
            dve.wait_ge(small_hi_ready, 1)
            V.tensor_tensor(small_lo[:, :, :], small_f[:, :, :], small_hi[:, :, :].bitcast(fp32),
                            ALU.subtract).then_inc(small_ready, 1)
            lo(2, 0)
            for j in range(4):
                dve.wait_ge(drained[j], DR["latent"][j] + 1)
                V.tensor_tensor(lat_sq[:, j, :], lat_raw[:, j, :], lat_raw[:, j, :], ALU.mult).then_inc(lat_sq_ready, 1)
            lo(3, 1)
            dve.wait_ge(const_in, 16 * 7)
            dve.wait_ge(pos_in_sem, 16)
            dve.wait_ge(small_ready, 1)
            then(V.tensor_scalar(ang[:, :], pos_i[:, :], col(C_INV), None, ALU.mult))
            for period, parts in ((BIG, BIG_PARTS), (TWO_PI, PI_PARTS)):
                then(V.tensor_scalar(turns[:, :], ang[:, :], 1.0 / period, MAGIC, ALU.mult, ALU.add))
                then(V.tensor_scalar(turns[:, :], turns[:, :], MAGIC, None, ALU.subtract))
                for part in parts:
                    then(V.scalar_tensor_tensor(ang[:, :], turns[:, :], -part, ang[:, :], ALU.mult, ALU.add))
            V.tensor_scalar(ang[:, :], ang[:, :], PI_MAX, -PI_MAX, ALU.min, ALU.max).then_inc(angle_ready, 1)
            lo(4, 0)
            dve.wait_ge(half_sin_ready, 1)
            then(V.tensor_tensor(cos_t[:, :], half_sin[:, :], half_sin[:, :], ALU.mult))
            then(V.tensor_scalar(cos_t[:, :], cos_t[:, :], -2.0, 1.0, ALU.mult, ALU.add))
            dve.wait_ge(sin_raw_ready, 1)
            then(V.tensor_scalar(sin_t[:, :], turns[:, :], col(C_SIGN), None, ALU.mult))
            dve.wait_ge(tile_ready[4], RD["krope"][4] + 1)
            V.tensor_tensor(rot_a[NOPE:QK, :], bank[4][0:32, :], cos_t[0:32, :], ALU.mult)
            V.tensor_tensor(rot_b[NOPE:QK, :], bank[4][32:64, :], sin_t[32:64, :], ALU.mult).then_inc(drained[4], 1)
            for n in range(2):
                dve.wait_ge(drained[5 + n], DR["sumsq"][5 + n] + 1)
                then(V.reciprocal(lat_rstd[:, n, :], lat_rstd[:, n, :]))
                if n == 0:
                    lo(CH["hconv"] + 1, 1)
            for j in range(4):
                V.scalar_tensor_tensor(lat_f[:, j, :], lat_raw[:, j, :], col((C_QG if j < 2 else C_KVG) + j % 2),
                                       lat_rstd[:, j // 2, :], ALU.mult, ALU.mult).then_inc(lat_f_ready, 1)
            for j in range(4):
                dve.wait_ge(lat_hi_ready, j + 1)
                V.tensor_tensor(lat_lo[:, j, :], lat_f[:, j, :], lat_hi[:, j, :].bitcast(fp32),
                                ALU.subtract).then_inc(lat_ready, 1)
            lo(CH["bgate"], 0)
            for j in range(4):
                weighted_ready(dve, "hconv", j, 0, CH["hconv"] + 1)
                V.tensor_tensor(u_conv[:, j, :], c_conv[:, j, :], bank[j][:, :], ALU.mult).then_inc(drained[j], 1)
            lo(CH["bgate"] + 1, 1)
            dve.wait_ge(drained[3], DR["hconv"][3] + 1)
            for j in range(4):
                def tap(w):
                    return col(C_CONV + 4 * w + j)
                then(V.tensor_scalar(c_conv[:, j, :], u_conv[:, j, :], tap(2), None, ALU.mult))
                then(V.scalar_tensor_tensor(c_conv[:, j, 1:S], u_conv[:, j, 0:S - 1], tap(1), c_conv[:, j, 1:S],
                                            ALU.mult, ALU.add))
                then(V.scalar_tensor_tensor(c_conv[:, j, 2:S], u_conv[:, j, 0:S - 2], tap(0), c_conv[:, j, 2:S],
                                            ALU.mult, ALU.add))
            laid_out(CH["uq"], 0, uq_parts)
            for j in range(4):
                weighted_ready(dve, "bgate", j, 0, CH["bgate"] + 1)
                V.tensor_tensor(b_conv[:, j, :], c_conv[:, j, :], bank[j][:, :], ALU.mult).then_inc(drained[j], 1)
            laid_out(CH["ukv"], 1, ukv_parts)
            dve.wait_ge(k_rope_ready, HEADS)
            for n in range(2):
                dve.wait_ge(tile_ready[n], RD["uq"][n] + 2)
                V.scalar_tensor_tensor(rot_a[:, :], bank[n][:, :], ATT_SCALE, cos_t[:, :], ALU.mult,
                                       ALU.mult).then_inc(drained[n], 1)
                if n == 0:
                    dve.wait_ge(tile_ready[2], RD["uq"][2] + 2)
                else:
                    dve.wait_ge(chunk_done, CH["uq"] + 1)
                V.scalar_tensor_tensor(rot_b[:, :], bank[2 + n][:, :], ATT_SCALE, sin_t[:, :], ALU.mult,
                                       ALU.mult).then_inc(drained[2 + n], 1)
                dve.wait_ge(drained[n], DR["uq"][n] + 2)
                dve.wait_ge(drained[2 + n], DR["uq"][2 + n] + 2)
                for r in range(4):
                    ins = V.tensor_tensor(q_mla[NOPE:QK, 4 * n + r, :], rot_a[32 * r:32 * r + 32, :],
                                          rot_b[32 * r:32 * r + 32, :], ALU.add)
                ins.then_inc(q_rope_ready, 1)
                dve.wait_ge(q_rope_ready, n + 1)

            def att_max(u):
                qt, h = u // HEADS, u % HEADS
                kv = (qt + 1) * P
                dve.wait_ge(tile_ready[u % 4], RD["att"][u % 4] + 2 * (u // 4) + 1)
                then(V.memset(bank[u % 4][0:CHUNK, kv - CHUNK:kv], NEG))
                V.tensor_reduce(col(C_NMAX + u), bank[u % 4][:, 0:kv], AX.X, ALU.max, negate=True).then_inc(
                    nmax_ready, 1)

            def att_norm(qt):
                u0 = qt * HEADS
                dve.wait_ge(pv_done, u0 + HEADS)
                then(V.reciprocal(col(C_RINV + u0, HEADS), col(C_RSUM + u0, HEADS)))
                V.tensor_tensor(y_acc[:, qt, 0:512].rearrange("p (h d) -> p h d", h=HEADS),
                                bank[4 + qt][:, :].rearrange("p (h d) -> p h d", h=HEADS),
                                col(C_RINV + u0, HEADS).unsqueeze(2).to_broadcast([P, HEADS, VD]),
                                ALU.mult).then_inc(drained[4 + qt], 1)

            def yb_lo(qt):
                dve.wait_ge(ya_hi_ready, 4 + qt + 1)
                V.tensor_tensor(aT_lo[:, 4:8, qt * P:(qt + 1) * P],
                                bank[4 + qt][:, :].rearrange("p (k t) -> p k t", k=4),
                                aT_hi[:, 4:8, qt * P:(qt + 1) * P].bitcast(fp32),
                                ALU.subtract).then_inc(drained[4 + qt], 1)

            for u in range(NT * HEADS):
                att_max(u)
                if u == 20:
                    lo(CH["out0"], 0)
                if u == 25:
                    lo(CH["out0"] + 1, 1)
                if 21 <= u < 25:
                    j = u - 21
                    dve.wait_ge(ya_hi_ready, j + 1)
                    V.tensor_tensor(aT_lo[:, j, :], b_conv[:, j, :], aT_hi[:, j, :].bitcast(fp32),
                                    ALU.subtract).then_inc(ya_ready, 1)
                if u % HEADS == 2 and u > HEADS:
                    att_norm(u // HEADS - 1)
                if u % HEADS == 5 and u > HEADS:
                    yb_lo(u // HEADS - 1)
            att_norm(NT - 1)
            yb_lo(NT - 1)

            def y0_gain(i, last=False):
                dve.wait_ge(final_gain_in if last else gain_in[i], 16 if last else 32)
                for t in range(NT):
                    dve.wait_ge(y0_sq, NT * (i - 1) + t + 1)
                    V.tensor_tensor(y_acc[:, t, 0:CW], y_acc[:, t, 0:CW], g_post[:, 0:CW], ALU.mult).then_inc(
                        y0_gained, 1)
                V.tensor_scalar(col(C_BIAS, NT), col(C_SS0, NT), EPS, None, ALU.add).then_inc(y_bias, 1)

            def norm_stage(i, phase, add, next_chunk, last=False):
                def y_last(t):
                    if add:
                        weighted_ready(dve, phase, 4 + t, 1, CH[phase] + 7)
                        V.tensor_tensor(y_acc[:, t, CW:D], y_acc[:, t, CW:D], bank[4 + t][:, :],
                                        ALU.add).then_inc(drained[4 + t], 1)
                        if last:
                            dve.wait_ge(drained[4 + t], DR[phase][4 + t] + 2)
                            V.tensor_tensor(y_gain[:, t % 2, :], y_acc[:, t, CW:D], g_post[:, CW:D],
                                            ALU.mult).then_inc(y1_gained, 1)
                    else:
                        dve.wait_ge(y1_sq, NT * (i - 1) + t + 1)
                        V.tensor_tensor(y_gain[:, t % 2, :], bank[4 + t][:, :], g_post[:, CW:D],
                                        ALU.mult).then_inc(drained[4 + t], 1)

                def x_add(t):
                    n = NT * (i - 1) + t
                    if add:
                        dve.wait_ge(y1_gained, NT * (i // 2 - 1) + t + 1)
                    else:
                        dve.wait_ge(drained[4 + t], DR[phase][4 + t] + 2)
                    dve.wait_ge(y_sq, n + 1)
                    then(V.reciprocal(col(C_RY + t), col(C_SSY + t)))
                    ins = V.scalar_tensor_tensor(x[:, t, 0:CW], y_acc[:, t, 0:CW], col(C_RY + t), x[:, t, 0:CW],
                                                 ALU.mult, ALU.add)
                    if last:
                        ins.then_inc(x_first, 1)
                    V.scalar_tensor_tensor(x[:, t, CW:D], y_gain[:, t % 2, :], col(C_RY + t), x[:, t, CW:D], ALU.mult,
                                           ALU.add).then_inc(x_new, 1)

                dve.wait_ge(y0_gained, NT * i)
                y_last(0)
                if last:
                    for t in range(NT):
                        x_add(t)
                        if t < NT - 1:
                            y_last(t + 1)
                    return
                x_add(0)
                y_last(1)
                pre_norm(i, 0)
                x_add(1)
                pre_norm(i, 1)
                norm_lo(i, 0)
                if add:
                    y_last(2)
                lo_first(next_chunk, 0)
                norm_lo(i, 1)
                if not add:
                    y_last(2)
                x_add(2)
                y_last(3)
                lo_first(next_chunk + 1, 1)
                pre_norm(i, 2)
                x_add(3)
                norm_lo(i, 2)
                pre_norm(i, 3)
                norm_lo(i, 3)

            def out_proj(i, phase):
                c = CH[phase]
                lo(c + 2, 0)
                lo(c + 3, 1)
                y0_gain(i)
                norm_stage(i, phase, False, c + 4)

            def mlp(l, i, next_chunk):
                for h in range(FH):
                    p1, p2 = f"w1{'ab'[h]}{l}", f"w2{'ab'[h]}{l}"
                    c1, c2 = CH[p1], CH[p2]
                    u0 = (l * FH + h) * 4 * FG

                    def group(g):
                        lo(g * 2 + (c1 + 2), 0)
                        for j in range(4):
                            dve.wait_ge(drained[j], g + (DR[p1][j] + 1))
                            V.tensor_tensor(usq[:, j % 2, :], relu[:, j % 2, :], relu[:, j % 2, :],
                                            ALU.mult).then_inc(u_sq, 1)
                            dve.wait_ge(u_sq, g * 4 + (u0 + j + 1 + 2))
                            dve.wait_ge(u_hi_ready, g * 4 + (u0 + j + 1))
                            V.tensor_tensor(uT_lo[:, bass.ds(g * 4 + j, 1), :].rearrange("p a t -> p (a t)"),
                                            usq[:, j % 2, :],
                                            uT_hi[:, bass.ds(g * 4 + j, 1), :].rearrange("p a t -> p (a t)").bitcast(
                                                fp32), ALU.subtract).then_inc(u_ready, 1)

                    if h == 0:
                        group(0)
                    with dve.Fori(1 - h, FG) as g:
                        lo(g * 2 + (c1 + 1), 1)
                        group(g)
                    if h == 0:
                        with dve.Fori(0, 2) as n:
                            for k in range(4):
                                lo(n * 4 + (c2 + k + 1), (k + 1) % 2)
                    else:
                        for k in range(4):
                            lo(c2 + k + 1, (k + 1) % 2)
                        for t in range(NT):
                            weighted_ready(dve, p2, 4 + t, 0, c2 + 3)
                            V.tensor_tensor(y_acc[:, t, 0:CW], y_acc[:, t, 0:CW], bank[4 + t][:, :],
                                            ALU.add).then_inc(drained[4 + t], 1)
                        lo(c2 + 5, 1)
                        lo(c2 + 6, 0)
                        lo(c2 + 7, 1)
                        y0_gain(i, last=next_chunk is None)
                        norm_stage(i, p2, True, next_chunk, last=next_chunk is None)

            out_proj(1, "out0")
            V.memset(col(C_DEN), 0.0).then_inc(u_sq, 2)
            mlp(0, 2, CH["qk"])

            dve.wait_ge(small_in[1], 16)
            then(V.memset(small_f[:, :, :], 0.0))
            V.tensor_copy(small_f[:, :, 0:4], small_raw[:, :, 0:4])
            V.tensor_copy(small_f[:, :, 32:36], small_raw[:, :, 4:8]).then_inc(small_f_ready, 1)
            dve.wait_ge(small_hi_ready, 2)
            V.tensor_tensor(small_lo[:, :, :], small_f[:, :, :], small_hi[:, :, :].bitcast(fp32),
                            ALU.subtract).then_inc(small_ready, 1)
            dve.wait_ge(small_ready, 2)
            V.memset(zero_row[:, :], 0.0)
            lo(CH["qk"] + 2, 0)
            lo(CH["qk"] + 3, 1)
            dve.wait_ge(tile_ready[4], RD["gates"][4] + 1)
            V.tensor_scalar(row_i[:, :], bank[4][0:4, :], col(C_BI, 1, 4), None, ALU.add)
            V.tensor_scalar(row_f[:, :], bank[4][32:36, :], col(C_BF, 1, 4), None, ALU.add).then_inc(drained[4], 1)
            dve.wait_ge(drained[4], DR["gates"][4] + 1)
            V.scalar_tensor_tensor(abs_row[:, :], row_f[:, :], -1.0, row_f[:, :], ALU.mult, ALU.max).then_inc(gate_f, 1)
            dve.wait_ge(gate_ln, 1)
            then(V.scalar_tensor_tensor(row_f[:, :], row_f[:, :], 0.0, e_row[:, :], ALU.min, ALU.subtract))
            V.tensor_tensor_scan(row_m[:, :], row_f[:, :], row_i[:, :], 0.0, ALU.add, ALU.max)
            for t in range(NT):
                ins = V.tensor_tensor_scan(row_b[:, t * P:(t + 1) * P], row_f[:, t * P:(t + 1) * P],
                                           zero_row[:, t * P:(t + 1) * P], 0.0, ALU.add, ALU.add)
            then(ins)
            then(V.tensor_tensor(row_i[:, :], row_i[:, :], row_b[:, :], ALU.subtract))
            then(V.tensor_tensor(row_f[:, :], row_b[:, :], row_m[:, :], ALU.subtract))
            for t in range(1, NT):
                at_t = FAR.index((0, t)) * P
                total = row_b[:, t * P - 1:t * P]
                if t > 1:
                    before = FAR.index((0, t - 1)) * P
                    V.tensor_scalar(row_far[:, at_t:at_t + (t - 1) * P], row_far[:, before:before + (t - 1) * P], total,
                                    None, ALU.add)
                ins = V.tensor_scalar(row_far[:, at_t + (t - 1) * P:at_t + t * P], row_i[:, (t - 1) * P:t * P], total,
                                      None, ALU.add)
                if t < NT - 1:
                    then(ins)
            ins.then_inc(rows_ready, 1)
            V.memset(v_aug[:, :, :, DH:DH + 1], 1.0).then_inc(v_ones, 1)
            lo(CH["qk"] + 4, 0)
            dve.wait_ge(row_hi_ready, 1)
            V.tensor_tensor(row_f_lo[:, :], row_f[:, :], row_f_hi[:, :].bitcast(fp32), ALU.subtract).then_inc(
                row_lo_ready, 1)
            for k in range(4, 8):
                lo(CH["qk"] + k + 1, (k + 1) % 2)
            c = CH["ogate"]
            for k in range(4):
                lo(c + k + 1, (k + 1) % 2)
            c = CH["v"]
            for k in range(4):
                lo(c + k + 1, (k + 1) % 2)

            posts = [(h, t) for h in range(ML_HEADS) for t in range(NT)]

            def den(h, t):
                n = h * NT + t
                dve.wait_ge(tile_ready[4 + t], RD["core"][4 + t] + h + 1)
                k = 5 * (n % 4)
                floor = ucol[:, len(PAIRS) + t, h:h + 1]
                then(V.tensor_scalar(col(C_DEN + k), bank[4 + t][:, DH:DH + 1], floor, None, ALU.max))
                then(V.scalar_tensor_tensor(col(C_DEN + k), bank[4 + t][:, DH:DH + 1], -1.0, col(C_DEN + k), ALU.mult,
                                            ALU.max))
                V.reciprocal(col(C_RDEN + k), col(C_DEN + k)).then_inc(den_ready, 1)

            def divide(h, t):
                n = h * NT + t
                dve.wait_ge(ssh_ready, n + 1)
                V.tensor_scalar(cell[:, t, h * DH:(h + 1) * DH], bank[4 + t][:, 0:DH], col(C_RDEN + 5 * (n % 4)),
                                None, ALU.mult).then_inc(drained[4 + t], 1)

            def head_norm(h0, h1, roots):
                if roots:
                    dve.wait_ge(rms_h_ready, 1 if h0 == 0 else 2)
                    c = col(C_RH, NT * 3) if h0 == 0 else col(C_RH + NT * 3, NT)
                    then(V.reciprocal(c, c))
                for h in range(h0, h1):
                    for t in range(NT):
                        part = cell[:, t, h * DH:(h + 1) * DH]
                        V.tensor_scalar(part, part, col(C_RH + h * NT + t), None, ALU.mult).then_inc(cell_ready, 1)

            def weights(i):
                s, bk = i % NT, 1 + i % 2
                dve.wait_ge(tile_ready[bk], RD["core"][bk] + i // 2 + 1)
                dve.wait_ge(decay_ready, i + 1)
                V.scalar_tensor_tensor(wgtT[:, i % 2, s * P:S], bank[bk][:, s * P:S], ML_SCALE,
                                       decay[:, i % 2, s * P:S], ALU.mult, ALU.mult).then_inc(wgt_ready, 1)

            for i in range(len(posts) - 1):
                if i == 3:
                    lo(CH["out1"] + 1, 1)
                weights(i)
                if i >= 1:
                    den(*posts[i - 1])
                if i >= 2 and i % NT != 1:
                    divide(*posts[i - 2])
                if i >= 2 and i % NT == 0:
                    divide(*posts[i - 1])
            weights(len(posts) - 1)
            head_norm(0, 2, True)
            def y_f(f):
                bk = f % 4
                dve.wait_ge(drained[bk], DR["ogate"][bk] + 2)
                if f >= 2:
                    dve.wait_ge(ya_ready, 4 + f - 1)
                dve.wait_ge(tile_ready[bk], RD["cellT"][bk] + f // 4 + 1)
                V.scalar_tensor_tensor(cell_f[:, f % 2, :], bank[bk][:, :], col(C_HEAD + f), o_ml[:, f, :], ALU.mult,
                                       ALU.mult).then_inc(drained[bk], 1)

            def y_lo(f):
                dve.wait_ge(cell_hi_ready, f + 1)
                V.tensor_tensor(aT_lo[:, f, :], cell_f[:, f % 2, :], aT_hi[:, f, :].bitcast(fp32),
                                ALU.subtract).then_inc(ya_ready, 1)

            for f0 in (0, 4):
                y_f(f0)
                y_f(f0 + 1)
                for f in range(f0, f0 + 4):
                    y_lo(f)
                    if f < f0 + 2:
                        y_f(f + 2)
                if f0 == 0:
                    divide(*posts[-3])
                    head_norm(2, 3, False)
                    den(*posts[-2])
                    den(*posts[-1])
                    divide(*posts[-2])
                    divide(*posts[-1])
                    head_norm(3, 4, True)
            out_proj(3, "out1")
            mlp(1, 4, None)

        @block.tensor
        def _(pe):
            def mm3(dst, st_hi, st_lo, mv_hi, mv_lo, start, stop):
                nc.tensor.matmul(dst, st_lo, mv_hi, start=start, stop=False)
                nc.tensor.matmul(dst, st_hi, mv_lo, start=False, stop=False)
                return nc.tensor.matmul(dst, st_hi, mv_hi, start=False, stop=stop)

            def w(half, kt, cols_):
                v = [z[half][:, :].rearrange("p (k f) -> p k f", k=CK)[:, kt, cols_] for z in (w_hi, w_lo)]
                return v

            def columns(phase, c0, rnd, loop_rnd=None):
                for kc in range(2):
                    pe.wait_ge(lo_split, c0 + (kc + 1))
                    for j in range(4):
                        if kc == 0:
                            pe.wait_ge(drained[j], rnd + DR[phase][j])
                        for kt in range(CK):
                            k = kc * CK + kt
                            wh, wl = w(kc, kt, slice(j * P, (j + 1) * P))
                            ins = mm3(bank[j][:, :], wh, wl, aT_hi[:, k, :], aT_lo[:, k, :], k == 0, k == KT - 1)
                        if j == 3:
                            ins.then_inc(chunk_done, 1)
                        elif kc == 1:
                            ins.then_inc(tile_ready[j], 1)

            def rows(phase, c0, rnd, nk, lhs_hi, lhs_lo, lhs_ready=None, order=None, after=None):
                def tile(kc, t):
                    if kc == 0:
                        pe.wait_ge(drained[4 + t], rnd + DR[phase][4 + t])
                    for kt in range(CK):
                        k = kc * CK + kt
                        wh, wl = w(kc % 2, kt, slice(0, CW))
                        ts = slice(t * P, (t + 1) * P)
                        if t == 0 and lhs_ready is not None:
                            lhs_ready(k)
                        ins = mm3(bank[4 + t][:, :], lhs_hi[:, k, ts], lhs_lo[:, k, ts], wh, wl, k == 0,
                                  k == nk * CK - 1)
                    if t == 3:
                        ins.then_inc(chunk_done, 1)
                    elif kc == nk - 1:
                        ins.then_inc(tile_ready[4 + t], 1)
                    if after is not None and (kc, t) in after:
                        after[kc, t]()

                steps = [(kc, t) for kc in range(nk) for t in range(NT)]
                if order is not None:
                    steps = steps[:-2 * NT] + [(nk - 2 + kc, t) for kc, t in order]
                for kc, t in steps:
                    if t == 0:
                        pe.wait_ge(lo_split, c0 + (kc + 1))
                    tile(kc, t)

            PAIRWISE = [(kc, t + d) for t in (0, 2) for kc in range(2) for d in range(2)]
            SINGLY = PAIRWISE[:4] + [(kc, t) for t in (2, 3) for kc in range(2)]

            def norm_first(i, nk):
                return {(nk - 2, 3): lambda: norm_T(i, 0), (nk - 1, 2): lambda: norm_T(i, 1)}

            def norm_T(i, t):
                pe.wait_ge(h_ready, NT * i + t + 1)
                for q in range(2):
                    bk = 2 * t + q
                    n = DR[f"norm{i}"][bk]
                    if n:
                        pe.wait_ge(drained[bk], n)
                    for k in range(4):
                        f = (4 * q + k) * P
                        ins = nc.tensor.transpose(bank[bk][:, k * P:(k + 1) * P], h_tok[:, t % 2, f:f + P], ident[:, :])
                    ins.then_inc(tile_ready[bk], 1)

            T_AFTER = (3, 2)

            def columns_halves(phase, i):
                c0 = CH[phase]
                for part in range(2):
                    ts = slice(part * S // 2, (part + 1) * S // 2)
                    for kc in range(2):
                        if part == 0:
                            pe.wait_ge(lo_split, c0 + kc + 1)
                        for n, j in enumerate((0, 2, 1, 3)):
                            if n == 0 and kc == 0:
                                for bk in (4 * part, 4 * part + 2):
                                    pe.wait_ge(drained[bk], DR[f"norm{i}"][bk] + 1)
                            if n == (2 if part == 0 else 0) and kc == part:
                                for bk in (4 * part + 1, 4 * part + 3):
                                    pe.wait_ge(drained[bk], DR[f"norm{i}"][bk] + 1)
                            for kt in range(CK):
                                k = kc * CK + kt
                                wh, wl = w(kc, kt, slice(j * P, (j + 1) * P))
                                ins = mm3(bank[j][:, ts], wh, wl, aT_hi[:, k, ts], aT_lo[:, k, ts], k == 0,
                                          k == KT - 1)
                            if part == 1 and j == 3:
                                ins.then_inc(chunk_done, 1)
                            elif part == 1 and kc == 1:
                                ins.then_inc(tile_ready[j], 1)
                            if part == 0 and n == T_AFTER[kc]:
                                norm_T(i, 2 + kc)

            pe.wait_ge(pool_const, 1)
            for _ in range(32):
                nc.tensor.transpose(bank[7][:, 0:P], ident[:, :], ident[:, :])
            norm_T(0, 0)
            norm_T(0, 1)
            for _ in range(16):
                nc.tensor.transpose(bank[7][:, 0:P], ident[:, :], ident[:, :])
            columns_halves("latent", 0)
            pe.wait_ge(small_ready, 1)
            for k in range(KT):
                ins = mm3(bank[4][0:64, :], small_hi[:, k, :], small_lo[:, k, :], aT_hi[:, k, :], aT_lo[:, k, :],
                          k == 0, k == KT - 1)
            ins.then_inc(tile_ready[4], 1)
            columns("cgate", CH["cgate"], 0)
            for n in range(2):
                pe.wait_ge(lat_sq_added, n + 1)
                nc.tensor.matmul(bank[5 + n][:, :], ones[:, :], lat_sq[:, 2 * n, :], start=True,
                                 stop=True).then_inc(tile_ready[5 + n], 1)
            columns("hconv", CH["hconv"], 0)
            columns("bgate", CH["bgate"], 0)

            def w2(half, k, c_):
                return [z[half][:, :].rearrange("p (k f) -> p k f", k=2)[:, k, c_] for z in (w_hi, w_lo)]

            pe.wait_ge(lo_split, CH["uq"] + 1)
            pe.wait_ge(lat_ready, 4)
            for rnd in range(2):
                for j in range(4):
                    pe.wait_ge(drained[j], DR["uq"][j] + rnd)
                    for k in range(2):
                        wh, wl = w2(0, k, slice((4 * rnd + j) * P, (4 * rnd + j + 1) * P))
                        ins = mm3(bank[j][:, :], wh, wl, lat_hi[:, k, :], lat_lo[:, k, :], k == 0, k == 1)
                    ins.then_inc(chunk_done if rnd == 1 and j == 3 else tile_ready[j], 1)
            pe.wait_ge(lo_split, CH["ukv"] + 1)
            for t in range(NT):
                pe.wait_ge(drained[4 + t], DR["ukv"][4 + t])
                for k in range(2):
                    wh, wl = w2(1, k, slice(512, 1024))
                    ts = slice(t * P, (t + 1) * P)
                    ins = mm3(bank[4 + t][:, :], lat_hi[:, 2 + k, ts], lat_lo[:, 2 + k, ts], wh, wl, k == 0, k == 1)
                ins.then_inc(tile_ready[4 + t], 1)
            for j in range(4):
                pe.wait_ge(drained[j], DR["ukv"][j])
                for k in range(2):
                    wh, wl = w2(1, k, slice(j * P, (j + 1) * P))
                    ins = mm3(bank[j][:, :], wh, wl, lat_hi[:, 2 + k, :], lat_lo[:, 2 + k, :], k == 0, k == 1)
                ins.then_inc(chunk_done if j == 3 else tile_ready[j], 1)

            def scores(u):
                qt, h = u // HEADS, u % HEADS
                bk = u % 4
                pe.wait_ge(drained[bk], DR["att"][bk] + 2 * (u // 4))
                if u < HEADS and h % 2 == 0:
                    pe.wait_ge(q_rope_ready, h // 4 + 1)
                    pe.wait_ge(drained[h // 2], DR["ukv"][h // 2] + 1)
                nc.tensor.matmul(bank[bk][:, 0:(qt + 1) * P], q_mla[:, h, qt * P:(qt + 1) * P],
                                 k_mla[:, h, 0:(qt + 1) * P], start=True, stop=True).then_inc(tile_ready[bk], 1)

            def turn(u):
                qt, bk = u // HEADS, u % 4
                pe.wait_ge(drained[bk], DR["att"][bk] + 2 * (u // 4) + 1)
                for s in range(qt + 1):
                    ins = nc.tensor.transpose(bank[bk][:, s * P:(s + 1) * P], probs[:, u % 2, s * P:(s + 1) * P],
                                              ident[:, :])
                ins.then_inc(tile_ready[bk], 1)

            def values(u):
                qt, h, bk = u // HEADS, u % HEADS, u % 4
                pe.wait_ge(drained[bk], DR["att"][bk] + 2 * (u // 4) + 2)
                if h == 0:
                    pe.wait_ge(drained[4 + qt], DR["att"][4 + qt])
                for s in range(qt + 1):
                    ins = nc.tensor.matmul(bank[4 + qt][:, h * VD:(h + 1) * VD], probsT[:, u % 2, s, :],
                                           v_mla[:, s, h * VD:(h + 1) * VD], start=(s == 0), stop=(s == qt))
                ins.then_inc(pv_done, 1)

            def yb_T(qt):
                pe.wait_ge(drained[4 + qt], DR["att"][4 + qt] + 1)
                for k in range(4):
                    ins = nc.tensor.transpose(bank[4 + qt][:, k * P:(k + 1) * P], y_acc[:, qt, k * P:(k + 1) * P],
                                              ident[:, :])
                ins.then_inc(tile_ready[4 + qt], 1)

            pe.wait_ge(k_rope_ready, HEADS)
            units = NT * HEADS
            scores(0)
            scores(1)
            for u in range(units + 1):
                if u + 2 < units:
                    scores(u + 2)
                if u < units:
                    turn(u)
                if u >= 1:
                    values(u - 1)
                if u % HEADS == 3 and u > HEADS:
                    yb_T(u // HEADS - 1)

            def out_proj(i, phase, ready, after=None):
                c = CH[phase]
                rows(phase, c, 0, 2, aT_hi, aT_lo, lhs_ready=ready, after=after)
                rows(phase, c + 2, 1, 2, aT_hi, aT_lo, order=PAIRWISE, after=norm_first(i, 2))

            def out0_ready(k):
                if k < 4:
                    pe.wait_ge(ya_ready, k + 1)
                elif k == 4:
                    for qt in range(NT):
                        pe.wait_ge(drained[4 + qt], DR["att"][4 + qt] + 2)

            def mlp(l, i):
                for h in range(FH):
                    p1, p2 = f"w1{'ab'[h]}{l}", f"w2{'ab'[h]}{l}"
                    c1, c2 = CH[p1], CH[p2]
                    u0 = (l * FH + h) * 4 * FG
                    if h == 0:
                        columns_halves(p1, i - 1)
                    with pe.Fori(1 - h, FG) as g:
                        columns(p1, g * 2 + c1, g)

                    def u_tile(k):
                        pe.wait_ge(u_ready, u0 + k + 1)

                    if h == 0:
                        with pe.Fori(0, 2) as n:
                            rows(p2, n * 4 + c2, n, 4, uT_hi, uT_lo, lhs_ready=u_tile)
                    else:
                        rows(p2, c2, 0, 4, uT_hi, uT_lo, lhs_ready=u_tile)
                        last = i == 4
                        rows(p2, c2 + 4, 1, 4, uT_hi, uT_lo, order=SINGLY if last else PAIRWISE,
                             after=None if last else norm_first(i, 4))

            out_proj(1, "out0", out0_ready, after={(0, 0): lambda: yb_T(NT - 1)})
            mlp(0, 2)
            columns_halves("qk", 2)

            pe.wait_ge(small_ready, 2)
            pe.wait_ge(drained[4], DR["gates"][4])
            for k in range(KT):
                ins = mm3(bank[4][0:64, :], small_hi[:, k, :], small_lo[:, k, :], aT_hi[:, k, :], aT_lo[:, k, :],
                          k == 0, k == KT - 1)
            ins.then_inc(tile_ready[4], 1)
            columns("qk", CH["qk"] + 2, 1)
            pe.wait_ge(rows_ready, 1)
            pe.wait_ge(drained[4], DR["gates"][4] + 1)
            for n, (s, t) in enumerate(PAIRS):
                row, r = (row_i, s) if s == t else (row_far, FAR.index((s, t)))
                nc.tensor.transpose(bank[4][:, 4 * n:4 * n + 4], row[:, r * P:(r + 1) * P], ident[0:4, 0:4])
            for t in range(NT):
                n = len(PAIRS) + t
                ins = nc.tensor.transpose(bank[4][:, 4 * n:4 * n + 4], row_m[:, t * P:(t + 1) * P], ident[0:4, 0:4])
            ins.then_inc(tile_ready[4], 1)
            with pe.Fori(2, 4) as g:
                columns("qk", g * 2 + CH["qk"], g)
            for g in range(2):
                columns("ogate", CH["ogate"] + 2 * g, g)
            rows("v", CH["v"], 0, 2, aT_hi, aT_lo)
            pe.wait_ge(sel_r_ready, 1)
            pe.wait_ge(row_lo_ready, 1)
            for bk in range(4):
                pe.wait_ge(drained[bk], DR["qk"][bk] + 4)

            def ml_row(h):
                if h == 0:
                    pe.wait_ge(drained[0], DR["core"][0])
                else:
                    pe.wait_ge(decay_raw, h * NT)
                sel = head_sel_r[:, h * P:(h + 1) * P]
                nc.tensor.matmul(bank[0][:, :], sel, row_f_lo[:, :], start=True, stop=False)
                nc.tensor.matmul(bank[0][:, :], sel, row_f_hi[:, :], start=False, stop=True).then_inc(tile_ready[0], 1)

            def ml_scores(i):
                h, s = i // NT, i % NT
                bk = 1 + i % 2
                if i >= 2:
                    pe.wait_ge(wgt_ready, i - 1)
                else:
                    pe.wait_ge(drained[bk], DR["core"][bk])
                for k in range(2):
                    ins = nc.tensor.matmul(bank[bk][:, s * P:S], qk_ml[:, 8 + 2 * h + k, s * P:(s + 1) * P],
                                           qk_ml[:, 2 * h + k, s * P:S], start=(k == 0), stop=(k == 1))
                ins.then_inc(tile_ready[bk], 1)

            def ml_values(i):
                h, s = i // NT, i % NT
                pe.wait_ge(wgt_ready, i + 1)
                if i == 0:
                    pe.wait_ge(v_ones, 1)
                if h == 0:
                    pe.wait_ge(drained[4 + s], DR["v"][4 + s] + 2)
                for t in range(s, NT):
                    if s == 0:
                        pe.wait_ge(drained[4 + t], DR["core"][4 + t] + h)
                    ins = nc.tensor.matmul(bank[4 + t][:, 0:DH + 1], wgtT[:, i % 2, t * P:(t + 1) * P],
                                           v_aug[:, s, h, :], start=(s == 0), stop=(s == t))
                    if t == s:
                        ins.then_inc(tile_ready[4 + t], 1)

            n_ml = ML_HEADS * NT
            ml_row(0)
            ml_scores(0)
            rows("v", CH["v"] + 2, 1, 2, aT_hi, aT_lo)
            for i in range(n_ml):
                if i + 1 < n_ml:
                    if (i + 1) % NT == 0:
                        ml_row((i + 1) // NT)
                    ml_scores(i + 1)
                ml_values(i)
            def cell_T(f):
                bk = f % 4
                pe.wait_ge(cell_ready, NT * (f // 2) + NT)
                if f == 0:
                    pe.wait_ge(decay_raw, n_ml)
                if f >= 4:
                    pe.wait_ge(drained[bk], DR["cellT"][bk] + f // 4)
                for t in range(NT):
                    ins = nc.tensor.transpose(bank[bk][:, t * P:(t + 1) * P], cell[:, t, f * P:(f + 1) * P],
                                              ident[:, :])
                ins.then_inc(tile_ready[bk], 1)

            def cell_T_last():
                for f in range(4, 8):
                    cell_T(f)

            for f in range(4):
                cell_T(f)

            def out1_ready(k):
                pe.wait_ge(ya_ready, 4 + k + 1)

            out_proj(3, "out1", out1_ready, after={(0, 1): cell_T_last})
            mlp(1, 4)


_INS = ["x", "positions", "norm_mix_pre", "norm_mix_post", "norm_mlp_pre", "norm_mlp_post", "hyb_w_in", "conv_w",
        "mla_q_norm", "mla_kv_norm", "mla_w_uq", "mla_w_ukv", "hyb_w_out", "ml_w_in", "ml_b_i", "ml_b_f",
        "ml_head_norm", "ml_w_out", "mlp_w1", "mlp_w2"]
_FLAT = {"x", "hyb_w_in", "conv_w", "mla_w_uq", "mla_w_ukv", "hyb_w_out", "ml_w_in", "ml_w_out"}


def kernel(**inputs):
    import numpy as _np
    import concourse.bacc as _bacc
    from concourse import mybir as _mybir
    from concourse.bass_utils import run_bass_kernel_spmd as _run

    nc = _bacc.Bacc("TRN2", target_bir_lowering=False, num_devices=1)
    arrays, args = {}, []

    def give(name, a):
        arrays[f"in_{name}_dram"] = a
        args.append(nc.dram_tensor(f"in_{name}_dram", a.shape, _mybir.dt.from_np(a.dtype), kind="ExternalInput").ap())

    for name in _INS:
        a = _np.ascontiguousarray(inputs[name])
        if name in _FLAT:
            a = a[0]
        give(name, a)
    half = ROPE // 2
    inv = _np.float32(10000.0) ** (-_np.arange(half, dtype=_np.float32) / _np.float32(half))
    sign = _np.where(_np.arange(P) % ROPE < half, -1.0, 1.0).astype(_np.float32)
    give("rope_const", _np.stack([_np.tile(inv, P // half), sign], axis=1))
    args.append(nc.dram_tensor("out_dram", (S, D), _mybir.dt.float32, kind="ExternalOutput").ap())
    trunk(nc, *args)
    r = _run(nc, [arrays], core_ids=[0])
    return r.results[0]["out_dram"].reshape(1, S, D)
```
